# Optimizing a Trainium2 kernel written in Bass

```python
import math
import jax
import jax.numpy as jnp
from jax import lax
import numpy as np

D_MODEL = 2048
BATCH = 1
SEQ = 256
DEPTH = 1
DEC_BATCH = 8
DEC_SEQ = 4
PAST_LEN = 2048
PAGE_SIZE = 128

MIX_A = D_MODEL // 2
MIX_B = D_MODEL - MIX_A
A_HEAD = 64
A_HEADS = MIX_A // A_HEAD
A_DECAY_RANK = 64
A_ICL_RANK = 64
A_GATE_RANK = 128
A_GN_EPS = A_HEAD * 1e-5
B_HEADS = 4
B_DV = MIX_B // B_HEADS
B_DQK = B_DV // 2
B_CONV = 4
B_CHUNK = 64
PEER_HEADS = 8
PEER_NKEYS = 128
PEER_NEXP = PEER_NKEYS * PEER_NKEYS
PEER_DKEY = 256
PEER_TOPK = 16
PEER_BLOCK = 128
NORM_EPS = 1e-6

A_SHIFT_COLS = 3 * MIX_A + A_DECAY_RANK + A_ICL_RANK + A_GATE_RANK
B_QK_COLS = 2 * B_HEADS * B_DQK
B_REST_COLS = 2 * MIX_B + 2 * B_HEADS
N_IN = A_SHIFT_COLS + B_QK_COLS + B_REST_COLS
A_SPLITS = (MIX_A, 2 * MIX_A, 3 * MIX_A, 3 * MIX_A + A_DECAY_RANK, 3 * MIX_A + A_DECAY_RANK + A_ICL_RANK)
B_SPLITS = (MIX_B, 2 * MIX_B, 2 * MIX_B + B_HEADS)

LAYER_PARAMS = ('w_ada', 'b_ada', 'norm_mix_g', 'w_in', 'a_mu', 'a_w0', 'a_w2', 'a_a0', 'a_a2', 'a_g2',
                'a_kk', 'a_ka', 'a_rk', 'a_lnw', 'a_lnb', 'b_conv_w', 'b_conv_b', 'b_ig_bias', 'b_fg_bias',
                'b_norm_g', 'w_out', 'norm_ffn_g', 'peer_wq', 'peer_keys', 'peer_u', 'peer_v')

kernel_name = 'hybrid_rwkv7_mlstm_peer_step'

def rmsnorm(x, g):
    xf = x.astype(jnp.float32)
    y = xf * lax.rsqrt(jnp.mean(xf * xf, axis=-1, keepdims=True) + NORM_EPS)
    return (y * g).astype(x.dtype)

def rwkv7_mix(z, shift_buf, wkv0, p):
    f32 = jnp.float32
    bsz, t_len, _ = z.shape
    prev = jnp.concatenate([shift_buf[:, None, :].astype(z.dtype), z[:, :-1]], axis=1)
    zs = z + (prev - z) * p['a_mu']
    r, k, v, xw, xa, xg = jnp.split(zs.astype(f32), A_SPLITS, axis=-1)
    w_log = -jax.nn.softplus(-(p['a_w0'] + jnp.tanh(xw) @ p['a_w2'])) - 0.5
    decay = jnp.exp(-jnp.exp(w_log))
    a = jax.nn.sigmoid(p['a_a0'] + xa @ p['a_a2'])
    g = jax.nn.sigmoid(xg) @ p['a_g2']
    heads = lambda t: t.reshape(bsz, t_len, A_HEADS, A_HEAD)
    kk = heads(k * p['a_kk'])
    kk = kk / jnp.maximum(jnp.linalg.norm(kk, axis=-1, keepdims=True), 1e-12)
    k = k * (1.0 + (a - 1.0) * p['a_ka'])
    rh, kh, vh, dh, ah = heads(r), heads(k), heads(v), heads(decay), heads(a)

    def step(S, inp):
        r_t, d_t, k_t, v_t, kk_t, a_t = inp
        sa = jnp.einsum('bhij,bhj->bhi', S, -kk_t)
        S = (S * d_t[:, :, None, :] + sa[..., None] * (kk_t * a_t)[:, :, None, :]
             + v_t[..., None] * k_t[:, :, None, :])
        return S, jnp.einsum('bhij,bhj->bhi', S, r_t)

    seq_first = lambda t: jnp.swapaxes(t, 0, 1)
    S_T, y = lax.scan(step, wkv0.astype(f32), tuple(seq_first(t) for t in (rh, dh, kh, vh, kk, ah)))
    y = seq_first(y)
    mu = jnp.mean(y, axis=-1, keepdims=True)
    var = jnp.mean(jnp.square(y - mu), axis=-1, keepdims=True)
    y = ((y - mu) * lax.rsqrt(var + A_GN_EPS)).reshape(bsz, t_len, MIX_A) * p['a_lnw'] + p['a_lnb']
    bonus = jnp.sum(rh * kh * p['a_rk'], axis=-1, keepdims=True) * vh
    y = (y + bonus.reshape(bsz, t_len, MIX_A)) * g
    return y, z[:, -1], S_T

def mlstm_chunkwise(q, k, v, ig, fg, C0, n0, m0):
    bsz, t_len = q.shape[:2]
    L = math.gcd(t_len, B_CHUNK)
    nc = t_len // L
    mask = jnp.tril(jnp.ones((L, L), dtype=bool))

    def chunks(t):
        t = t.reshape((bsz, nc, L) + t.shape[2:])
        return jnp.moveaxis(jnp.moveaxis(t, 1, 0), 2, 3)

    def step(carry, inp):
        C, n, m = carry
        qc, kc, vc, ic, fc = inp
        b = jnp.cumsum(jax.nn.log_sigmoid(fc), axis=-1)
        inter = b + m[..., None]
        logD = jnp.where(mask, b[..., :, None] - b[..., None, :] + ic[..., None, :], -jnp.inf)
        m_t = jnp.maximum(inter, jnp.max(logD, axis=-1))
        S = jnp.einsum('bhtd,bhsd->bhts', qc, kc) * jnp.exp(logD - m_t[..., None])
        w_inter = jnp.exp(inter - m_t)
        num = S @ vc + w_inter[..., None] * jnp.einsum('bhtd,bhdv->bhtv', qc, C)
        den = jnp.sum(S, axis=-1) + w_inter * jnp.einsum('bhtd,bhd->bht', qc, n)
        h = num / jnp.maximum(jnp.abs(den), jnp.exp(-m_t))[..., None]
        m_new = m_t[..., -1]
        ws = jnp.exp(b[..., -1:] - b + ic - m_new[..., None])
        dC = jnp.exp(b[..., -1] + m - m_new)
        C_new = dC[..., None, None] * C + jnp.einsum('bhs,bhsd,bhsv->bhdv', ws, kc, vc)
        n_new = dC[..., None] * n + jnp.einsum('bhs,bhsd->bhd', ws, kc)
        return (C_new, n_new, m_new), h

    (C, n, m), h = lax.scan(step, (C0, n0, m0), tuple(chunks(t) for t in (q, k, v, ig, fg)))
    h = jnp.transpose(h, (1, 0, 3, 2, 4)).reshape(bsz, t_len, B_HEADS, B_DV)
    return h, C, n, m

def mlstm_mix(z_qk, z_rest, conv_buf, C0, n0, m0, p):
    f32 = jnp.float32
    bsz, t_len, _ = z_qk.shape
    zp = jnp.concatenate([conv_buf.astype(z_qk.dtype), z_qk], axis=1)
    qk = lax.conv_general_dilated(zp, p['b_conv_w'][:, None, :].astype(zp.dtype), (1,), 'VALID',
                                  dimension_numbers=('NWC', 'WIO', 'NWC'),
                                  feature_group_count=B_QK_COLS) + p['b_conv_b']
    qk = jax.nn.silu(qk.astype(f32))
    q, k = jnp.split(qk, 2, axis=-1)
    v, o, ig, fg = jnp.split(z_rest.astype(f32), B_SPLITS, axis=-1)
    q = q.reshape(bsz, t_len, B_HEADS, B_DQK)
    k = k.reshape(bsz, t_len, B_HEADS, B_DQK) * (B_DQK ** -0.5)
    v = v.reshape(bsz, t_len, B_HEADS, B_DV)
    h, C, n, m = mlstm_chunkwise(q, k, v, ig + p['b_ig_bias'], fg + p['b_fg_bias'],
                                 C0.astype(f32), n0.astype(f32), m0.astype(f32))
    h = h * lax.rsqrt(jnp.mean(h * h, axis=-1, keepdims=True) + NORM_EPS)
    h = h.reshape(bsz, t_len, MIX_B) * p['b_norm_g'] * jax.nn.sigmoid(o)
    return h, zp[:, zp.shape[1] - (B_CONV - 1):], C, n, m

def peer_ffn(h, w_q, keys, u, v):
    bsz, t_len, dm = h.shape
    x = h.reshape(bsz * t_len, dm)
    ntok = x.shape[0]
    q = (x @ w_q).astype(jnp.float32).reshape(ntok, PEER_HEADS, 2, PEER_DKEY // 2)
    s = jnp.einsum('nhpd,phkd->nhpk', q, keys.astype(jnp.float32))
    s_top, i_top = lax.top_k(s, PEER_TOPK)
    cand_s = (s_top[:, :, 0, :, None] + s_top[:, :, 1, None, :]).reshape(ntok, PEER_HEADS, PEER_TOPK * PEER_TOPK)
    cand_i = (i_top[:, :, 0, :, None] * PEER_NKEYS + i_top[:, :, 1, None, :]).reshape(ntok, PEER_HEADS, PEER_TOPK * PEER_TOPK)
    best_s, pos = lax.top_k(cand_s, PEER_TOPK)
    idx = jnp.take_along_axis(cand_i, pos, axis=-1).reshape(ntok, PEER_HEADS * PEER_TOPK)
    gate = jax.nn.softmax(best_s, axis=-1).reshape(ntok, PEER_HEADS * PEER_TOPK).astype(x.dtype)
    nb = -(-ntok // PEER_BLOCK)
    pad = nb * PEER_BLOCK - ntok
    xb = jnp.pad(x, ((0, pad), (0, 0))).reshape(nb, PEER_BLOCK, dm)
    ib = jnp.pad(idx, ((0, pad), (0, 0))).reshape(nb, PEER_BLOCK, -1)
    gb = jnp.pad(gate, ((0, pad), (0, 0))).reshape(nb, PEER_BLOCK, -1)

    def block(args):
        xt, it, gt = args
        ue = jnp.take(u, it, axis=0)
        act = jax.nn.gelu(jnp.einsum('nd,ned->ne', xt, ue), approximate=False) * gt
        ve = jnp.take(v, it, axis=0)
        return jnp.einsum('ne,ned->nd', act, ve)

    out = lax.map(block, (xb, ib, gb)).reshape(nb * PEER_BLOCK, dm)[:ntok]
    return out.reshape(bsz, t_len, dm)

def trunk(x, c, states, P):
    shift_s, wkv_s, conv_s, C_s, n_s, m_s = states
    outs = ([], [], [], [], [], [])
    for l in range(DEPTH):
        p = {name: P[name][l] for name in LAYER_PARAMS}
        mod = (jax.nn.silu(c) @ p['w_ada'] + p['b_ada'])[:, None, :]
        sh_a, sc_a, g_a, sh_c, sc_c, g_c = jnp.split(mod, 6, axis=-1)
        h = rmsnorm(x, p['norm_mix_g']) * (1.0 + sc_a) + sh_a
        z = h @ p['w_in']
        z_a = z[..., :A_SHIFT_COLS]
        z_qk = z[..., A_SHIFT_COLS:A_SHIFT_COLS + B_QK_COLS]
        z_rest = z[..., A_SHIFT_COLS + B_QK_COLS:]
        y_a, new_shift, new_wkv = rwkv7_mix(z_a, shift_s[l], wkv_s[l], p)
        y_b, new_conv, new_C, new_n, new_m = mlstm_mix(z_qk, z_rest, conv_s[l], C_s[l], n_s[l], m_s[l], p)
        y_mix = jnp.concatenate([y_a, y_b], axis=-1).astype(x.dtype) @ p['w_out']
        x = x + g_a * y_mix
        h = rmsnorm(x, p['norm_ffn_g']) * (1.0 + sc_c) + sh_c
        x = x + g_c * peer_ffn(h, p['peer_wq'], p['peer_keys'], p['peer_u'], p['peer_v'])
        for lst, val in zip(outs, (new_shift, new_wkv, new_conv, new_C, new_n, new_m)):
            lst.append(val.astype(x.dtype))
    mod = (jax.nn.silu(c) @ P['w_ada_final'] + P['b_ada_final'])[:, None, :]
    shift, scale = jnp.split(mod, 2, axis=-1)
    y = rmsnorm(x, P['norm_final_g']) * (1.0 + scale) + shift
    return y, tuple(jnp.stack(o, axis=0) for o in outs)

def setup_inputs(seed: int = 0) -> dict:
    key = jax.random.key(seed)
    ks = iter(jax.random.split(key, 48))
    f32 = jnp.float32
    nrm = lambda shape, s=1.0: s * jax.random.normal(next(ks), shape, f32)
    uni = lambda shape, lo, hi: jax.random.uniform(next(ks), shape, f32, lo, hi)
    lin = lambda lo, hi, n: jnp.broadcast_to(jnp.linspace(lo, hi, n, dtype=f32), (DEPTH, n))
    D = D_MODEL
    return {
        'x_prompt': nrm((BATCH, SEQ, D)),
        'x_sample': nrm((DEC_BATCH, DEC_SEQ, D)),
        'c_prompt': nrm((BATCH, D)),
        'c_sample': nrm((DEC_BATCH, D)),
        'state_rwkv_shift': nrm((DEPTH, DEC_BATCH, A_SHIFT_COLS)),
        'state_rwkv_wkv': nrm((DEPTH, DEC_BATCH, A_HEADS, A_HEAD, A_HEAD), 0.3),
        'state_mlstm_conv': nrm((DEPTH, DEC_BATCH, B_CONV - 1, B_QK_COLS)),
        'state_mlstm_C': nrm((DEPTH, DEC_BATCH, B_HEADS, B_DQK, B_DV), 0.3),
        'state_mlstm_n': nrm((DEPTH, DEC_BATCH, B_HEADS, B_DQK), 0.3),
        'state_mlstm_m': nrm((DEPTH, DEC_BATCH, B_HEADS)),
        'w_ada': nrm((DEPTH, D, 6 * D), 0.5 * D ** -0.5),
        'b_ada': nrm((DEPTH, 6 * D), 0.02),
        'norm_mix_g': 1.0 + nrm((DEPTH, D), 0.02),
        'w_in': nrm((DEPTH, D, N_IN), D ** -0.5),
        'a_mu': uni((DEPTH, A_SHIFT_COLS), 0.0, 1.0),
        'a_w0': lin(-6.0, -1.0, MIX_A) + nrm((DEPTH, MIX_A), 0.1),
        'a_w2': nrm((DEPTH, A_DECAY_RANK, MIX_A), 0.5 * A_DECAY_RANK ** -0.5),
        'a_a0': nrm((DEPTH, MIX_A), 0.1),
        'a_a2': nrm((DEPTH, A_ICL_RANK, MIX_A), 0.5 * A_ICL_RANK ** -0.5),
        'a_g2': nrm((DEPTH, A_GATE_RANK, MIX_A), A_GATE_RANK ** -0.5),
        'a_kk': 0.85 + nrm((DEPTH, MIX_A), 0.02),
        'a_ka': 1.0 + nrm((DEPTH, MIX_A), 0.02),
        'a_rk': nrm((DEPTH, A_HEADS, A_HEAD), 0.1),
        'a_lnw': 1.0 + nrm((DEPTH, MIX_A), 0.02),
        'a_lnb': nrm((DEPTH, MIX_A), 0.02),
        'b_conv_w': nrm((DEPTH, B_CONV, B_QK_COLS), B_CONV ** -0.5),
        'b_conv_b': nrm((DEPTH, B_QK_COLS), 0.02),
        'b_ig_bias': nrm((DEPTH, B_HEADS), 0.1),
        'b_fg_bias': lin(3.0, 6.0, B_HEADS) + nrm((DEPTH, B_HEADS), 0.1),
        'b_norm_g': 1.0 + nrm((DEPTH, MIX_B), 0.02),
        'w_out': nrm((DEPTH, D, D), D ** -0.5),
        'norm_ffn_g': 1.0 + nrm((DEPTH, D), 0.02),
        'peer_wq': nrm((DEPTH, D, PEER_HEADS * PEER_DKEY), D ** -0.5),
        'peer_keys': nrm((DEPTH, 2, PEER_HEADS, PEER_NKEYS, PEER_DKEY // 2), (PEER_DKEY // 2) ** -0.5),
        'peer_u': nrm((DEPTH, PEER_NEXP, D), D ** -0.5),
        'peer_v': nrm((DEPTH, PEER_NEXP, D), 0.5),
        'w_ada_final': nrm((D, 2 * D), 0.5 * D ** -0.5),
        'b_ada_final': nrm((2 * D,), 0.02),
        'norm_final_g': 1.0 + nrm((D,), 0.02),
    }

def reference(x_prompt, x_sample, c_prompt, c_sample, state_rwkv_shift, state_rwkv_wkv, state_mlstm_conv,
              state_mlstm_C, state_mlstm_n, state_mlstm_m, w_ada, b_ada, norm_mix_g, w_in, a_mu, a_w0, a_w2,
              a_a0, a_a2, a_g2, a_kk, a_ka, a_rk, a_lnw, a_lnb, b_conv_w, b_conv_b, b_ig_bias, b_fg_bias,
              b_norm_g, w_out, norm_ffn_g, peer_wq, peer_keys, peer_u, peer_v, w_ada_final, b_ada_final,
              norm_final_g):
    P = dict(w_ada=w_ada, b_ada=b_ada, norm_mix_g=norm_mix_g, w_in=w_in, a_mu=a_mu, a_w0=a_w0, a_w2=a_w2,
             a_a0=a_a0, a_a2=a_a2, a_g2=a_g2, a_kk=a_kk, a_ka=a_ka, a_rk=a_rk, a_lnw=a_lnw, a_lnb=a_lnb,
             b_conv_w=b_conv_w, b_conv_b=b_conv_b, b_ig_bias=b_ig_bias, b_fg_bias=b_fg_bias,
             b_norm_g=b_norm_g, w_out=w_out, norm_ffn_g=norm_ffn_g, peer_wq=peer_wq, peer_keys=peer_keys,
             peer_u=peer_u, peer_v=peer_v, w_ada_final=w_ada_final, b_ada_final=b_ada_final,
             norm_final_g=norm_final_g)
    bp = x_prompt.shape[0]
    dt = x_prompt.dtype
    zero_states = (jnp.zeros((DEPTH, bp, A_SHIFT_COLS), dt),
                   jnp.zeros((DEPTH, bp, A_HEADS, A_HEAD, A_HEAD), dt),
                   jnp.zeros((DEPTH, bp, B_CONV - 1, B_QK_COLS), dt),
                   jnp.zeros((DEPTH, bp, B_HEADS, B_DQK, B_DV), dt),
                   jnp.zeros((DEPTH, bp, B_HEADS, B_DQK), dt),
                   jnp.zeros((DEPTH, bp, B_HEADS), dt))
    y_prompt, p_states = trunk(x_prompt, c_prompt, zero_states, P)
    y_sample, s_states = trunk(x_sample, c_sample,
                               (state_rwkv_shift, state_rwkv_wkv, state_mlstm_conv,
                                state_mlstm_C, state_mlstm_n, state_mlstm_m), P)
    p_shift, p_wkv, p_conv, p_C, p_n, p_m = p_states
    s_shift, s_wkv, s_conv, s_C, s_n, s_m = s_states
    return (y_prompt, y_sample, p_shift, p_wkv, p_conv, p_C, p_n, p_m,
            s_shift, s_wkv, s_conv, s_C, s_n, s_m)


_drawn_inputs = setup_inputs


def setup_inputs(seed=0):
    import zlib

    import numpy as np

    out = dict(_drawn_inputs(seed))
    spreads = {}
    factors = {'a_lnw': 79.767,
     'a_lnb': 78.55,
     'b_norm_g': 80.253,
     'norm_ffn_g': 19.125,
     'norm_final_g': 23.302,
     'b_ada_final': 2.74,
     'a_rk': 4.942}
    for name, (base, spread) in spreads.items():
        noise = np.random.default_rng([zlib.crc32(name.encode()), seed]).standard_normal(out[name].shape)
        drawn = base * np.exp(spread * noise) if base else spread * noise
        out[name] = jnp.asarray(drawn.astype(out[name].dtype))
    for name, factor in factors.items():
        out[name] = (out[name] * factor).astype(out[name].dtype)
    return out
```

```python
import math
from contextlib import ExitStack

import numpy as np

import concourse.bass as bass
from concourse import mybir

F32 = mybir.dt.float32
U32 = mybir.dt.uint32
ALU = mybir.AluOpType
ACT = mybir.ActivationFunctionType
AX = mybir.AxisListType

P = 128
D = 2048
KT = D // P
TP, NB, TS = 256, 8, 4
SM = NB * TS
N = TP + SM
NS = NB + 1
MIX = D // 2
MT = MIX // P
AH, AHD = 16, 64
SHIFT = 3 * MIX + 256
AT = SHIFT // P
BH, DQK, DV = 4, 128, 256
CONV = 4
L = 128
CH = TP // L
HG = 8
PH, NK, TOPK = 8, 128, 16
NEG = -3.0e38

def columns(sizes):
    at, out = 0, {}
    for name, n in sizes:
        out[name] = (at, n)
        at += n
    return out, at


CST0, CST0_N = columns([("ident", P), ("ones", P), ("iota", P)])
LEVELS = 7
CST1, CST1_N = columns([
    ("blk", P), ("level", LEVELS * P), ("strict", P), ("incl", P), ("slevel", 2 * SM), ("sstrict", SM), ("sincl", SM),
    ("seq", NB), ("wreset", N), ("breset", N), ("mreset", N), ("sel", BH * P), ("fold", 16), ("seqcol", NB * SM)])
PRM, PRM_N = columns([
    ("mu", AT), ("w0", MT), ("a0", MT), ("kk", MT), ("ka", MT), ("rk", MT), ("lnw", MT), ("lnb", MT),
    ("convw", CONV * MT), ("convb", MT), ("bnorm", MT), ("gmix", KT), ("gffn", KT), ("gfin", KT),
    ("bada", 8 * KT), ("gatebias", 1), ("eps", 1), ("gneps", 1), ("zero", 1)])

ARENA = 53208
RING_SLOTS = 4
M_CST0 = 0
M_MODS = M_CST0 + CST0_N
M_PRM = M_MODS + 8 * KT * NS
M_RING = (M_PRM + PRM_N + 7) // 8 * 8
M_BASE = M_RING + RING_SLOTS * D
M_CST1 = M_BASE
M_SILC = M_CST1 + (CST1_N + 7) // 8 * 8
AUX, AUX_N = columns([("n0", NB * BH), ("m0", NB), ("conv", MT * NB * 3), ("shift", AT * NB), ("wg", KT * 36),
                      ("w2", MIX), ("a2", MIX), ("g2", MIX)])
M_AUX = M_SILC + KT * 32
M_ADAS = M_AUX + AUX_N
M_YMIX = M_ADAS + D
M_H = M_YMIX + KT * N
M_Q = M_H + KT * N
M_H2 = M_BASE
M_MISC = M_H2 + KT * N
M_G = ARENA - NK * N
assert M_MISC + 1376 <= M_G


def constants():
    c0 = np.zeros((P, CST0_N), np.float32)
    c1 = np.zeros((P, CST1_N), np.float32)

    def put(c, cols, name, a):
        at, n = cols[name]
        c[:a.shape[0], at:at + n] = a.reshape(a.shape[0], n)

    i = np.arange(P)
    put(c0, CST0, "ident", np.eye(P))
    put(c0, CST0, "ones", np.ones((P, P)))
    put(c0, CST0, "iota", np.broadcast_to(i, (P, P)))
    s, t = i[:, None], i[None, :]
    put(c1, CST1, "blk", (s // AHD == t // AHD))
    lev = [(s >> (l + 1) == t >> (l + 1)) & (s >> l != t >> l) & (s < t) for l in range(LEVELS)]
    put(c1, CST1, "level", np.stack(lev, 1))
    put(c1, CST1, "strict", s < t)
    put(c1, CST1, "incl", s <= t)
    put(c1, CST1, "slevel", np.stack([m[:SM, :SM] for m in lev[:2]], 1))
    same = (s // TS == t // TS)[:SM, :SM]
    put(c1, CST1, "sstrict", same & (s < t)[:SM, :SM])
    put(c1, CST1, "sincl", same & (s <= t)[:SM, :SM])
    put(c1, CST1, "seq", (i[:SM, None] // TS == np.arange(NB)[None, :]))
    n = np.arange(N)
    starts = ((n >= TP) & ((n - TP) % TS == 0)) | (n == 0)
    put(c1, CST1, "wreset", np.broadcast_to(~(starts | ((n < TP) & (n % L == 0))), (P, N)))
    put(c1, CST1, "breset", np.broadcast_to(~starts, (P, N)))
    put(c1, CST1, "mreset", np.broadcast_to(np.where(starts, NEG, 0.0), (P, N)))
    put(c1, CST1, "sel", np.repeat(np.eye(BH), P, axis=1))
    fold = np.zeros((P, 16))
    for r in range(NS):
        fold[r::32, r] = 1.0
    put(c1, CST1, "fold", fold)
    put(c1, CST1, "seqcol", np.broadcast_to(np.repeat(np.eye(NB), TS, axis=1), (P, NB, SM)))
    return c0, c1


class Chain:

    def __init__(self, eng, sem):
        self.eng, self.sem, self.n = eng, sem, 0

    def link(self, ins):
        self.n = self.n + 1
        ins.then_inc(self.sem, 1)
        self.eng.wait_ge(self.sem, self.n)


def build(nc, T):
    ctx = ExitStack()
    with ctx:
        mem = ctx.enter_context(nc.sbuf_tensor("mem", [P, ARENA], F32))
        ps = [ctx.enter_context(nc.psum_tensor(f"bank{i}", [P, 512], F32)) for i in range(8)]
        x1_dram = nc.dram_tensor("x1_spill", (P, KT, N), F32, kind="Internal").ap()

        sems = {}

        def S(name):
            if name not in sems:
                sems[name] = ctx.enter_context(nc.semaphore(name))
            return sems[name]

        def words(at, *dims, rows=P, first=0):
            v = mem[first:first + rows, at:at + math.prod(dims)]
            if len(dims) > 1:
                names = "abcd"[:len(dims)]
                v = v.rearrange(f"p ({' '.join(names)}) -> p {' '.join(names)}", **dict(zip(names[1:], dims[1:])))
            return v

        def cst0(name, rows=P):
            return words(M_CST0 + CST0[name][0], CST0[name][1], rows=rows)

        def cst1(name, *dims, rows=P):
            return words(M_CST1 + CST1[name][0], *(dims or (CST1[name][1],)), rows=rows)

        def prm(name, i=None, n=1, rows=P, first=0):
            at, size = PRM[name]
            return words(M_PRM + at + (i or 0), n if i is not None else size, rows=rows, first=first)

        def aux(name, *dims, rows=P):
            return words(M_AUX + AUX[name][0], *(dims or (AUX[name][1],)), rows=rows)

        def over(v, axis, n):
            v = v.unsqueeze(axis)
            return v.broadcast_to([n if i == axis else d for i, d in enumerate(v.shape)])

        ident, ones, iota = cst0("ident"), cst0("ones"), cst0("iota")
        blk = cst1("blk")
        mods = words(M_MODS, 8, KT, NS)
        SH_A, SC_A, G_A, SH_C, SC_C, G_C, SH_F, SC_F = range(8)
        ring = [words(M_RING + i * D, D) for i in range(RING_SLOTS)]
        silc = words(M_SILC, KT, 32)
        adas = words(M_ADAS, D)
        ymix = words(M_YMIX, KT, N)
        hT = words(M_H, KT, N)

        xT = words(M_Q, KT, N)
        xsq = words(M_Q + KT * N, KT, N)
        rms = words(M_Q + 2 * KT * N, 2, N)
        gain = words(M_Q + 2 * KT * N + 2 * N, KT, NS)

        craw = words(M_Q + 2 * KT * N + 2 * N + KT * NS, KT, NS)
        csig = words(M_Q + 2 * KT * N + 2 * N + 2 * KT * NS, KT, NS)

        q0 = M_Q
        ZQW = TP + 3 + NB * 7
        ZQS = ZQW + 5
        zq = words(q0, 2, ZQS)
        conv = words(q0 + 2 * ZQS, 2, ZQS)
        q1 = q0 + 4 * ZQS
        qk = words(q1, MT, N)
        bv = words(q1 + MT * N, MT, N)
        q2 = q1 + 2 * MT * N
        ROWS = ["i", "f", "t", "b", "g", "g2", "mx", "m", "em", "ws", "wi"]
        row = {n: words(q2 + j * N, N, rows=BH) for j, n in enumerate(ROWS)}
        q3 = q2 + len(ROWS) * N
        cvo = words(q3, MT, NS, 3)
        sho = words(q3 + MT * NS * 3, AT, NS)
        mo = words(q3 + MT * NS * 3 + AT * NS, NS, rows=BH)
        q4 = q3 + MT * NS * 3 + AT * NS + NS
        ZXW = TP + 1 + NB * 5
        zx = words(q4, 2, ZXW + 1)
        zd = words(q4 + 2 * (ZXW + 1), 2, ZXW + 1)
        q5 = q4 + 4 * (ZXW + 1)
        bc = words(q5, 2, BH, N)
        wib = words(q5 + 2 * BH * N, BH, SM)
        colg = words(q5 + 2 * BH * N + BH * SM, 3, 2, BH)
        q6 = q5 + 2 * BH * N + BH * SM + 24
        ktok = words(q6, 2, BH, P)
        ktok_s = words(q6 + 2 * BH * P, BH, P, rows=SM)
        q7 = q6 + 3 * BH * P
        vtok = words(q7, 2, BH, DV + 1)
        vtok_s = words(q7 + 2 * BH * (DV + 1), BH, DV + 1, rows=SM)
        q8 = q7 + 3 * BH * (DV + 1)
        DW = TP + P + SM
        dd = words(q0, 2, DW)
        qw = words(q0 + 2 * DW, 2, SM)
        assert 2 * DW + 2 * SM <= 4 * ZQS
        kwm = words(q4, NB, P, rows=SM)
        assert NB * P <= 4 * (ZXW + 1)
        hsq = words(q2, 2, N)
        hh = words(M_AUX + AUX["wg"][0], 2, N)
        c_out = words(M_H + 2 * NB * DV, 2, DV)
        rec = words(q8, 2, N)
        n_out = words(q8 + 2 * N, BH, NS)
        q10 = q8 + 2 * N + BH * NS
        cring = words(M_H, 2, NB, DV)
        za = ARENA - (2 * MT + 2) * N
        assert q10 <= za, (q10, za)
        r = words(M_YMIX, MT, N)
        k = words(za, MT, N)
        v = words(za + MT * N, MT, N)
        low = words(za + 2 * MT * N, 2, N)
        arz = words(M_Q, AH, 2, TP)
        arz_s = words(M_Q + AH * 2 * TP, AH, 2, SM)
        m1 = M_Q + AH * 2 * N
        B = words(m1, MT, N)
        kk = words(m1 + MT * N, MT, N)
        bonus = words(m1 + 2 * MT * N, MT, N)
        lg = words(M_H, MT, N)
        t1 = words(M_H + MT * N, MT, N)
        flat = MT * N
        lgf, t1f, Bf, kkf, bonusf = (words(a, flat) for a in (M_H, M_H + flat, m1, m1 + flat, m1 + 2 * flat))
        rf, kf, vf = words(M_YMIX, flat), words(za, flat), words(za + flat, flat)
        m2 = m1 + 3 * flat
        cen = words(m2, 3, MT, CH)
        cen_s = words(m2 + 3 * MT * CH, MT, NB)
        m3 = m2 + 3 * MT * CH + MT * NB
        state = words(m3, MT, AHD)
        state_c = words(m3 + MT * AHD, MT, AHD)
        HW = HG * AHD
        tok = words(m3 + 2 * MT * AHD, 3, HW)
        tok_s = words(m3 + 2 * MT * AHD, 3, HW, rows=SM)
        assert m3 + 2 * MT * AHD + 3 * HW <= za
        gram = words(M_H, HG, 4, L)
        Ti = words(m1 + flat, HG, L)
        Tt = words(m1 + flat + HG * L, HG, L)
        X = words(M_AUX + AUX["w2"][0], HG, L)
        masked = words(M_AUX + AUX["a2"][0], HG, L)
        W = words(M_AUX + AUX["a2"][0], HW)
        SA = words(M_AUX + AUX["a2"][0] + HW, HW)
        tn = words(M_AUX + AUX["wg"][0], 2, N)
        hrt = words(M_H, 2, N)
        gram_s = words(M_H, HG, 4, SM, rows=SM)
        azm = words(M_H + HG * 4 * SM, HG, NB, SM)
        Ti_s = words(m1 + flat, HG, SM, rows=SM)
        Tt_s = words(m1 + flat + HG * L, HG, SM, rows=SM)
        X_s = words(M_AUX + AUX["w2"][0], HG, SM, rows=SM)
        masked_s = words(M_AUX + AUX["a2"][0], HG, SM, rows=SM)
        W_s = words(M_AUX + AUX["a2"][0], HW, rows=SM)
        SA_s = words(M_AUX + AUX["a2"][0] + HW, HW, rows=SM)
        wkv_s = words(M_Q, MT, NB, AHD)
        sam = words(M_Q + MT * NB * AHD, 2, 4, NB, AHD, rows=SM)

        h2 = words(M_H2, KT, N)
        x1 = words(M_Q, KT, N)
        x1sq = words(M_Q + KT * N, KT, N)
        rms2 = words(M_Q + 2 * KT * N, 2, N)
        gain2 = words(M_Q + 2 * KT * N + 2 * N, KT, NS)
        xt_s = words(M_Q + 2 * KT * N + 2 * N + KT * NS, SM)
        qT = words(M_Q + 3 * KT * N, KT, N)
        keys = words(M_Q + 4 * KT * N, KT, NK)
        assert M_Q + 4 * KT * N + KT * NK <= ARENA
        GR = 2 * PH
        p0 = M_Q
        sc = words(p0, GR, NK)
        sc2 = words(p0 + 2048, GR, NK)
        cand = words(p0 + 4096, PH, TOPK * TOPK)
        cand2 = words(p0 + 6144, PH, TOPK * TOPK)
        eq = words(p0 + 8192, PH * TOPK, TOPK)
        p1 = p0 + 10240
        top = words(p1, GR, TOPK)
        topi = words(p1 + 256, GR, TOPK)
        topf = words(p1 + 512, GR, TOPK)
        best = words(p1 + 768, PH, TOPK)
        posi = words(p1 + 896, PH, TOPK)
        part = words(p1 + 1024, 2, PH, TOPK)
        partf = words(p1 + 1280, 2, PH, TOPK)
        pick = words(p1 + 1536, 3, PH * TOPK)
        psum8 = words(p1 + 1920, 2, PH)
        assert p1 + 1936 <= M_Q + 3 * KT * N
        pickT = words(M_MISC, 3, N)
        hot1 = words(M_MODS, 2, 2, NK)
        hot2 = words(M_MISC + 3 * N, 2, 2, NK)
        G = words(M_G, NK, N)
        gel = words(M_MISC, 2, N)
        xo = words(M_H2, KT, N)
        ysq = words(M_G, KT, N)
        yn = words(M_G + KT * N, KT, N)
        rms3 = words(M_G + 2 * KT * N, 2, N)
        gain3 = words(M_G + 2 * KT * N + 2 * N, KT, NS)
        xs3 = words(M_MISC, SM)

        def samp(v):
            names = " ".join("xyz"[:len(v.shape) - 2])
            return v[..., TP:N].rearrange(f"p {names} (b t) -> p {names} b t", t=TS)

        ADA_TILES, Z_TILES = KT, 2 * AT - 2
        n_ada0 = 0
        n_z = n_ada0 + 2 * ADA_TILES
        n_ada1 = n_z + 50
        n_wo = n_ada1 + 6 * ADA_TILES
        n_q = n_wo + KT
        n_u = n_q + KT
        n_v = n_u + NK
        landed = [S(f"slot{i}_landed") for i in range(RING_SLOTS)]
        used = S("weights_used")

        def arrived(eng, n, i=0):
            eng.wait_ge(landed[n % RING_SLOTS], (i + (n // RING_SLOTS + 1)) * 16)

        ada_order = [SH_A, SC_A, G_A, SH_C, SC_C, G_C, SH_F, SC_F]

        block = ctx.enter_context(nc.Block())

        @block.sync
        def _(sp):
            def load(n, src, i=0, wait=True):
                if wait:
                    sp.wait_ge(used, i * RING_SLOTS + (n - RING_SLOTS + 1))
                sp.dma_start(ring[n % RING_SLOTS], src).then_inc(landed[n % RING_SLOTS], 16)

            def ada(j):
                part = ada_order[j]
                w, at = (T["w_ada"], part * D) if part < 6 else (T["w_adaf"], (part - 6) * D)
                for kt in range(KT):
                    n = (n_ada0 + j * KT if j < 2 else n_ada1 + (j - 2) * KT) + kt
                    load(n, w[kt * P:(kt + 1) * P, at:at + D], wait=n >= RING_SLOTS)

            def tiles(n, src, count, at=0):
                with sp.Fori(0, count // RING_SLOTS) as i:
                    for j in range(RING_SLOTS):
                        load(n + j, src[bass.ds(i * RING_SLOTS + (at + j), 1)].rearrange("o p c -> (o p) c"), i)

            for j in range(2):
                ada(j)
            tiles(n_z, T["w_in"], 24, AT)
            tiles(n_z + 24, T["w_in"], 24)
            for j in range(2):
                load(n_z + 48 + j, T["w_in"][24 + j])
            for j in range(2, 8):
                ada(j)
            tiles(n_wo, T["w_out"], KT)
            tiles(n_q, T["w_q"], KT)
            tiles(n_u, T["peer_u"], NK)
            v_dram = T["peer_v"].rearrange("(a b) d -> b a d", b=NK)
            for half in range(2):
                with sp.Fori(0, NK // 2 // RING_SLOTS) as i:
                    for j in range(RING_SLOTS):
                        n = n_v + half * NK // 2 + j
                        sp.wait_ge(used, i * RING_SLOTS + (n - RING_SLOTS + 1))
                        src = v_dram[bass.ds(i * 2 * RING_SLOTS + 2 * j, 2), :, half * D // 2:(half + 1) * D // 2]
                        sp.dma_start(ring[n % RING_SLOTS].rearrange("p (b d) -> p b d", b=2),
                                     src.rearrange("b a d -> a b d")).then_inc(landed[n % RING_SLOTS], 16)
            for half in range(2):
                sp.wait_ge(S("y_done"), 2)
                sp.dma_start(T["y"][:, half * 8:(half + 1) * 8], yn[:, half * 8:(half + 1) * 8]).then_inc(S("y_stored"), 16)
            sp.wait_ge(S("y_stored"), 32)

        @block.gpsimd
        def _(pool):
            for name, count in (("z_free", 2), ("zq_free", 2), ("zx_free", 2), ("out_free", 2), ("q_free", 2),
                                ("g_free", 2), ("gelu_done", 4), ("acts_ready", 2)):
                pool.sem_inc(S(name), count)
            def store_c(h):
                pool.wait_ge(S("c_new"), h + 1)
                pool.dma_start(T["c_s"][h], cring[:, h % 2]).then_inc(S(f"c_stored{h % 2}"), 16)
                pool.dma_start(T["c_p"][h], c_out[:, h % 2]).then_inc(S(f"cp_stored{h % 2}"), 16)

            pool.wait_ge(used, n_z + 50)
            for h in range(BH):
                if h >= 2:
                    pool.wait_ge(S(f"c_stored{h % 2}"), 16)
                pool.dma_start(cring[:, h % 2], T["c0"][h]).then_inc(S(f"c_landed{h % 2}"), 16)
                if h >= 1:
                    store_c(h - 1)
            store_c(BH - 1)
            pool.wait_ge(S("c_new"), BH)
            pool.dma_start(T["n_all"], n_out).then_inc(S("small_stored"), 16)
            pool.dma_start(T["m_all"], mo).then_inc(S("small_stored"), 16)
            pool.dma_start(T["conv_all"], cvo).then_inc(S("small_stored"), 16)
            pool.dma_start(T["shift_all"], sho).then_inc(S("small_stored"), 16)
            pool.wait_ge(S("small_stored"), 64)
            for slot in range(2):
                pool.wait_ge(S(f"cp_stored{slot}"), 32)
            pool.memset(words(M_Q, AH * 2 * N), 0.0).then_inc(S("arz_clear"), 1)
            pool.wait_ge(S("state_step"), 4)
            pool.dma_start(T["wkv_p"], state).then_inc(S("wkv_stored"), 16)
            pool.dma_start(wkv_s, T["wkv0"]).then_inc(S("wkv_landed"), 16)
            pool.wait_ge(S("wkv_new"), MT)
            pool.dma_start(T["wkv_s"], wkv_s).then_inc(S("wkv_stored"), 16)
            pool.wait_ge(S("wkv_stored"), 32)
            pool.dma_start(x1, T["x"]).then_inc(S("x_again"), 16)
            pool.dma_start(keys, T["keys"]).then_inc(S("keys_landed"), 16)
            pool.wait_ge(S("out_free"), KT + 2)
            pool.dma_start(x1_dram, x1).then_inc(S("x1_spilled"), 16)
            pool.wait_ge(S("x1_spilled"), 16)
            pool.wait_ge(used, n_u + NK)
            pool.dma_start(xo, x1_dram).then_inc(S("x1_back"), 16)
            for slot in range(2):
                pool.wait_ge(S(f"c_stored{slot}"), 32)

        @block.tensor
        def _(pe):
            def matmul(out, lhsT, rhs, start=True, stop=True):
                return pe.matmul(out, lhsT, rhs, start=start, stop=stop)

            def turn(out, in_):
                return pe.transpose(out, in_, ident[0:in_.shape[0], 0:in_.shape[0]])

            def norm_sum(sq, count, bank):
                pe.wait_ge(S("squares"), count)
                for kt in range(KT):
                    mm = matmul(ps[bank][:, 0:N], ones, sq[:, kt, :], kt == 0, kt == KT - 1)
                mm.then_inc(S("square_sum"), 1)

            def ada_turn(j):
                pe.wait_ge(S("ada_copied"), j + 1)
                for b in range(KT):
                    mm = matmul(ps[4][:, b * NS:(b + 1) * NS], adas[:, b * P:(b + 1) * P], cst1("fold")[:, 0:NS])
                mm.then_inc(S("ada_turned"), 1)

            def ada_quarter(j, quarter):
                if quarter == 0 and j > 0:
                    if j != 2:
                        ada_turn(j - 1)
                    pe.wait_ge(S("mods_raw"), j)
                for kt in range(4 * quarter, 4 * quarter + 4):
                    n = (n_ada0 + j * KT if j < 2 else n_ada1 + (j - 2) * KT) + kt
                    arrived(pe, n)
                    g = kt % 4
                    for b in range(4):
                        mm = matmul(ps[4 + b][32 * g:32 * g + 32, :], silc[:, kt, :],
                                    ring[n % RING_SLOTS][:, b * 512:(b + 1) * 512], kt < 4, kt >= KT - 4)
                    mm.then_inc(used, 1)

            pending = [(j, q) for j in range(2, 8) for q in range(4)]

            def ada_more(count):
                for _ in range(min(count, len(pending))):
                    ada_quarter(*pending.pop(0))

            def dense(n, src, i, bank):
                arrived(pe, n, i)
                for kt in range(KT):
                    mm = matmul(ps[bank][:, 0:N], ring[n % RING_SLOTS][:, kt * P:(kt + 1) * P], src[:, kt, :],
                                kt == 0, kt == KT - 1)
                mm.then_inc(used, 1)

            def turn_picks(b):
                w = P if b < 2 else SM
                pe.wait_ge(S("picks_ready"), b + 1)
                if b:
                    pe.wait_ge(S("picks_copied"), b)
                for q in range(3):
                    mm = turn(ps[4][:, q * P:q * P + w], pick[0:w, q, :])
                mm.then_inc(S("picks_turned"), 1)

            pe.wait_ge(S("const_in"), 64)
            norm_sum(xsq, 1, 0)
            pe.wait_ge(S("cond_ready"), 1)
            for j in range(2):
                for q in range(4):
                    ada_quarter(j, q)
            ada_turn(1)

            pe.wait_ge(S("h_ready"), 1)
            pe.wait_ge(S("h_ready_act"), 1)
            with pe.Fori(0, 6) as i:
                for j in range(4):
                    pe.wait_ge(S("z_free"), i * 4 + (j + 1))
                    dense(n_z + j, hT, i, j % 2)
            pe.wait_ge(S("aux_in"), 128)
            wg = aux("wg", KT, 36)
            for kt in range(KT):
                mm = matmul(ps[2][0:36, 0:N], wg[:, kt, :], hT[:, kt, :], kt == 0, kt == KT - 1)
            mm.then_inc(S("gates_ready"), 1)
            with pe.Fori(0, 6) as i:
                for j in range(4):
                    pe.wait_ge(S("z_free"), i * 4 + (24 + j + 1))
                    dense(n_z + 24 + j, hT, i, j % 2)
            for j in range(2):
                pe.wait_ge(S("z_free"), 48 + j + 1)
                dense(n_z + 48 + j, hT, 0, j % 2)

            pe.wait_ge(S("row_exp"), 1)
            for u in range(2 * BH):
                q, h = u // BH, u % BH
                if u >= 2:
                    pe.wait_ge(S("bc_done"), u - 1)
                matmul(ps[2 + u % 2][:, 0:N], cst1("sel", BH, P, rows=BH)[:, h, :],
                       row["em" if q else "mx"]).then_inc(S("bc_ready"), 1)
            pe.wait_ge(S("z_free"), 52)
            for h in range(BH):
                mm = matmul(ps[0][:, h * SM:(h + 1) * SM], cst1("sel", BH, P, rows=BH)[:, h, :], row["wi"][:, 0:SM])
            for q, name in enumerate(("g", "ws")):
                for b in range(3):
                    w = P if b < 2 else SM
                    at = 4 * (2 * b + q)
                    mm = turn(ps[1][0:w, at:at + 4], row[name][:, b * P:b * P + w])
            mm.then_inc(S("cols_ready"), 1)
            pe.wait_ge(S("cols_done"), 1)
            pe.wait_ge(S("bc_done"), 2 * BH)
            fills = [("v", b, g) for b in range(3) for g in range(2)] + [("k", b, 0) for b in range(3)]
            for u, (what, b, g) in enumerate(fills):
                if u >= 4:
                    pe.wait_ge(S("turn_done"), u - 3)
                w = P if b < 2 else SM
                for j in range(4):
                    src = bv[:, 4 * g + j, b * P:b * P + w] if what == "v" else qk[:, BH + j, b * P:b * P + w]
                    mm = turn(ps[u % 4][0:w, j * P:(j + 1) * P], src)
                mm.then_inc(S("turn_ready"), 1)
            pe.wait_ge(S("turn_done"), 9)
            for h in range(BH):
                if h >= 1:
                    pe.wait_ge(S("ms_root"), h)
                matmul(ps[0][:, 0:TP], qk[:, BH + h, 0:P], qk[:, h, 0:TP])
                matmul(ps[0][:, TP:TP + P], qk[:, BH + h, P:TP], qk[:, h, P:TP])
                matmul(ps[0][0:SM, TP + P:DW], qk[:, BH + h, TP:N], qk[:, h, TP:N]).then_inc(S("qk_ready"), 1)
                ada_more(1)
                pe.wait_ge(S("s_ready"), h + 1)
                pe.wait_ge(S(f"c_landed{h % 2}"), 16 * (h // 2 + 1))
                for half in range(3):
                    def vt(b, rows=P):
                        if half == 2:
                            return ones[0:rows, :]
                        src = vtok[:, b, h] if b < 2 else vtok_s[:, h]
                        return src[:, half * P:(half + 1) * P]
                    out = ps[1 + half]
                    matmul(out[:, 0:TP], vt(0), dd[:, 1, 0:TP], True, False)
                    matmul(out[:, P:TP], vt(1), dd[:, 1, TP:TP + P], False, True)
                    mm = matmul(out[:, TP:N], vt(2, SM), dd[0:SM, 1, TP + P:DW], True, False)
                    if half < 2:
                        for b in range(NB):
                            mm = matmul(out[:, TP + b * TS:TP + (b + 1) * TS],
                                        cring[:, h % 2, b, half * P:(half + 1) * P], qw[:, 0, b * TS:(b + 1) * TS],
                                        False, b == NB - 1)
                    else:
                        mm = matmul(out[:, TP:N], ones, qw[:, 1, :], False, True)
                mm.then_inc(S("num_ready"), 1)
                ada_more(1)
                pe.wait_ge(S("hsq_ready"), h + 1)
                pe.wait_ge(S("num_used"), h + 1)
                for i in range(2):
                    mm = matmul(ps[0][:, 0:N], ones, hsq[:, i, :], i == 0, i == 1)
                mm.then_inc(S("ms_ready"), 1)
                pe.wait_ge(S("kwm_ready"), h + 1)
                for u in range(NS):
                    if u >= 3 or h > 0:
                        pe.wait_ge(S("upd_used"), h * NS + u - 2)
                    out = ps[1 + u % 3][:, 0:DV + 1]
                    if u < NB:
                        mm = matmul(out, kwm[:, u, :], vtok_s[:, h, :])
                    else:
                        matmul(out, ktok[:, 0, h, :], vtok[:, 0, h, :], True, False)
                        mm = matmul(out, ktok[:, 1, h, :], vtok[:, 1, h, :], False, True)
                    mm.then_inc(S("upd_ready"), 1)
                pe.wait_ge(S("upd_used"), (h + 1) * NS)

            pe.wait_ge(S("low_ready"), 1)
            pe.wait_ge(S("ms_root"), BH)
            for f in range(MT):
                for q, w in enumerate((aux("w2"), aux("a2"))):
                    if f >= 2:
                        pe.wait_ge(S("low_used"), 2 * (f - 2) + q + 1)
                    matmul(ps[2 * q + f % 2][:, 0:N], w[:, f * P:(f + 1) * P], low[:, 0, :]).then_inc(S("low_sum"), 1)
            ada_more(1)

            def head_sums(src, ready, made, taken):
                pe.wait_ge(S(ready), 1)
                for f in range(MT):
                    if f >= 4:
                        pe.wait_ge(S(taken), f - 3)
                    matmul(ps[f % 4][:, 0:N], blk, src[:, f, :]).then_inc(S(made), 1)

            pe.wait_ge(S("low_used"), 2 * MT)
            head_sums(bonus, "kksq_ready", "kk_sum", "kk_root")
            ada_more(1)
            pe.wait_ge(S("kk_root"), MT)
            head_sums(bonus, "rk_ready", "rk_sum", "bonus_done")
            ada_more(1)
            pe.wait_ge(S("bonus_done"), MT)
            pe.wait_ge(S("ops_ready"), 1)

            for it in range(2 * CH + 2):
                c, hg = (it // 2, it % 2)
                sample = c == CH
                w = SM if sample else L
                f0 = 4 * hg
                cols = slice(TP, N) if sample else slice(c * L, (c + 1) * L)
                if it:
                    pe.wait_ge(S("y_taken"), it)
                    pe.wait_ge(S("state_step") if it <= 4 else S("wkv_new"), min(it, 4) if it <= 4 else 4)
                tk = tok_s if sample else tok
                for q, src in enumerate((B, k, v)):
                    for j in range(4):
                        mm = turn(ps[q][0:w, j * P:(j + 1) * P], src[:, f0 + j, cols])
                    mm.then_inc(S("tok_ready"), 1)
                az = arz_s if sample else arz
                zc = slice(0, SM) if sample else cols
                if sample:
                    for q, src in enumerate((B, k)):
                        if q:
                            pe.wait_ge(S("tok_done"), it * 3 + 3)
                        for d in range(HG):
                            mm = matmul(ps[3 * (1 - q)][0:SM, d * 2 * SM:(d + 1) * 2 * SM],
                                        src[:, f0 + d // 2, cols], az[:, f0 * 2 + d, :, :])
                        mm.then_inc(S("gram_ready"), 1)
                    gram_n = 4 * 8 + 2 * hg
                    pe.wait_ge(S("gram_done"), gram_n + 2)
                else:
                    for g in range(8):
                        q, pair = g // 4, g % 4
                        if g == 1:
                            pe.wait_ge(S("tok_done"), it * 3 + 3)
                        if g >= 4:
                            pe.wait_ge(S("gram_done"), it * 8 + g - 3)
                        for d in (2 * pair, 2 * pair + 1):
                            mm = matmul(ps[(3 + g) % 4][:, (d % 2) * 2 * L:(d % 2 + 1) * 2 * L],
                                        (B, k)[q][:, f0 + d // 2, cols], az[:, f0 * 2 + d, :, cols])
                        mm.then_inc(S("gram_ready"), 1)
                    pe.wait_ge(S("gram_done"), it * 8 + 8)
                ada_more(2)
                levels = 2 if sample else LEVELS
                done = LEVELS * it if it <= 4 else LEVELS * 4 + 2 * hg
                ti, tt, x, mk = (Ti_s, Tt_s, X_s, masked_s) if sample else (Ti, Tt, X, masked)
                halves = 1 if sample else 2
                per = HG // halves
                xd = 2 * LEVELS * min(it, 4) + (2 * hg if sample else 0)
                td = 4 * LEVELS * min(it, 4) + (4 * hg if sample else 0)
                def level(i):
                    pe.wait_ge(S("masked_ready"), i + (done + 1))
                    for q in range(halves):
                        for d in range(q * per, (q + 1) * per):
                            mm = matmul(ps[q][0:w, (d % per) * w:(d % per + 1) * w], mk[:, d, :], ti[:, d, :])
                        mm.then_inc(S("x_sum"), 1)
                    for q in range(halves):
                        pe.wait_ge(S("x_copied"), i * halves + (xd + q + 1))
                        for d in range(q * per, (q + 1) * per):
                            mm = matmul(ps[2 + q][0:w, (d % per) * w:(d % per + 1) * w], tt[:, d, :], x[:, d, :])
                        mm.then_inc(S("t_sum"), 1)
                        for d in range(q * per, (q + 1) * per):
                            mm = matmul(ps[q][0:w, (d % per) * w:(d % per + 1) * w], x[:, d, :], tt[:, d, :])
                        mm.then_inc(S("t_sum"), 1)
                if sample:
                    for i in range(levels):
                        level(i)
                else:
                    with pe.Fori(0, levels) as i:
                        level(i)
                pe.wait_ge(S("t_added"), td + (4 if sample else 4 * LEVELS))
                gm = gram_s if sample else gram
                if sample:
                    pe.wait_ge(S("wkv_landed"), 16)
                    pe.wait_ge(S("azm_ready"), hg + 1)
                for d in range(HG):
                    h, f = f0 * 2 + d, f0 + d // 2
                    out = ps[0][0:w, d * AHD:(d + 1) * AHD]
                    if sample:
                        for b in range(NB):
                            matmul(out, azm[:, d, b, :], wkv_s[:, f, b, :], b == 0, False)
                    elif c:
                        matmul(out, az[:, h, 0, cols], state_c[:, f, :], True, False)
                    mm = matmul(out, gm[:, d, 2, :], tk[:, 2, d * AHD:(d + 1) * AHD], not sample and not c, True)
                mm.then_inc(S("w_sum"), 1)
                pe.wait_ge(S("w_copied"), it + 1)
                ws_, sa_ = (W_s, SA_s) if sample else (W, SA)
                for d in range(HG):
                    mm = matmul(ps[1][0:w, d * AHD:(d + 1) * AHD], tt[:, d, :], ws_[:, d * AHD:(d + 1) * AHD])
                mm.then_inc(S("sa_sum"), 1)
                ada_more(1)
                pe.wait_ge(S("sa_copied"), it + 1)
                for d in range(HG):
                    h, f, hp = f0 * 2 + d, f0 + d // 2, d % 2
                    out = ps[2][64 * hp:64 * hp + 64, (d // 2) * w:(d // 2 + 1) * w]
                    hs = slice(d * AHD, (d + 1) * AHD)
                    matmul(out, sa_[:, hs], gm[:, d, 1, :], True, False)
                    last = not sample and not c
                    mm = matmul(out, tk[:, 2, hs], gm[:, d, 3, :], False, last)
                    if sample:
                        for b in range(NB):
                            mm = matmul(out[:, b * TS:(b + 1) * TS], wkv_s[:, f, b, :],
                                        az[:, h, 1, b * TS:(b + 1) * TS], False, b == NB - 1)
                    elif c:
                        mm = matmul(out, state_c[:, f, :], az[:, h, 1, cols], False, True)
                mm.then_inc(S("y_sum"), 1)
                if not sample:
                    for d in range(HG):
                        hp = d % 2
                        hs = slice(d * AHD, (d + 1) * AHD)
                        out = ps[3][64 * hp:64 * hp + 64, (d // 2) * AHD:(d // 2 + 1) * AHD]
                        matmul(out, tk[:, 0, hs], sa_[:, hs], True, False)
                        mm = matmul(out, tk[:, 1, hs], tk[:, 2, hs], False, True)
                    mm.then_inc(S("state_sum"), 1)
                else:
                    for j in range(4):
                        f = f0 + j
                        if j % 2 == 0:
                            pe.wait_ge(S("sam_ready"), 2 * hg + j // 2 + 1)
                        bank = 3 if j % 2 else 1
                        if f >= 2:
                            pe.wait_ge(S("wkv_new"), f - 1)
                        for hp in range(2):
                            d = 2 * j + hp
                            hs = slice(d * AHD, (d + 1) * AHD)
                            out = ps[bank][64 * hp:64 * hp + 64, :]
                            e = d % 4
                            matmul(out, tk[:, 0, hs], sam[:, 0, e].rearrange("p b i -> p (b i)"), True, False)
                            mm = matmul(out, tk[:, 1, hs], sam[:, 1, e].rearrange("p b i -> p (b i)"), False, True)
                        mm.then_inc(S("wkv_sum"), 1)
            pe.wait_ge(S("wkv_new"), MT)
            pe.wait_ge(S("y_taken"), 2 * CH + 2)

            for f in range(MT):
                if f >= 4:
                    pe.wait_ge(S("centred"), f - 3)
                matmul(ps[f % 4][:, 0:N], blk, ymix[:, f, :]).then_inc(S("mean_sum"), 1)
            pe.wait_ge(S("centred"), MT)
            for f in range(MT):
                pe.wait_ge(S("ysq_ready"), f + 1)
                if f >= 2:
                    pe.wait_ge(S("var_root"), f - 1)
                    pe.wait_ge(S("gated"), f - 1)
                matmul(ps[f % 2][:, 0:N], blk, tn[:, f % 2, :]).then_inc(S("var_sum"), 1)
                matmul(ps[2 + f % 2][:, 0:N], aux("g2")[:, f * P:(f + 1) * P], low[:, 1, :]).then_inc(S("gate_sum"), 1)
            ada_more(len(pending))
            ada_turn(7)

            pe.wait_ge(S("gated"), MT)
            pe.wait_ge(S("var_root"), MT)
            with pe.Fori(0, KT // 4) as i:
                for j in range(4):
                    pe.wait_ge(S("out_free"), i * 4 + (j + 1))
                    dense(n_wo + j, ymix, i, j % 2)
            norm_sum(x1sq, 2, 2)
            pe.wait_ge(S("h_ready"), 2)
            pe.wait_ge(S("h_ready_act"), 2)
            pe.wait_ge(S("out_free"), KT + 2)
            with pe.Fori(0, KT // 4) as i:
                for j in range(4):
                    pe.wait_ge(S("q_free"), i * 4 + (j + 1))
                    dense(n_q + j, h2, i, j % 2)
            pe.wait_ge(S("q_free"), KT + 2)
            pe.wait_ge(S("keys_landed"), 16)

            for b in range(3):
                w = P if b < 2 else SM
                if b:
                    pe.wait_ge(S("score_copied"), b)
                for g in range(GR):
                    key = (g % 2) * PH + g // 2
                    mm = matmul(ps[g // 4][0:w, (g % 4) * NK:(g % 4 + 1) * NK], qT[:, g, b * P:b * P + w],
                                keys[:, key, :])
                mm.then_inc(S("scores"), 1)
                if b:
                    turn_picks(b - 1)
            turn_picks(2)

            pe.wait_ge(S("picks_copied"), 3)
            with pe.Fori(0, N // 4) as i:
                for s in range(2):
                    pe.wait_ge(S("hot_ready"), i * 2 + (s + 1))
                    pe.wait_ge(S("g_free"), i * 2 + (s + 1))
                    for e in range(2):
                        mm = matmul(ps[s][:, e * NK:(e + 1) * NK], hot1[:, s, e, :], hot2[:, s, e, :])
                    mm.then_inc(S("g_sum"), 1)
            pe.wait_ge(S("g_free"), N // 2 + 2)

            with pe.Fori(0, NK // 4) as i:
                for j in range(4):
                    pe.wait_ge(S("gelu_done"), i * 4 + (j + 1))
                    dense(n_u + j, h2, i, j)
            pe.wait_ge(S("gelu_done"), NK + 4)
            pe.wait_ge(S("acts_ready"), NK + 2)

            def v_tiles(half, i, first, last):
                n0 = n_v + half * NK // 2
                for j in range(RING_SLOTS):
                    arrived(pe, n0 + j, i)
                    for e in range(2):
                        for dt in range(8):
                            if first and half and j == 0 and e == 0:
                                pe.wait_ge(S("out_taken"), dt + 1)
                            row_i = (G[:, i * 8 + 2 * j + e, :] if isinstance(i, int) else
                                     G[:, bass.ds(i * 8 + (2 * j + e), 1), :].rearrange("p o n -> p (o n)"))
                            mm = matmul(ps[dt][:, 0:N], ring[(n0 + j) % RING_SLOTS][:, (e * 8 + dt) * P:(e * 8 + dt + 1) * P],
                                        row_i, first and j == 0 and e == 0, last and j == RING_SLOTS - 1 and e == 1)
                    mm.then_inc(used, 1)

            for half in range(2):
                v_tiles(half, 0, True, False)
                with pe.Fori(1, NK // 8 - 1) as i:
                    v_tiles(half, i, False, False)
                v_tiles(half, NK // 8 - 1, False, True)
            pe.wait_ge(S("out_taken"), KT)
            norm_sum(ysq, 3, 0)

        @block.scalar
        def _(act):
            chain = Chain(act, S("act_step"))
            eps = prm("eps", 0)

            def activate(out, in_, func, **kw):
                return act.activation(out, in_, func, **kw)

            def copy(out, in_):
                return act.activation(out, in_, ACT.Copy)

            def root(out, in_, scale, bias):
                return act.activation(out, in_, ACT.Sqrt, bias=bias, scale=scale)

            def norm_root(x_ready, src, sq, roots, c, bank):
                for kt in range(KT):
                    if x_ready:
                        x_ready(kt)
                    ins = activate(sq[:, kt, :], src[:, kt, :], ACT.Square)
                ins.then_inc(S("squares"), 1)
                act.wait_ge(S("square_sum"), c)
                root(roots[:, 0, :], ps[bank][:, 0:N], 1.0 / D, eps).then_inc(S("norm_root"), 1)

            def affine(dst, gains, shift, c, done):
                act.wait_ge(S("xn_ready"), c)
                for kt in range(1, KT, 2):
                    ins = activate(dst[:, kt, 0:TP], dst[:, kt, 0:TP], ACT.Identity, bias=mods[:, shift, kt, 0:1],
                                   scale=gains[:, kt, 0:1])
                ins.then_inc(done, 1)

            def ada_take(j):
                act.wait_ge(used, (n_ada0 + (j + 1) * KT) if j < 2 else (n_ada1 + (j - 1) * KT))
                for b in range(4):
                    ins = copy(adas[:, b * 512:(b + 1) * 512], ps[4 + b][:, :])
                ins.then_inc(S("ada_copied"), 1)

            def ada_store(j):
                act.wait_ge(S("ada_turned"), j + 1)
                copy(mods[:, ada_order[j]].rearrange("p k s -> p (k s)"), ps[4][:, 0:KT * NS]).then_inc(S("mods_raw"), 1)

            pending = [(j, q) for j in range(2, 8) for q in range(4)]

            def ada_more(count):
                for _ in range(min(count, len(pending))):
                    j, q = pending.pop(0)
                    if q == 0 and j > 2:
                        ada_store(j - 1)
                    if q == 3:
                        ada_take(j)

            act.dma_start(words(M_PRM, PRM_N), T["prm"]).then_inc(S("const_in"), 16)
            act.dma_start(craw, T["c"]).then_inc(S("const_in"), 16)
            act.dma_start(words(M_CST0, CST0_N), T["cst0"]).then_inc(S("const_in"), 16)
            act.dma_start(words(M_CST1, CST1_N), T["cst1"]).then_inc(S("const_in"), 16)
            for half in range(2):
                act.dma_start(xT[:, half * 8:(half + 1) * 8], T["x"][:, half * 8:(half + 1) * 8]).then_inc(S("x_in"), 16)
            for name, src, dst in (("n0", T["n0"], aux("n0")), ("m0", T["m0"], aux("m0", rows=BH)),
                                   ("conv", T["conv0"], aux("conv")), ("shift", T["shift0"], aux("shift")),
                                   ("wg", T["w_g"], aux("wg")), ("w2", T["w2"], aux("w2")), ("a2", T["a2"], aux("a2")),
                                   ("g2", T["g2"], aux("g2"))):
                act.dma_start(dst, src).then_inc(S("aux_in"), 16)

            act.wait_ge(S("const_in"), 64)
            activate(csig, craw, ACT.Sigmoid).then_inc(S("cond_sig"), 1)
            act.wait_ge(S("x_in"), 32)
            norm_root(None, xT, xsq, rms, 1, 0)
            ada_take(0)
            ada_store(0)
            ada_take(1)
            ada_store(1)
            affine(hT, gain, SH_A, 1, S("h_ready_act"))

            act.wait_ge(S("aux_in"), 128)
            zqs = zq[:, :, TP + 3:ZQW].rearrange("p s (b t) -> p s b t", t=7)
            conv0 = aux("conv", MT, NB, 3)
            act.wait_ge(S("pads_ready"), 3)
            with act.Fori(0, 2) as i:
                for j in range(4):
                    act.wait_ge(used, i * 4 + (n_z + j + 1))
                    act.wait_ge(S("zq_free"), i * 4 + (j + 1))
                    copy(zq[:, j % 2, 3:TP + 3], ps[j % 2][:, 0:TP])
                    copy(zqs[:, j % 2, :, 3:7], ps[j % 2][:, TP:N].rearrange("p (b t) -> p b t", t=TS)).then_inc(S("z_free"), 1)
                    copy(zqs[:, j % 2, :, 0:3],
                         conv0[:, bass.ds(i * 4 + j, 1)].rearrange("p o b t -> p (o b) t")).then_inc(S("zq_full"), 1)
                    act.wait_ge(S("conv_ready"), i * 4 + (j + 1))
                    activate(conv[:, 1, 0:TP + 56], conv[:, 0, 0:TP + 56], ACT.Sigmoid).then_inc(S("sig_ready"), 1)
            with act.Fori(0, 2) as i:
                for j in range(4):
                    act.wait_ge(used, i * 4 + (n_z + 8 + j + 1))
                    copy(bv[:, bass.ds(i * 4 + j, 1)].rearrange("p o n -> p (o n)"), ps[j % 2][:, 0:N]).then_inc(S("z_free"), 1)
            with act.Fori(0, 2) as i:
                for j in range(4):
                    act.wait_ge(used, i * 4 + (n_z + 16 + j + 1))
                    activate(ymix[:, bass.ds(i * 4 + (MT + j), 1)].rearrange("p o n -> p (o n)"), ps[j % 2][:, 0:N],
                             ACT.Sigmoid).then_inc(S("z_free"), 1)
            act.wait_ge(S("row_abs"), 1)
            chain.link(activate(row["t"], row["t"], ACT.Exp, scale=-1.0))
            activate(row["t"], row["t"], ACT.Ln, bias=ones[0:BH, 0:1]).then_inc(S("row_ln"), 1)
            act.wait_ge(S("row_done"), 1)
            activate(row["em"], row["m"], ACT.Exp, scale=-1.0)
            activate(row["ws"], row["ws"], ACT.Exp)
            activate(row["wi"][:, 0:SM], row["wi"][:, 0:SM], ACT.Exp).then_inc(S("row_exp"), 1)

            zxs = zx[:, :, TP + 1:ZXW].rearrange("p s (b t) -> p s b t", t=5)
            shift0 = aux("shift", AT, NB)

            def take_z(i, j, n):
                act.wait_ge(used, i * 4 + (n_z + 24 + n + 1))
                act.wait_ge(S("zx_free"), i * 4 + (n + 1))
                copy(zx[:, j % 2, 1:TP + 1], ps[j % 2][:, 0:TP])
                copy(zxs[:, j % 2, :, 1:5], ps[j % 2][:, TP:N].rearrange("p (b t) -> p b t", t=TS)).then_inc(S("z_free"), 1)
                src = shift0[:, n] if isinstance(i, int) else shift0[:, bass.ds(i * 4 + n, 1)].rearrange("p o b -> p (o b)")
                copy(zxs[:, j % 2, :, 0], src).then_inc(S("zx_full"), 1)

            with act.Fori(0, 6) as i:
                for j in range(4):
                    take_z(i, j, j)
            for j in range(2):
                take_z(0, j, 24 + j)
            act.wait_ge(S("zx_free"), AT + 2)
            activate(low[0:64, 0, :], low[0:64, 0, :], ACT.Tanh)
            activate(low[:, 1, :], low[:, 1, :], ACT.Sigmoid).then_inc(S("low_ready"), 1)

            for u in range(2 * BH):
                act.wait_ge(S("bc_ready"), u + 1)
                copy(bc[:, u // BH, u % BH, :], ps[2 + u % 2][:, 0:N]).then_inc(S("bc_done"), 1)
            for h in range(BH):
                ada_more(1)
                act.wait_ge(S("d_ready"), h + 1)
                activate(dd[:, 0, 0:TP + P], dd[:, 0, 0:TP + P], ACT.Exp, scale=-1.0)
                activate(dd[0:SM, 0, TP + P:DW], dd[0:SM, 0, TP + P:DW], ACT.Exp, scale=-1.0).then_inc(S("d_exp"), 1)
                ada_more(1)
                act.wait_ge(S("num_used"), h + 1)
                activate(hsq, hh, ACT.Square).then_inc(S("hsq_ready"), 1)
                act.wait_ge(S("ms_ready"), h + 1)
                root(rec[:, 1, :], ps[0][:, 0:N], 1.0 / DV, eps).then_inc(S("ms_root"), 1)

            for slot in range(2):
                act.wait_ge(S(f"c_stored{slot}"), 32)
            act.wait_ge(S("arz_clear"), 1)
            act.wait_ge(S("c_new"), BH)
            for f in range(MT):
                for q, dst, bias in ((0, lg, "w0"), (1, B, "a0")):
                    act.wait_ge(S("low_sum"), 2 * f + q + 1)
                    activate(dst[:, f, :], ps[2 * q + f % 2][:, 0:N], ACT.Sigmoid, bias=prm(bias, f)).then_inc(S("low_used"), 1)
            ada_more(1)
            act.wait_ge(S("kk_ready"), 1)
            activate(bonus, kk, ACT.Square).then_inc(S("kksq_ready"), 1)
            ada_more(1)
            for f in range(MT):
                act.wait_ge(S("kk_sum"), f + 1)
                root(bonus[:, f, :], ps[f % 4][:, 0:N], 1.0, prm("zero", 0)).then_inc(S("kk_root"), 1)
            act.wait_ge(S("logs_ready"), 1)
            activate(words(m2, 3 * MT * CH + MT * NB), words(m2, 3 * MT * CH + MT * NB), ACT.Exp)
            activate(t1, t1, ACT.Exp).then_inc(S("before_ready"), 1)
            act.wait_ge(S("a_done"), 1)
            chain.link(activate(t1, lg, ACT.Exp))
            activate(lg, lg, ACT.Exp, scale=-1.0).then_inc(S("decays_ready"), 1)
            ada_more(1)

            for it in range(2 * CH + 2):
                c, hg = it // 2, it % 2
                sample = c == CH
                w = SM if sample else L
                f0 = 4 * hg
                tk = tok_s if sample else tok
                for q in range(3):
                    act.wait_ge(S("tok_ready"), it * 3 + q + 1)
                    copy(tk[:, q, :], ps[q][0:w, :]).then_inc(S("tok_done"), 1)
                ada_more(2)
                levels = 2 if sample else LEVELS
                halves = 1 if sample else 2
                x = X_s if sample else X
                per = HG // halves
                xd = 2 * LEVELS * min(it, 4) + (2 * hg if sample else 0)
                with act.Fori(0, levels) as i:
                    for q in range(halves):
                        act.wait_ge(S("x_sum"), i * halves + (xd + q + 1))
                        copy(x[:, q * per:(q + 1) * per, :].rearrange("p h t -> p (h t)"),
                             ps[q][0:w, 0:per * w]).then_inc(S("x_copied"), 1)
                act.wait_ge(S("w_sum"), it + 1)
                copy(W_s if sample else W, ps[0][0:w, :]).then_inc(S("w_copied"), 1)
                act.wait_ge(S("sa_sum"), it + 1)
                copy(SA_s if sample else SA, ps[1][0:w, :]).then_inc(S("sa_copied"), 1)
                ada_more(1)
                act.wait_ge(S("y_sum"), it + 1)
                copy(ymix[:, f0:f0 + 4, slice(TP, N) if sample else slice(c * L, (c + 1) * L)],
                     ps[2][:, 0:4 * w].rearrange("p (f t) -> p f t", f=4)).then_inc(S("y_taken"), 1)

            for f in range(MT):
                act.wait_ge(S("centred"), f + 1)
                if f >= 2:
                    act.wait_ge(S("var_sum"), f - 1)
                activate(tn[:, f % 2, :], ymix[:, f, :], ACT.Square).then_inc(S("ysq_ready"), 1)
                act.wait_ge(S("var_sum"), f + 1)
                root(hrt[:, f % 2, :], ps[f % 2][:, 0:N], 1.0 / AHD, prm("gneps", 0)).then_inc(S("var_root"), 1)
            ada_more(len(pending))
            ada_store(7)

            def x1_tile(kt):
                act.wait_ge(S("out_free"), kt + 3)
            norm_root(x1_tile, x1, x1sq, rms2, 2, 2)
            affine(h2, gain2, SH_C, 2, S("h_ready_act"))
            with act.Fori(0, KT // 4) as i:
                for j in range(4):
                    act.wait_ge(used, i * 4 + (n_q + j + 1))
                    copy(qT[:, bass.ds(i * 4 + j, 1)].rearrange("p o n -> p (o n)"), ps[j % 2][:, 0:N]).then_inc(S("q_free"), 1)

            def copy_picks(b):
                w = P if b < 2 else SM
                act.wait_ge(S("picks_turned"), b + 1)
                copy(pickT[:, :, b * P:b * P + w],
                     ps[4][:, 0:3 * P].rearrange("p (q t) -> p q t", q=3)[:, :, 0:w]).then_inc(S("picks_copied"), 1)

            act.wait_ge(S("x1_spilled"), 16)
            for b in range(3):
                w = P if b < 2 else SM
                act.wait_ge(S("scores"), b + 1)
                if b:
                    act.wait_ge(S("picks_ready"), b)
                for q in range(4):
                    ins = copy(sc[0:w, 4 * q:4 * q + 4].rearrange("p g k -> p (g k)"), ps[q][0:w, :])
                ins.then_inc(S("score_copied"), 1)
                if b:
                    copy_picks(b - 1)
                act.wait_ge(S("gate_arg"), b + 1)
                activate(best[0:w], best[0:w], ACT.Exp).then_inc(S("gate_exp"), 1)
            copy_picks(2)

            with act.Fori(0, N // 4) as i:
                for s in range(2):
                    act.wait_ge(S("g_sum"), i * 2 + (s + 1))
                    copy(G[:, :, bass.ds(i * 4 + 2 * s, 2)].rearrange("p k t -> p t k"),
                         ps[s][:, 0:2 * NK].rearrange("p (t k) -> p t k", t=2)).then_inc(S("g_free"), 1)
            with act.Fori(0, NK // 4) as i:
                for j in range(4):
                    act.wait_ge(used, i * 4 + (n_u + j + 1))
                    act.wait_ge(S("acts_ready"), i * 4 + (j + 1))
                    activate(gel[:, j % 2, :], ps[j][:, 0:N], ACT.Gelu).then_inc(S("gelu_done"), 1)

            act.wait_ge(used, n_v + NK)
            def x2_tile(kt):
                act.wait_ge(S("out_taken"), kt + 1)
            norm_root(x2_tile, xo, ysq, rms3, 3, 0)
            affine(yn, gain3, SH_F, 3, S("y_done"))

        @block.vector
        def _(dve):
            chain = Chain(dve, S("dve_step"))
            link = chain.link
            tt = dve.tensor_tensor
            stt = dve.scalar_tensor_tensor

            def ts(out, in_, s1, s2, op0, op1=None):
                if op1 is None:
                    return dve.tensor_scalar(out, in_, s1, None, op0)
                return dve.tensor_scalar(out, in_, s1, s2, op0, op1)

            def add_bias(first, count):
                m = mods[:, first:first + count].rearrange("p m k s -> p (m k) s")
                link(tt(m, m, over(prm("bada", first * KT, count * KT), 2, NS), ALU.add))

            def norm(src, dst, roots, gains, shift, scale, g, c, done):
                link(stt(out=gains, in0=mods[:, scale], scalar=1.0, in1=over(prm(g), 2, NS), op0=ALU.add, op1=ALU.mult))
                dve.wait_ge(S("norm_root"), c)
                link(dve.reciprocal(roots[:, 1, :], roots[:, 0, :]))
                tt(dst, src, over(roots[:, 1, :], 1, KT), ALU.mult).then_inc(S("xn_ready"), 1)
                dve.wait_ge(S("xn_ready"), c)
                for kt in range(0, KT, 2):
                    ts(dst[:, kt, 0:TP], dst[:, kt, 0:TP], gains[:, kt, 0:1], mods[:, shift, kt, 0:1], ALU.mult, ALU.add)
                link(tt(samp(dst), samp(dst), over(gains[:, :, 1:], 3, TS), ALU.mult))
                tt(samp(dst), samp(dst), over(mods[:, shift, :, 1:], 3, TS), ALU.add).then_inc(done, 1)

            dve.wait_ge(S("cond_sig"), 1)
            link(dve.memset(silc, 0.0))
            tt(silc[:, :, 0:NS], craw, csig, ALU.mult).then_inc(S("cond_ready"), 1)
            dve.wait_ge(S("mods_raw"), 2)
            add_bias(0, 2)
            norm(xT, hT, rms, gain, SH_A, SC_A, "gmix", 1, S("h_ready"))
            dve.wait_ge(S("h_ready"), 1)
            dve.wait_ge(S("h_ready_act"), 1)

            dve.memset(zq, 0.0).then_inc(S("pads_ready"), 1)
            dve.memset(zx, 0.0).then_inc(S("pads_ready"), 1)
            dve.memset(words(q7, 3 * BH * (DV + 1)), 1.0).then_inc(S("pads_ready"), 1)
            CW = TP + 56
            dve.wait_ge(S("pads_ready"), 3)
            for is_k in range(2):
                scale = 1.0 if is_k == 0 else DQK ** -0.5
                for j in range(4):
                    n = 4 * is_k + j
                    dve.wait_ge(S("zq_free"), n + 2)
                    dve.wait_ge(S("zq_full"), n + 1)
                    z = zq[:, j % 2]
                    wcol = [prm("convw", tap * MT + n) for tap in range(CONV)]
                    dve.tensor_copy(cvo[:, n], z[:, TP:TP + 7 * NS].rearrange("p (b t) -> p b t", t=7)[:, :, 0:3])
                    link(ts(conv[:, 0, 0:CW], z[:, 0:CW], wcol[0], prm("convb", n), ALU.mult, ALU.add))
                    for tap in range(1, CONV):
                        ins = stt(out=conv[:, 0, 0:CW], in0=z[:, tap:tap + CW], scalar=wcol[tap], in1=conv[:, 0, 0:CW],
                                  op0=ALU.mult, op1=ALU.add)
                        if tap < CONV - 1:
                            link(ins)
                    ins.then_inc(S("conv_ready"), 1)
                    dve.wait_ge(S("sig_ready"), n + 1)
                    stt(out=qk[:, n, 0:TP], in0=conv[:, 0, 0:TP], scalar=scale, in1=conv[:, 1, 0:TP], op0=ALU.mult, op1=ALU.mult)
                    c4 = [conv[:, e, TP + 3:TP + 3 + 56].rearrange("p (b t) -> p b t", t=7)[:, :, 0:TS] for e in range(2)]
                    stt(out=qk[:, n, TP:N].rearrange("p (b t) -> p b t", t=TS), in0=c4[0], scalar=scale, in1=c4[1],
                        op0=ALU.mult, op1=ALU.mult).then_inc(S("zq_free"), 1)

            dve.wait_ge(S("gates_ready"), 1)
            ts(row["i"], ps[2][0:BH, 0:N], prm("gatebias", 0, rows=BH), None, ALU.add)
            link(ts(row["f"], ps[2][32:32 + BH, 0:N], prm("gatebias", 0, rows=BH, first=32), None, ALU.add))
            stt(out=row["t"], in0=row["f"], scalar=-1.0, in1=row["f"], op0=ALU.mult, op1=ALU.max).then_inc(S("row_abs"), 1)
            dve.wait_ge(S("row_ln"), 1)
            link(stt(out=row["f"], in0=row["f"], scalar=0.0, in1=row["t"], op0=ALU.min, op1=ALU.subtract))
            link(dve.tensor_tensor_scan(row["b"], cst1("breset", rows=BH), row["f"], 0.0, ALU.mult, ALU.add))
            link(tt(row["g"], row["i"], row["b"], ALU.subtract))
            link(dve.tensor_copy(row["g2"], row["g"]))
            ts(row["g2"][:, 0:1], row["g"][:, 0:1], 0.0, None, ALU.max)
            link(tt(row["g2"][:, TP:N:TS], row["g"][:, TP:N:TS], aux("m0", rows=BH), ALU.max))
            link(dve.tensor_tensor_scan(row["mx"], cst1("mreset", rows=BH), row["g2"], 0.0, ALU.add, ALU.max))
            tt(row["m"], row["b"], row["mx"], ALU.add)
            ts(row["ws"][:, 0:TP], row["g"][:, 0:TP], row["mx"][:, TP - 1:TP], None, ALU.subtract)
            tt(samp(row["ws"]), samp(row["g"]), over(row["mx"][:, TP + 3:N:TS], 2, TS), ALU.subtract)
            link(tt(row["wi"][:, 0:SM].rearrange("p (b t) -> p b t", t=TS), over(aux("m0", rows=BH), 2, TS),
                    samp(row["mx"]), ALU.subtract))
            dve.tensor_copy(mo, row["m"][:, TP - 1:N:TS]).then_inc(S("row_done"), 1)

            zxs = zx[:, :, TP + 1:ZXW].rearrange("p s (b t) -> p s b t", t=5)
            zds = zd[:, 0, TP:ZXW - 1].rearrange("p (b t) -> p b t", t=5)

            def shift_z(i, j, n, dst, at):
                def pick_(a, m):
                    return a[:, m] if isinstance(i, int) else a[:, bass.ds(i * 4 + m, 1)].rearrange("p o n -> p (o n)")
                mu = prm("mu", n) if isinstance(i, int) else prm("mu")[:, bass.ds(i * 4 + n, 1)]
                dve.wait_ge(S("zx_free"), i * 4 + (n + 2))
                dve.wait_ge(S("zx_full"), i * 4 + (n + 1))
                z = zx[:, j % 2]
                link(tt(zd[:, 0, 0:ZXW - 1], z[:, 0:ZXW - 1], z[:, 1:ZXW], ALU.subtract))
                out = pick_(dst, at)
                stt(out=out[:, 0:TP], in0=zd[:, 0, 0:TP], scalar=mu, in1=z[:, 1:TP + 1], op0=ALU.mult, op1=ALU.add)
                stt(out=out[:, TP:N].rearrange("p (b t) -> p b t", t=TS), in0=zds[:, :, 1:5], scalar=mu,
                    in1=zxs[:, j % 2, :, 1:5], op0=ALU.mult, op1=ALU.add)
                dve.tensor_copy(pick_(sho, n), z[:, TP:ZXW:5]).then_inc(S("zx_free"), 1)

            for first, count, dst in ((0, 2, r), (8, 4, words(za, 2 * MT, N))):
                base = chain.n
                with dve.Fori(0, count) as i:
                    chain.n = i * 4 + base
                    for j in range(4):
                        shift_z(i, j, first + j, dst, j)
                chain.n = base + 4 * count
            for j in range(2):
                shift_z(0, j, 24 + j, low, j)

            dve.wait_ge(S("cols_ready"), 1)
            dve.tensor_copy(wib.rearrange("p h t -> p (h t)"), ps[0][:, 0:BH * SM])
            dve.tensor_copy(colg[:, 0:2].rearrange("p b q h -> p (b q h)"), ps[1][:, 0:16])
            ins = dve.tensor_copy(colg[0:SM, 2].rearrange("p q h -> p (q h)"), ps[1][0:SM, 16:24])
            ins.then_inc(S("cols_done"), 1)
            dve.wait_ge(S("cols_done"), 1)
            fills = [("v", b, g) for b in range(3) for g in range(2)] + [("k", b, 0) for b in range(3)]
            for u, (what, b, g) in enumerate(fills):
                dve.wait_ge(S("turn_ready"), u + 1)
                w = P if b < 2 else SM
                src = ps[u % 4][0:w, :]
                if what == "v":
                    out = vtok[:, b] if b < 2 else vtok_s
                    ins = dve.tensor_copy(out[:, 2 * g:2 * g + 2, 0:DV], src.rearrange("p (h d) -> p h d", h=2))
                else:
                    out = ktok[:, b] if b < 2 else ktok_s
                    ins = tt(out, src.rearrange("p (h d) -> p h d", h=BH), over(colg[0:w, b, 1, :], 2, P), ALU.mult)
                ins.then_inc(S("turn_done"), 1)
            dve.wait_ge(S("turn_done"), 9)
            dve.wait_ge(S("bc_done"), 2 * BH)
            incl, sincl = cst1("incl"), cst1("sincl", rows=SM)
            n0 = aux("n0", BH, NB)
            for h in range(BH):
                if h:
                    dve.wait_ge(S("c_new"), h)
                mx = bc[:, 0, h, :]
                ts(dd[:, 0, 0:TP], mx[:, 0:TP], colg[:, 0, 0, h:h + 1], 0.0, ALU.subtract, ALU.max)
                ts(dd[:, 0, TP:TP + P], mx[:, P:TP], colg[:, 1, 0, h:h + 1], 0.0, ALU.subtract, ALU.max)
                ts(dd[0:SM, 0, TP + P:DW], mx[0:SM, TP:N], colg[0:SM, 2, 0, h:h + 1], 0.0, ALU.subtract,
                   ALU.max).then_inc(S("d_ready"), 1)
                link(tt(qw[:, 0, :], qk[:, h, TP:N], wib[:, h, :], ALU.mult))
                tt(qw[:, 1, :].rearrange("p (b t) -> p b t", t=TS), qw[:, 0, :].rearrange("p (b t) -> p b t", t=TS),
                   over(n0[:, h, :], 2, TS), ALU.mult)
                tt(kwm, over(ktok_s[:, h, :], 1, NB), over(cst1("seq", rows=SM), 2, P), ALU.mult).then_inc(S("kwm_ready"), 1)
                dve.wait_ge(S("d_exp"), h + 1)
                tt(dd[:, 0, 0:P], dd[:, 0, 0:P], incl, ALU.mult)
                tt(dd[:, 0, TP:TP + P], dd[:, 0, TP:TP + P], incl, ALU.mult)
                link(tt(dd[0:SM, 0, TP + P:DW], dd[0:SM, 0, TP + P:DW], sincl, ALU.mult))
                dve.wait_ge(S("qk_ready"), h + 1)
                tt(dd[:, 1, 0:TP + P], ps[0][:, 0:TP + P], dd[:, 0, 0:TP + P], ALU.mult)
                tt(dd[0:SM, 1, TP + P:DW], ps[0][0:SM, TP + P:DW], dd[0:SM, 0, TP + P:DW], ALU.mult).then_inc(S("s_ready"), 1)
                dve.wait_ge(S("num_ready"), h + 1)
                link(stt(out=rec[:, 0, :], in0=ps[3][:, 0:N], scalar=-1.0, in1=bc[:, 1, h, :], op0=ALU.mult, op1=ALU.max))
                link(tt(rec[:, 0, :], ps[3][:, 0:N], rec[:, 0, :], ALU.max))
                link(dve.reciprocal(rec[:, 0, :], rec[:, 0, :]))
                tt(hh[:, 0, :], ps[1][:, 0:N], rec[:, 0, :], ALU.mult)
                tt(hh[:, 1, :], ps[2][:, 0:N], rec[:, 0, :], ALU.mult).then_inc(S("num_used"), 1)
                if h >= 2:
                    dve.wait_ge(S(f"cp_stored{h % 2}"), 16)
                for u in range(NS):
                    dve.wait_ge(S("upd_ready"), h * NS + u + 1)
                    out = ps[1 + u % 3]
                    if u < NB:
                        dC = wib[:, h, u * TS + 3:u * TS + 4]
                        c_u = cring[:, h % 2, u, :]
                        stt(out=c_u, in0=c_u, scalar=dC, in1=out[:, 0:DV], op0=ALU.mult, op1=ALU.add)
                        ins = stt(out=n_out[:, h, u + 1:u + 2], in0=n0[:, h, u:u + 1], scalar=dC, in1=out[:, DV:DV + 1],
                                  op0=ALU.mult, op1=ALU.add)
                    else:
                        dve.tensor_copy(n_out[:, h, 0:1], out[:, DV:DV + 1])
                        ins = dve.tensor_copy(c_out[:, h % 2, :], out[:, 0:DV])
                    ins.then_inc(S("upd_used"), 1)
                dve.wait_ge(S("upd_used"), (h + 1) * NS)
                dve.wait_ge(S("num_used"), h + 1)
                dve.wait_ge(S("ms_root"), h + 1)
                link(dve.reciprocal(rec[:, 1, :], rec[:, 1, :]))
                for i in range(2):
                    n = 2 * h + i
                    ins = stt(out=hh[:, i, :], in0=hh[:, i, :], scalar=prm("bnorm", n), in1=rec[:, 1, :], op0=ALU.mult,
                              op1=ALU.mult)
                link(ins)
                tt(ymix[:, MT + 2 * h:MT + 2 * h + 2, :], ymix[:, MT + 2 * h:MT + 2 * h + 2, :], hh,
                   ALU.mult).then_inc(S("c_new"), 1)
            dve.wait_ge(S("c_new"), BH)

            dve.wait_ge(S("arz_clear"), 1)
            dve.wait_ge(S("low_used"), 2 * MT)
            tt(kk, k, over(prm("kk"), 2, N), ALU.mult).then_inc(S("kk_ready"), 1)
            link(ts(t1f, lgf, -math.exp(-0.5), None, ALU.mult))
            for f in range(MT):
                ins = dve.tensor_tensor_scan(lg[:, f, :], cst1("wreset"), t1[:, f, :], 0.0, ALU.mult, ALU.add)
            link(ins)
            centre, end = lg[:, :, L // 2 - 1:TP:L], lg[:, :, L - 1:TP:L]
            dve.tensor_copy(cen[:, 0], centre)
            dve.tensor_copy(cen[:, 2], end)
            dve.tensor_copy(cen_s, lg[:, :, TP + TS - 1:N:TS])
            link(tt(cen[:, 1], end, centre, ALU.subtract))
            lgp = lg[:, :, 0:TP].rearrange("p f (c t) -> p f c t", t=L)
            link(tt(lgp, lgp, over(cen[:, 0], 3, L), ALU.subtract))
            tt(t1f, lgf, t1f, ALU.subtract).then_inc(S("logs_ready"), 1)
            dve.wait_ge(S("kk_root"), MT)
            link(ts(bonusf, bonusf, 1e-12, None, ALU.max))
            link(dve.reciprocal(bonusf, bonusf))
            link(tt(kkf, kkf, bonusf, ALU.mult))

            def halves(slot, op):
                for hp in range(2):
                    rows = slice(64 * hp, 64 * hp + 64)
                    op(arz[rows, hp::2, slot, :], rows, slice(0, TP))
                    ins = op(arz_s[rows, hp::2, slot, :], rows, slice(TP, N))
                return ins

            dve.wait_ge(S("before_ready"), 1)
            halves(0, lambda out, rows, cols: stt(out=out, in0=kk[rows, :, cols], scalar=-1.0, in1=t1[rows, :, cols],
                                                  op0=ALU.mult, op1=ALU.mult)).then_inc(S("a_done"), 1)
            link(stt(out=bonus, in0=B, scalar=-1.0, in1=over(prm("ka"), 2, N), op0=ALU.add, op1=ALU.mult))
            link(stt(out=kf, in0=bonusf, scalar=1.0, in1=kf, op0=ALU.add, op1=ALU.mult))
            tt(Bf, Bf, kkf, ALU.mult)
            link(tt(bonusf, rf, kf, ALU.mult))
            tt(bonus, bonus, over(prm("rk"), 2, N), ALU.mult).then_inc(S("rk_ready"), 1)
            dve.wait_ge(S("rk_ready"), 1)
            dve.wait_ge(S("decays_ready"), 1)
            halves(1, lambda out, rows, cols: tt(out, r[rows, :, cols], t1[rows, :, cols], ALU.mult))
            tt(kf, kf, lgf, ALU.mult)
            tt(Bf, Bf, lgf, ALU.mult).then_inc(S("ops_ready"), 1)
            for f in range(MT):
                dve.wait_ge(S("rk_sum"), f + 1)
                tt(bonus[:, f, :], ps[f % 4][:, 0:N], v[:, f, :], ALU.mult).then_inc(S("bonus_done"), 1)

            both = words(M_CST1 + CST1["strict"][0], 2 * L)
            both_s = words(M_CST1 + CST1["sstrict"][0], 2 * SM, rows=SM)
            for it in range(2 * CH + 2):
                c, hg = it // 2, it % 2
                sample = c == CH
                w = SM if sample else L
                f0 = 4 * hg
                ti, tt_, mk, gm = (Ti_s, Tt_s, masked_s, gram_s) if sample else (Ti, Tt, masked, gram)
                fills = 2 if sample else 8
                n_gram = 8 * min(it, 4) + (2 * hg if sample else 0)
                for g in range(fills):
                    dve.wait_ge(S("gram_ready"), n_gram + g + 1)
                    if sample:
                        ins = tt(gm[:, :, 2 * g:2 * g + 2, :].rearrange("p h q t -> p h (q t)"),
                                 ps[3 * (1 - g)][0:w, :].rearrange("p (h x) -> p h x", h=HG), over(both_s, 1, HG), ALU.mult)
                    else:
                        q, pair = g // 4, g % 4
                        ins = tt(gm[:, 2 * pair:2 * pair + 2, 2 * q:2 * q + 2, :].rearrange("p h q t -> p h (q t)"),
                                 ps[(3 + g) % 4][:, :].rearrange("p (h x) -> p h x", h=2), over(both, 1, 2), ALU.mult)
                    ins.then_inc(S("gram_done"), 1)
                    if g == 0:
                        dve.tensor_copy(ti, over(ident[0:w, 0:w], 1, HG))
                        link(dve.tensor_copy(tt_, over(ident[0:w, 0:w], 1, HG)))
                        if sample:
                            tt(azm, over(arz_s[:, 2 * f0:2 * f0 + HG, 0, :], 2, NB), over(cst1("seqcol", NB, SM), 1, HG),
                               ALU.mult).then_inc(S("azm_ready"), 1)
                dve.wait_ge(S("gram_done"), n_gram + fills)
                levels = 2 if sample else LEVELS
                halves_ = 1 if sample else 2
                per = HG // halves_
                td = 4 * LEVELS * min(it, 4) + (4 * hg if sample else 0)
                masks = cst1("slevel", 2, SM, rows=SM) if sample else cst1("level", LEVELS, L)
                with dve.Fori(0, levels) as i:
                    tt(mk, gm[:, :, 0, :], over(masks[:, bass.ds(i, 1)].rearrange("p o t -> p (o t)"), 1, HG),
                       ALU.mult).then_inc(S("masked_ready"), 1)
                    for q in range(halves_):
                        hs = slice(q * per, (q + 1) * per)
                        for e, (dst, bank) in enumerate(((ti, 2 + q), (tt_, q))):
                            k_ = 2 * q + e
                            dve.wait_ge(S("t_sum"), i * (2 * halves_) + (td + k_ + 1))
                            tt(dst[:, hs, :], dst[:, hs, :], ps[bank][0:w, 0:per * w].rearrange("p (h t) -> p h t", h=per),
                               ALU.add).then_inc(S("t_added"), 1)
                    dve.wait_ge(S("t_added"), i * (2 * halves_) + (td + 2 * halves_))
                if not sample:
                    fs = slice(f0, f0 + 4)
                    dve.wait_ge(S("state_sum"), it + 1)
                    src = ps[3][:, 0:4 * AHD].rearrange("p (f i) -> p f i", f=4)
                    fresh = over(cen[:, 1, fs, c], 2, AHD)
                    if c == 0:
                        link(tt(state[:, fs], src, fresh, ALU.mult))
                        tt(state_c[:, fs], state[:, fs], over(cen[:, 0, fs, 1], 2, AHD), ALU.mult).then_inc(S("state_step"), 1)
                    else:
                        tmp = words(M_AUX + AUX["w2"][0], 4, AHD)
                        tt(tmp, src, fresh, ALU.mult)
                        link(tt(state[:, fs], state[:, fs], over(cen[:, 2, fs, c], 2, AHD), ALU.mult))
                        tt(state[:, fs], state[:, fs], tmp, ALU.add).then_inc(S("state_step"), 1)
                else:
                    dve.wait_ge(S("sa_copied"), it + 1)
                    for j in range(4):
                        f = f0 + j
                        if j % 2 == 0:
                            if f:
                                dve.wait_ge(S("wkv_sum"), f)
                            hs = slice(2 * j, 2 * j + 4)
                            for q, src in enumerate((SA_s, tok_s[:, 2, :])):
                                src = src.rearrange("p (h i) -> p h i", h=HG)[:, hs]
                                ins = tt(sam[:, q], over(src, 2, NB), over(over(cst1("seq", rows=SM), 1, 4), 3, AHD), ALU.mult)
                            ins.then_inc(S("sam_ready"), 1)
                        dve.wait_ge(S("wkv_sum"), f + 1)
                        bank = 3 if j % 2 else 1
                        s_f = wkv_s[:, f]
                        link(tt(s_f, s_f, ps[bank][:, :].rearrange("p (b i) -> p b i", b=NB), ALU.add))
                        tt(s_f, s_f, over(cen_s[:, f, :], 2, AHD), ALU.mult).then_inc(S("wkv_new"), 1)

            for f in range(MT):
                dve.wait_ge(S("mean_sum"), f + 1)
                stt(out=ymix[:, f, :], in0=ps[f % 4][:, 0:N], scalar=-1.0 / AHD, in1=ymix[:, f, :], op0=ALU.mult,
                    op1=ALU.add).then_inc(S("centred"), 1)
            for f in range(MT):
                y = ymix[:, f, :]
                dve.wait_ge(S("var_root"), f + 1)
                link(dve.reciprocal(hrt[:, f % 2, :], hrt[:, f % 2, :]))
                link(tt(y, y, hrt[:, f % 2, :], ALU.mult))
                link(ts(y, y, prm("lnw", f), prm("lnb", f), ALU.mult, ALU.add))
                link(tt(y, y, bonus[:, f, :], ALU.add))
                dve.wait_ge(S("gate_sum"), f + 1)
                tt(y, ps[2 + f % 2][:, 0:N], y, ALU.mult).then_inc(S("gated"), 1)

            def gated_add(src, dst, gate, gate_s, tmp):
                link(tt(tmp.rearrange("p (b t) -> p b t", t=TS), src[:, TP:N].rearrange("p (b t) -> p b t", t=TS),
                        over(gate_s, 2, TS), ALU.mult))
                stt(out=dst[:, 0:TP], in0=src[:, 0:TP], scalar=gate, in1=dst[:, 0:TP], op0=ALU.mult, op1=ALU.add)
                return tt(dst[:, TP:N], dst[:, TP:N], tmp, ALU.add)

            dve.wait_ge(S("mods_raw"), 8)
            add_bias(2, 6)
            dve.wait_ge(S("x_again"), 16)
            base = chain.n
            with dve.Fori(0, KT // 4) as i:
                chain.n = i * 4 + base
                for j in range(4):
                    dve.wait_ge(used, i * 4 + (n_wo + j + 1))
                    dve.wait_ge(S("out_free"), i * 4 + (j + 2))
                    def at(a):
                        return a[:, bass.ds(i * 4 + j, 1)].rearrange("p o n -> p (o n)")
                    ga = at(mods[:, G_A])
                    gated_add(ps[j % 2], at(x1), ga[:, 0:1], ga[:, 1:NS], xt_s).then_inc(S("out_free"), 1)
            chain.n = base + KT
            dve.wait_ge(S("out_free"), KT + 2)
            norm(x1, h2, rms2, gain2, SH_C, SC_C, "gffn", 2, S("h_ready"))

            iota16 = iota[:, 0:TOPK]
            for b in range(3):
                w = P if b < 2 else SM
                R = slice(0, w)
                dve.wait_ge(S("score_copied"), b + 1)
                if b:
                    dve.wait_ge(S("picks_ready"), b)
                def best16(src, rest, out, index, groups):
                    for g in range(groups):
                        ins = dve.max(out[R, g, 0:8], src[R, g])
                    link(ins)
                    for g in range(groups):
                        dve.max_index(index[R, g, 0:8], out[R, g, 0:8], src[R, g])
                        ins = dve.match_replace(rest[R, g], out[R, g, 0:8], src[R, g], NEG)
                    link(ins)
                    for g in range(groups):
                        ins = dve.max(out[R, g, 8:16], rest[R, g])
                    link(ins)
                    for g in range(groups):
                        ins = dve.max_index(index[R, g, 8:16], out[R, g, 8:16], rest[R, g])
                    link(ins)
                best16(sc, sc2, top, topi.bitcast(U32), GR)
                link(dve.tensor_copy(topf[R], topi.bitcast(U32)[R]))
                t4 = top.rearrange("p (h q) k -> p h q k", q=2)
                link(tt(cand[R].rearrange("p h (a c) -> p h a c", a=TOPK), over(t4[R, :, 0], 3, TOPK),
                        over(t4[R, :, 1], 2, TOPK), ALU.add))
                best16(cand, cand2, best, posi.bitcast(U32), PH)
                pu = part.bitcast(U32)
                dve.tensor_scalar(pu[R, 0], posi.bitcast(U32)[R], 4, None, ALU.logical_shift_right)
                link(dve.tensor_scalar(pu[R, 1], posi.bitcast(U32)[R], TOPK - 1, None, ALU.bitwise_and))
                link(dve.tensor_copy(partf[R], pu[R]))
                link(dve.tensor_copy(psum8[R, 1], best[R, :, 0]))
                tt(best[R], best[R], over(psum8[R, 1], 2, TOPK), ALU.subtract).then_inc(S("gate_arg"), 1)
                if b:
                    dve.wait_ge(S("picks_turned"), b)
                f4 = topf.rearrange("p (h q) k -> p h q k", q=2)
                for q in range(2):
                    at = partf[R, q].rearrange("p h s -> p (h s)")
                    link(tt(eq[R], over(at, 2, TOPK), over(iota16[R], 1, PH * TOPK), ALU.is_equal))
                    e4 = eq[R].rearrange("p (h s) a -> p h s a", h=PH)
                    link(tt(e4, e4, over(f4[R, :, q], 2, TOPK), ALU.mult))
                    link(dve.tensor_reduce(pick[R, q], eq[R], AX.X, ALU.add))
                dve.wait_ge(S("gate_exp"), b + 1)
                link(dve.tensor_reduce(psum8[R, 0], best[R], AX.X, ALU.add))
                link(dve.reciprocal(psum8[R, 1], psum8[R, 0]))
                tt(pick[R, 2].rearrange("p (h s) -> p h s", h=PH), best[R], over(psum8[R, 1], 2, TOPK),
                   ALU.mult).then_inc(S("picks_ready"), 1)

            dve.wait_ge(S("picks_copied"), 3)
            with dve.Fori(0, N // 4) as i:
                for s in range(2):
                    dve.wait_ge(S("g_free"), i * 2 + (s + 1))
                    for e in range(2):
                        def at(q):
                            return pickT[:, q, bass.ds(i * 4 + (2 * s + e), 1)]
                        ts(hot1[:, s, e, :], iota, at(0), at(2), ALU.is_equal, ALU.mult)
                        ins = ts(hot2[:, s, e, :], iota, at(1), None, ALU.is_equal)
                    ins.then_inc(S("hot_ready"), 1)
            dve.wait_ge(S("g_free"), N // 2 + 2)
            with dve.Fori(0, NK // 4) as i:
                for j in range(4):
                    dve.wait_ge(S("gelu_done"), i * 4 + (4 + j + 1))
                    g_row = G[:, bass.ds(i * 4 + j, 1), :].rearrange("p o n -> p (o n)")
                    tt(g_row, g_row, gel[:, j % 2, :], ALU.mult).then_inc(S("acts_ready"), 1)

            dve.wait_ge(S("x1_back"), 16)
            for half in range(2):
                dve.wait_ge(used, n_v + (half + 1) * NK // 2)
                for dt in range(8):
                    n = half * 8 + dt
                    if n:
                        dve.wait_ge(S("out_taken"), n)
                    gated_add(ps[dt], xo[:, n, :], mods[:, G_C, n, 0:1], mods[:, G_C, n, 1:NS], xs3).then_inc(S("out_taken"), 1)
            dve.wait_ge(S("out_taken"), KT)
            norm(xo, yn, rms3, gain3, SH_F, SC_F, "gfin", 3, S("y_done"))


OUTS = {
    "y": (P, KT, N), "shift_all": (P, AT, NS), "wkv_p": (P, MT, AHD), "wkv_s": (P, MT, NB, AHD),
    "conv_all": (P, MT, NS, 3), "c_p": (BH, P, DV), "c_s": (BH, P, NB, DV), "n_all": (P, BH, NS), "m_all": (BH, NS),
}


def tiled(w):
    c = w.shape[1] // P
    return np.ascontiguousarray(w.reshape(KT, P, c, P).transpose(2, 1, 0, 3)).reshape(c, P, D)


def by_tile(a, n=P):
    a = a.reshape(-1, a.shape[-1] // n, n)
    return a.transpose(2, 1, 0)


def kernel(x_prompt, x_sample, c_prompt, c_sample, state_rwkv_shift, state_rwkv_wkv, state_mlstm_conv,
           state_mlstm_C, state_mlstm_n, state_mlstm_m, w_ada, b_ada, norm_mix_g, w_in, a_mu, a_w0, a_w2,
           a_a0, a_a2, a_g2, a_kk, a_ka, a_rk, a_lnw, a_lnb, b_conv_w, b_conv_b, b_ig_bias, b_fg_bias,
           b_norm_g, w_out, norm_ffn_g, peer_wq, peer_keys, peer_u, peer_v, w_ada_final, b_ada_final,
           norm_final_g):
    import concourse.bacc as bacc
    from concourse.bass_utils import run_bass_kernel_spmd

    f = np.float32
    A = lambda a: np.asarray(a)
    c0, c1 = constants()
    prm = np.zeros((P, PRM_N), f)

    def vec(name, a):
        at, n = PRM[name]
        prm[:, at:at + n] = A(a).reshape(n, P).T

    for name, a in (("mu", a_mu), ("w0", a_w0), ("a0", a_a0), ("kk", a_kk), ("ka", a_ka), ("rk", a_rk), ("lnw", a_lnw),
                    ("lnb", a_lnb), ("convw", b_conv_w), ("convb", b_conv_b), ("bnorm", b_norm_g),
                    ("gmix", norm_mix_g), ("gffn", norm_ffn_g), ("gfin", norm_final_g)):
        vec(name, a)
    vec("bada", np.concatenate([A(b_ada)[0], A(b_ada_final)]))
    at = PRM["gatebias"][0]
    prm[0:BH, at] = A(b_ig_bias)[0]
    prm[32:32 + BH, at] = A(b_fg_bias)[0]
    prm[:, PRM["eps"][0]] = 1e-6
    prm[:, PRM["gneps"][0]] = AHD * 1e-5

    w_in0 = A(w_in)[0]
    w_g = np.zeros((P, KT, 36), f)
    gates = w_in0[:, 6400:6408].reshape(KT, P, 2 * BH).transpose(1, 0, 2)
    w_g[:, :, 0:BH] = gates[:, :, 0:BH]
    w_g[:, :, 32:36] = gates[:, :, BH:]
    w2, a2 = np.zeros((P, MIX), f), np.zeros((P, MIX), f)
    w2[0:64] = A(a_w2)[0]
    a2[64:128] = A(a_a2)[0]
    x = np.concatenate([A(x_prompt)[0], A(x_sample).reshape(SM, D)])
    c = np.concatenate([A(c_prompt), A(c_sample)])
    u = A(peer_u)[0].reshape(NK, NK, KT, P)
    ins = {
        "x": by_tile(x), "c": by_tile(c), "prm": prm, "cst0": c0, "cst1": c1,
        "w_ada": A(w_ada)[0], "w_adaf": A(w_ada_final), "w_in": tiled(w_in0[:, 0:6400]), "w_g": w_g.reshape(P, -1),
        "w_out": tiled(A(w_out)[0]), "w_q": tiled(A(peer_wq)[0]),
        "peer_u": np.ascontiguousarray(u.transpose(1, 3, 2, 0)).reshape(NK, P, D), "peer_v": A(peer_v)[0],
        "keys": A(peer_keys)[0].transpose(3, 0, 1, 2).reshape(P, 2 * PH, NK),
        "w2": w2, "a2": a2, "g2": A(a_g2)[0],
        "shift0": by_tile(A(state_rwkv_shift)[0]).reshape(P, -1),
        "conv0": A(state_mlstm_conv)[0].reshape(NB, 3, MT, P).transpose(3, 2, 0, 1).reshape(P, -1),
        "wkv0": A(state_rwkv_wkv)[0].reshape(NB, MT, 2, AHD, AHD).transpose(2, 4, 1, 0, 3).reshape(P, MT, NB, AHD),
        "c0": A(state_mlstm_C)[0].transpose(1, 2, 0, 3),
        "n0": A(state_mlstm_n)[0].transpose(2, 1, 0).reshape(P, -1),
        "m0": A(state_mlstm_m)[0].T,
    }
    nc = bacc.Bacc("TRN2", target_bir_lowering=False, num_devices=1)
    arrays, T = {}, {}
    for name, a in ins.items():
        arrays[f"in_{name}"] = np.ascontiguousarray(a)
        T[name] = nc.dram_tensor(f"in_{name}", a.shape, F32, kind="ExternalInput").ap()
    for name, shape in OUTS.items():
        T[name] = nc.dram_tensor(f"out_{name}", shape, F32, kind="ExternalOutput").ap()
    build(nc, T)
    res = run_bass_kernel_spmd(nc, [arrays], core_ids=[0]).results[0]
    o = {name: res[f"out_{name}"] for name in OUTS}

    y = o["y"].transpose(2, 1, 0).reshape(N, D)
    shift = o["shift_all"].transpose(2, 1, 0).reshape(NS, SHIFT)
    conv = o["conv_all"].transpose(2, 3, 1, 0).reshape(NS, 3, MIX)
    n_all = o["n_all"].transpose(2, 1, 0)
    wkv_p = o["wkv_p"].reshape(2, AHD, MT, AHD).transpose(2, 0, 3, 1).reshape(1, 1, AH, AHD, AHD)
    wkv_s = o["wkv_s"].reshape(2, AHD, MT, NB, AHD).transpose(3, 2, 0, 4, 1).reshape(1, NB, AH, AHD, AHD)
    out = (y[:TP].reshape(1, TP, D), y[TP:].reshape(NB, TS, D),
           shift[None, 0:1], wkv_p, conv[None, 0:1], o["c_p"][None, None], n_all[None, 0:1], o["m_all"].T[None, 0:1],
           shift[None, 1:], wkv_s, conv[None, 1:], o["c_s"].transpose(2, 0, 1, 3)[None], n_all[None, 1:],
           o["m_all"].T[None, 1:])
    return tuple(np.ascontiguousarray(a) for a in out)
```

```python
import math
from contextlib import ExitStack

import numpy as np

import concourse.bass as bass
from concourse import mybir

F32 = mybir.dt.float32
F32R = mybir.dt.float32r
U32 = mybir.dt.uint32
ALU = mybir.AluOpType
ACT = mybir.ActivationFunctionType
AX = mybir.AxisListType

P = 128
D = 2048
KT = D // P
TP, NB, TS = 256, 8, 4
SM = NB * TS
N = TP + SM
NS = NB + 1
MIX = D // 2
MT = MIX // P
AH, AHD = 16, 64
SHIFT = 3 * MIX + 256
AT = SHIFT // P
BH, DQK, DV = 4, 128, 256
CONV = 4
L = 128
CH = TP // L
HG = 8
PH, NK, TOPK = 8, 128, 16
NEG = -3.0e38

def columns(sizes):
    at, out = 0, {}
    for name, n in sizes:
        out[name] = (at, n)
        at += n
    return out, at


CST0, CST0_N = columns([("ident", P), ("ones", P), ("iota", P)])
LEVELS = 7
CST1, CST1_N = columns([
    ("blk", P), ("level", LEVELS * P), ("strict", P), ("incl", P), ("slevel", 2 * SM), ("sstrict", SM), ("sincl", SM),
    ("seq", NB), ("wreset", N), ("breset", N), ("mreset", N), ("sel", BH * P), ("fold", 16), ("seqcol", NB * SM)])
PRM, PRM_N = columns([
    ("mu", AT), ("w0", MT), ("a0", MT), ("kk", MT), ("ka", MT), ("rk", MT), ("lnw", MT), ("lnb", MT),
    ("convw", CONV * MT), ("convb", MT), ("bnorm", MT), ("gmix", KT), ("gffn", KT), ("gfin", KT),
    ("bada", 8 * KT), ("gatebias", 1), ("eps", 1), ("gneps", 1), ("zero", 1)])

ARENA = 53208
RING_SLOTS = 4
M_CST0 = 0
M_MODS = M_CST0 + CST0_N
M_PRM = M_MODS + 8 * KT * NS
M_RING = (M_PRM + PRM_N + 7) // 8 * 8
M_BASE = M_RING + RING_SLOTS * D
M_CST1 = M_BASE
M_SILC = M_CST1 + (CST1_N + 7) // 8 * 8
AUX, AUX_N = columns([("n0", NB * BH), ("m0", NB), ("conv", MT * NB * 3), ("shift", AT * NB), ("wg", KT * 36),
                      ("w2", MIX), ("a2", MIX), ("g2", MIX)])
M_AUX = M_SILC + KT * 32
M_ADAS = M_AUX + (AUX_N + 7) // 8 * 8
M_YMIX = M_ADAS + D
M_H = M_YMIX + KT * N
M_Q = M_H + KT * N
QUARTER = NK // 4
M_HI2 = M_BASE
M_H2 = M_HI2 + 2 * D
M_H2HI = M_H2 + KT * N
M_ACTS = M_H2HI + KT * N
M_VACT = M_ACTS + 2 * QUARTER * N
M_PICKT = M_VACT + 8 * N
M_X1 = 45200
M_HOT = M_X1 + KT * N
GATE_TOKENS = N // QUARTER
HOT_TOKENS = GATE_TOKENS // 3
CHUNK = N // 8
M_SMALL = M_HOT
M_TMP = M_HOT + 3 * HOT_TOKENS * 2 * NK
assert M_PICKT + 3 * N <= M_X1 and M_SMALL + 1200 <= M_TMP and M_TMP + SM <= ARENA
assert 2 * GATE_TOKENS * NK <= 8 * N and 2 * CHUNK * QUARTER <= M_TMP - M_HOT


def constants():
    c0 = np.zeros((P, CST0_N), np.float32)
    c1 = np.zeros((P, CST1_N), np.float32)

    def put(c, cols, name, a):
        at, n = cols[name]
        c[:a.shape[0], at:at + n] = a.reshape(a.shape[0], n)

    i = np.arange(P)
    put(c0, CST0, "ident", np.eye(P))
    put(c0, CST0, "ones", np.ones((P, P)))
    put(c0, CST0, "iota", np.broadcast_to(i, (P, P)))
    s, t = i[:, None], i[None, :]
    put(c1, CST1, "blk", (s // AHD == t // AHD))
    lev = [(s >> (l + 1) == t >> (l + 1)) & (s >> l != t >> l) & (s < t) for l in range(LEVELS)]
    put(c1, CST1, "level", np.stack(lev, 1))
    put(c1, CST1, "strict", s < t)
    put(c1, CST1, "incl", s <= t)
    put(c1, CST1, "slevel", np.stack([m[:SM, :SM] for m in lev[:2]], 1))
    same = (s // TS == t // TS)[:SM, :SM]
    put(c1, CST1, "sstrict", same & (s < t)[:SM, :SM])
    put(c1, CST1, "sincl", same & (s <= t)[:SM, :SM])
    put(c1, CST1, "seq", (i[:SM, None] // TS == np.arange(NB)[None, :]))
    n = np.arange(N)
    starts = ((n >= TP) & ((n - TP) % TS == 0)) | (n == 0)
    put(c1, CST1, "wreset", np.broadcast_to(~(starts | ((n < TP) & (n % L == 0))), (P, N)))
    put(c1, CST1, "breset", np.broadcast_to(~starts, (P, N)))
    put(c1, CST1, "mreset", np.broadcast_to(np.where(starts, NEG, 0.0), (P, N)))
    put(c1, CST1, "sel", np.repeat(np.eye(BH), P, axis=1))
    fold = np.zeros((P, 16))
    for r in range(NS):
        fold[r::32, r] = 1.0
    put(c1, CST1, "fold", fold)
    put(c1, CST1, "seqcol", np.broadcast_to(np.repeat(np.eye(NB), TS, axis=1), (P, NB, SM)))
    return c0, c1


class Chain:

    def __init__(self, eng, sem):
        self.eng, self.sem, self.n = eng, sem, 0

    def link(self, ins):
        self.n = self.n + 1
        ins.then_inc(self.sem, 1)
        self.eng.wait_ge(self.sem, self.n)


def build(nc, T):
    ctx = ExitStack()
    with ctx:
        kept = ctx.enter_context(nc.sbuf_tensor("kept", [P, M_BASE], F32))
        staged = ctx.enter_context(nc.sbuf_tensor("staged", [P, ARENA - M_BASE], F32))
        ps = [ctx.enter_context(nc.psum_tensor(f"bank{i}", [P, 512], F32)) for i in range(8)]

        sems = {}

        def S(name):
            if name not in sems:
                sems[name] = ctx.enter_context(nc.semaphore(name))
            return sems[name]

        def words(at, *dims, rows=P, first=0):
            mem, at = (kept, at) if at < M_BASE else (staged, at - M_BASE)
            v = mem[first:first + rows, at:at + math.prod(dims)]
            if len(dims) > 1:
                names = "abcd"[:len(dims)]
                v = v.rearrange(f"p ({' '.join(names)}) -> p {' '.join(names)}", **dict(zip(names[1:], dims[1:])))
            return v

        def cst0(name, rows=P):
            return words(M_CST0 + CST0[name][0], CST0[name][1], rows=rows)

        def cst1(name, *dims, rows=P):
            return words(M_CST1 + CST1[name][0], *(dims or (CST1[name][1],)), rows=rows)

        def prm(name, i=None, n=1, rows=P, first=0):
            at, size = PRM[name]
            return words(M_PRM + at + (i or 0), n if i is not None else size, rows=rows, first=first)

        def aux(name, *dims, rows=P):
            return words(M_AUX + AUX[name][0], *(dims or (AUX[name][1],)), rows=rows)

        def over(v, axis, n):
            v = v.unsqueeze(axis)
            return v.broadcast_to([n if i == axis else d for i, d in enumerate(v.shape)])

        ident, ones, iota = cst0("ident"), cst0("ones"), cst0("iota")
        blk = cst1("blk")
        mods = words(M_MODS, 8, KT, NS)
        SH_A, SC_A, G_A, SH_C, SC_C, G_C, SH_F, SC_F = range(8)
        ring = [words(M_RING + i * D, D) for i in range(RING_SLOTS)]
        silc = words(M_SILC, KT, 32)
        adas = words(M_ADAS, D)
        ymix = words(M_YMIX, KT, N)
        hT = words(M_H, KT, N)

        xT = words(M_Q, KT, N)
        xsq = words(M_Q + KT * N, KT, N)
        rms = words(M_Q + 2 * KT * N, 2, N)
        gain = words(M_Q + 2 * KT * N + 2 * N, KT, NS)

        craw = words(M_Q + 2 * KT * N + 2 * N + KT * NS, KT, NS)
        csig = words(M_Q + 2 * KT * N + 2 * N + 2 * KT * NS, KT, NS)

        q0 = M_Q
        ZQW = TP + 3 + NB * 7
        ZQS = ZQW + 5
        zq = words(q0, 2, ZQS)
        conv = words(q0 + 2 * ZQS, 2, ZQS)
        q1 = q0 + 4 * ZQS
        qk = words(q1, MT, N)
        bv = words(q1 + MT * N, MT, N)
        q2 = q1 + 2 * MT * N
        ROWS = ["i", "f", "t", "b", "g", "g2", "mx", "m", "em", "ws", "wi"]
        row = {n: words(q2 + j * N, N, rows=BH) for j, n in enumerate(ROWS)}
        q3 = q2 + len(ROWS) * N
        cvo = words(q3, MT, NS, 3)
        sho = words(q3 + MT * NS * 3, AT, NS)
        mo = words(q3 + MT * NS * 3 + AT * NS, NS, rows=BH)
        q4 = q3 + MT * NS * 3 + AT * NS + NS
        ZXW = TP + 1 + NB * 5
        zx = words(q4, 2, ZXW + 1)
        zd = words(q4 + 2 * (ZXW + 1), 2, ZXW + 1)
        q5 = M_Q + (q4 + 4 * (ZXW + 1) - M_Q + 7) // 8 * 8
        bc = words(q5, 2, BH, N)
        wib = words(q5 + 2 * BH * N, BH, SM)
        colg = words(q5 + 2 * BH * N + BH * SM, 3, 2, BH)
        q6 = q5 + 2 * BH * N + BH * SM + 24
        ktok = words(q6, 2, BH, P)
        ktok_s = words(q6 + 2 * BH * P, BH, P, rows=SM)
        q7 = q6 + 3 * BH * P
        vtok = words(q7, 2, BH, DV + 1)
        vtok_s = words(q7 + 2 * BH * (DV + 1), BH, DV + 1, rows=SM)
        q8 = q7 + 3 * BH * (DV + 1)
        DW = TP + P + SM
        dd = words(q0, 2, DW)
        qw = words(q0 + 2 * DW, 2, SM)
        assert 2 * DW + 2 * SM <= 4 * ZQS
        kwm = words(q4, NB, P, rows=SM)
        assert NB * P <= 4 * (ZXW + 1)
        hsq = words(q2, 2, N)
        hh = words(M_AUX + AUX["wg"][0], 2, N)
        c_out = words(M_H + 2 * NB * DV, 2, DV)
        rec = words(q8, 2, N)
        n_out = words(q8 + 2 * N, BH, NS)
        q10 = q8 + 2 * N + BH * NS
        cring = words(M_H, 2, NB, DV)
        za = ARENA - (2 * MT + 2) * N
        assert q10 <= za, (q10, za)
        r = words(M_YMIX, MT, N)
        k = words(za, MT, N)
        v = words(za + MT * N, MT, N)
        low = words(za + 2 * MT * N, 2, N)
        arz = words(M_Q, AH, 2, TP)
        arz_s = words(M_Q + AH * 2 * TP, AH, 2, SM)
        m1 = M_Q + AH * 2 * N
        B = words(m1, MT, N)
        kk = words(m1 + MT * N, MT, N)
        bonus = words(m1 + 2 * MT * N, MT, N)
        lg = words(M_H, MT, N)
        t1 = words(M_H + MT * N, MT, N)
        flat = MT * N
        lgf, t1f, Bf, kkf, bonusf = (words(a, flat) for a in (M_H, M_H + flat, m1, m1 + flat, m1 + 2 * flat))
        rf, kf, vf = words(M_YMIX, flat), words(za, flat), words(za + flat, flat)
        m2 = m1 + 3 * flat
        cen = words(m2, 3, MT, CH)
        cen_s = words(m2 + 3 * MT * CH, MT, NB)
        m3 = m2 + 3 * MT * CH + MT * NB
        state = words(m3, MT, AHD)
        state_c = words(m3 + MT * AHD, MT, AHD)
        HW = HG * AHD
        tok = words(m3 + 2 * MT * AHD, 3, HW)
        tok_s = words(m3 + 2 * MT * AHD, 3, HW, rows=SM)
        assert m3 + 2 * MT * AHD + 3 * HW <= za
        gram = words(M_H, HG, 4, L)
        Ti = words(m1 + flat, HG, L)
        Tt = words(m1 + flat + HG * L, HG, L)
        X = words(M_AUX + AUX["w2"][0], HG, L)
        masked = words(M_AUX + AUX["a2"][0], HG, L)
        W = words(M_AUX + AUX["a2"][0], HW)
        SA = words(M_AUX + AUX["a2"][0] + HW, HW)
        tn = words(M_AUX + AUX["wg"][0], 2, N)
        hrt = words(M_H, 2, N)
        gram_s = words(M_H, HG, 4, SM, rows=SM)
        azm = words(M_H + HG * 4 * SM, HG, NB, SM)
        Ti_s = words(m1 + flat, HG, SM, rows=SM)
        Tt_s = words(m1 + flat + HG * L, HG, SM, rows=SM)
        X_s = words(M_AUX + AUX["w2"][0], HG, SM, rows=SM)
        masked_s = words(M_AUX + AUX["a2"][0], HG, SM, rows=SM)
        W_s = words(M_AUX + AUX["a2"][0], HW, rows=SM)
        SA_s = words(M_AUX + AUX["a2"][0] + HW, HW, rows=SM)
        wkv_s = words(M_Q, MT, NB, AHD)
        sam = words(M_Q + MT * NB * AHD, 2, 4, NB, AHD, rows=SM)

        h2 = words(M_H2, KT, N)
        x1 = words(M_X1, KT, N)
        keys = words(30100, KT, NK)
        qT = words(M_ACTS, KT, N)
        assert M_ACTS + KT * N <= 30100 and 30100 + KT * NK <= M_ACTS + QUARTER * N
        m4 = M_ACTS + QUARTER * N
        x1sq = words(m4, KT, N)
        rms2 = words(m4 + KT * N, 2, N)
        gain2 = words(m4 + KT * N + 2 * N, KT, NS)
        xt_s = words(m4 + KT * N + 2 * N + KT * NS, SM)
        m_yhi = (m4 + KT * N + 2 * N + KT * NS + SM + 7) // 8 * 8
        assert m_yhi + KT * N <= m1 + 2 * flat
        GR = 2 * PH
        sc = words(m4, 3, GR, NK)
        rest = words(m4 + 3 * GR * NK, GR, NK)
        eq = words(m4 + 3 * GR * NK, PH * TOPK, TOPK)
        assert 4 * GR * NK <= QUARTER * N
        top = words(M_SMALL, GR, TOPK)
        topi = words(M_SMALL + 256, GR, TOPK)
        topf = words(M_SMALL + 512, GR, TOPK)
        posi = words(M_SMALL + 768, PH, TOPK)
        part = words(M_SMALL + 256, 2, PH, TOPK)
        partf = words(M_SMALL, 2, PH, TOPK)
        psum8 = words(M_SMALL + 896, 3, 2, PH)
        pick = words(M_VACT, 3, 3, PH * TOPK)
        best = words(M_VACT + 9 * PH * TOPK, 3, PH, TOPK)
        pickT = words(M_PICKT, 3, N)
        hot1 = words(M_HOT, 3, HOT_TOKENS, NK)
        hot2 = words(M_HOT + 3 * HOT_TOKENS * NK, 3, HOT_TOKENS, NK)
        stage = [words(M_VACT + b * GATE_TOKENS * NK, 4, GATE_TOKENS, QUARTER) for b in range(2)]
        gates_in = [words(M_HOT + b * CHUNK * QUARTER, CHUNK * QUARTER) for b in range(2)]
        gates_dram = nc.dram_tensor("gates_spill", (3, P, N * QUARTER), F32, kind="Internal").ap()
        acts = [words(M_ACTS + b * QUARTER * N, QUARTER, N) for b in range(2)]
        xo = x1
        ysq = words(M_ACTS, KT, N)
        yn = words(M_ACTS + KT * N, KT, N)
        rms3 = words(M_ACTS + 2 * KT * N, 2, N)
        gain3 = words(M_ACTS + 2 * KT * N + 2 * N, KT, NS)
        xs3 = words(M_TMP, SM)

        base = nc.lookup_mloc(kept).addr
        assert nc.lookup_mloc(staged).addr == base + 4 * M_BASE

        def parts(name, at, *dims):
            t = nc.alloc_sbuf_tensor_at(name, [P, math.prod(dims)], F32R, offset=base + 4 * at)[:, :]
            if len(dims) > 1:
                names = "abcd"[:len(dims)]
                t = t.rearrange(f"p ({' '.join(names)}) -> p {' '.join(names)}", **dict(zip(names[1:], dims[1:])))
            return t

        ring_lo = parts("ring_lo", M_RING, RING_SLOTS, D)
        hi_front = [parts("hi_front0", M_ADAS, D), parts("hi_front1", q5, D)]
        hi_peer = parts("hi_peer", M_HI2, 2, D)
        h_hi, h_lo = parts("h_hi", q5 + D, KT, N), parts("h_lo", M_H, KT, N)
        assert q5 + D + KT * N <= za
        y_hi, y_lo = parts("y_hi", m_yhi, KT, N), parts("y_lo", M_YMIX, KT, N)
        h2_hi, h2_lo = parts("h2_hi", M_H2HI, KT, N), parts("h2_lo", M_H2, KT, N)
        act_hi, act_lo = parts("act_hi", M_VACT, 2, 2, N), parts("act_lo", M_VACT + 4 * N, 2, 2, N)

        def samp(v):
            names = " ".join("xyz"[:len(v.shape) - 2])
            return v[..., TP:N].rearrange(f"p {names} (b t) -> p {names} b t", t=TS)

        ADA_TILES, Z_TILES = KT, 2 * AT - 2
        n_ada0 = 0
        n_z = n_ada0 + 2 * ADA_TILES
        n_ada1 = n_z + 50
        n_wo = n_ada1 + 6 * ADA_TILES
        n_q = n_wo + KT
        n_p = n_q + KT
        SEG = QUARTER
        segments = [("u", 0), ("u", 1), ("v", 0), ("u", 2), ("v", 1), ("u", 3), ("v", 2), ("v", 3)]
        n_end = n_p + len(segments) * SEG
        landed = [S(f"slot{i}_landed") for i in range(RING_SLOTS)]
        used = S("weights_used")

        def arrived(eng, n, i=0):
            eng.wait_ge(landed[n % RING_SLOTS], (i + (n // RING_SLOTS + 1)) * 16)

        def dense_index(n):
            return n - n_z if n < n_ada1 else n - n_wo + 50

        def acts_split_n(n):
            s = (n - n_p) // SEG
            return SEG * sum(what == "v" for what, _ in segments[:s]) + (n - n_p) % SEG

        def hi_slot(n):
            return hi_front[n % 2] if n < n_ada1 else hi_peer[:, n % 2]

        ada_order = [SH_A, SC_A, G_A, SH_C, SC_C, G_C, SH_F, SC_F]

        block = ctx.enter_context(nc.Block())

        @block.sync
        def _(sp):
            def load(n, src, i=0, wait=True):
                if wait:
                    sp.wait_ge(used, i * RING_SLOTS + (n - RING_SLOTS + 1))
                sp.dma_start(ring[n % RING_SLOTS], src).then_inc(landed[n % RING_SLOTS], 16)

            def ada(j):
                part = ada_order[j]
                w, at = (T["w_ada"], part * D) if part < 6 else (T["w_adaf"], (part - 6) * D)
                for kt in range(KT):
                    n = (n_ada0 + j * KT if j < 2 else n_ada1 + (j - 2) * KT) + kt
                    load(n, w[kt * P:(kt + 1) * P, at:at + D], wait=n >= RING_SLOTS)

            def tiles(n, src, count, at=0):
                with sp.Fori(0, count // RING_SLOTS) as i:
                    for j in range(RING_SLOTS):
                        load(n + j, src[bass.ds(i * RING_SLOTS + (at + j), 1)].rearrange("o p c -> (o p) c"), i)

            def load_gates(q, i, slot):
                sp.wait_ge(S("gates_applied"), i * 2 + (8 * (q - 1) + slot + 1))
                at = bass.ds(i * (2 * CHUNK * QUARTER) + slot * CHUNK * QUARTER, CHUNK * QUARTER)
                sp.dma_start(gates_in[slot], gates_dram[q - 1][:, at]).then_inc(S(f"gates_in{slot}"), 16)

            for j in range(2):
                ada(j)
            tiles(n_z, T["w_in"], 24, AT)
            tiles(n_z + 24, T["w_in"], 24)
            for j in range(2):
                load(n_z + 48 + j, T["w_in"][24 + j])
            for j in range(2, 8):
                ada(j)
            tiles(n_wo, T["w_out"], KT)
            tiles(n_q, T["w_q"], KT)
            v_dram = T["peer_v"].rearrange("(a b) d -> b a d", b=NK)
            for s, (what, q) in enumerate(segments):
                n0 = n_p + s * SEG
                if s == 3:
                    for slot in range(2):
                        sp.wait_ge(S(f"gates_stored{slot}"), 16 * (SEG // 2 + 1))
                if what == "u" and q < 2:
                    tiles(n0, T["peer_u"], SEG, q * QUARTER)
                elif what == "u":
                    with sp.Fori(0, SEG // 8) as i:
                        for j in range(8):
                            load(n0 + j, T["peer_u"][bass.ds(i * 8 + (q * QUARTER + j), 1)].rearrange("o p c -> (o p) c"),
                                 i * 2)
                            if j % 4 == 3:
                                load_gates(q - 1, i, j // 4)
                else:
                    for half in range(2):
                        with sp.Fori(0, SEG // 16) as i:
                            for j in range(8):
                                n = n0 + half * SEG // 2 + j
                                src = v_dram[bass.ds(i * 16 + (q * QUARTER + 2 * j), 2), :,
                                             half * D // 2:(half + 1) * D // 2]
                                sp.wait_ge(used, i * 8 + (n - RING_SLOTS + 1))
                                sp.dma_start(ring[n % RING_SLOTS].rearrange("p (b d) -> p b d", b=2),
                                             src.rearrange("b a d -> a b d")).then_inc(landed[n % RING_SLOTS], 16)
                                if s == 6 and j % 4 == 3:
                                    load_gates(3, i + 2 * half, j // 4)
            for half in range(2):
                sp.wait_ge(S("y_done"), 2)
                sp.dma_start(T["y"][:, half * 8:(half + 1) * 8], yn[:, half * 8:(half + 1) * 8]).then_inc(S("y_stored"), 16)
            sp.wait_ge(S("y_stored"), 32)

        @block.gpsimd
        def _(pool):
            for name, count in (("z_free", 2), ("zq_free", 2), ("zx_free", 2), ("out_free", 2), ("q_free", 2),
                                ("hot_done", 3), ("gelu_done", 4), ("gates_copied", 3), ("gates_stored0", 16),
                                ("gates_stored1", 16), ("g_mul", 2), ("gates_applied", 2)):
                pool.sem_inc(S(name), count)
            def store_c(h):
                pool.wait_ge(S("c_new"), h + 1)
                pool.dma_start(T["c_s"][h], cring[:, h % 2]).then_inc(S(f"c_stored{h % 2}"), 16)
                pool.dma_start(T["c_p"][h], c_out[:, h % 2]).then_inc(S(f"cp_stored{h % 2}"), 16)

            def lo(n, i=0):
                for c in range(2):
                    cols = slice(c * D // 2, (c + 1) * D // 2)
                    pool.wait_ge(S("hi_ready"), i * 8 + (2 * dense_index(n) + c + 1))
                    pool.tensor_tensor(ring_lo[:, n % RING_SLOTS, cols], ring[n % RING_SLOTS][:, cols],
                                       hi_slot(n)[:, cols].bitcast(F32), ALU.subtract).then_inc(S("lo_ready"), 1)

            def lo_tiles(n, count):
                with pool.Fori(0, count // RING_SLOTS) as i:
                    for j in range(RING_SLOTS):
                        lo(n + j, i)

            lo_tiles(n_z, 48)
            for j in range(48, 50):
                lo(n_z + j)
            pool.wait_ge(used, n_z + 50)
            for h in range(BH):
                if h >= 2:
                    pool.wait_ge(S(f"c_stored{h % 2}"), 16)
                pool.dma_start(cring[:, h % 2], T["c0"][h]).then_inc(S(f"c_landed{h % 2}"), 16)
                if h >= 1:
                    store_c(h - 1)
            store_c(BH - 1)
            pool.wait_ge(S("c_new"), BH)
            pool.dma_start(T["n_all"], n_out).then_inc(S("small_stored"), 16)
            pool.dma_start(T["m_all"], mo).then_inc(S("small_stored"), 16)
            pool.dma_start(T["conv_all"], cvo).then_inc(S("small_stored"), 16)
            pool.dma_start(T["shift_all"], sho).then_inc(S("small_stored"), 16)
            pool.wait_ge(S("small_stored"), 64)
            for slot in range(2):
                pool.wait_ge(S(f"cp_stored{slot}"), 32)
            pool.memset(words(M_Q, AH * 2 * N), 0.0).then_inc(S("arz_clear"), 1)
            pool.wait_ge(S("state_step"), 4)
            pool.dma_start(T["wkv_p"], state).then_inc(S("wkv_stored"), 16)
            pool.dma_start(wkv_s, T["wkv0"]).then_inc(S("wkv_landed"), 16)
            pool.wait_ge(S("wkv_new"), MT)
            pool.dma_start(T["wkv_s"], wkv_s).then_inc(S("wkv_stored"), 16)
            pool.wait_ge(S("wkv_stored"), 32)
            pool.wait_ge(S("gated"), MT)
            pool.dma_start(x1, T["x"]).then_inc(S("x_again"), 16)
            pool.dma_start(keys, T["keys"]).then_inc(S("keys_landed"), 16)
            lo_tiles(n_wo, n_end - n_wo)
            for slot in range(2):
                pool.wait_ge(S(f"c_stored{slot}"), 32)

        @block.tensor
        def _(pe):
            def matmul(out, lhsT, rhs, start=True, stop=True):
                return pe.matmul(out, lhsT, rhs, start=start, stop=stop)

            def turn(out, in_):
                return pe.transpose(out, in_, ident[0:in_.shape[0], 0:in_.shape[0]])

            def norm_sum(sq, count, bank):
                pe.wait_ge(S("squares"), count)
                for kt in range(KT):
                    mm = matmul(ps[bank][:, 0:N], ones, sq[:, kt, :], kt == 0, kt == KT - 1)
                mm.then_inc(S("square_sum"), 1)

            def ada_turn(j):
                pe.wait_ge(S("ada_copied"), j + 1)
                for b in range(KT):
                    mm = matmul(ps[4][:, b * NS:(b + 1) * NS], adas[:, b * P:(b + 1) * P], cst1("fold")[:, 0:NS])
                mm.then_inc(S("ada_turned"), 1)

            def ada_quarter(j, quarter):
                if quarter == 0 and j > 0:
                    if j != 2:
                        ada_turn(j - 1)
                    pe.wait_ge(S("mods_raw"), j)
                for kt in range(4 * quarter, 4 * quarter + 4):
                    n = (n_ada0 + j * KT if j < 2 else n_ada1 + (j - 2) * KT) + kt
                    arrived(pe, n)
                    g = kt % 4
                    for b in range(4):
                        mm = matmul(ps[4 + b][32 * g:32 * g + 32, :], silc[:, kt, :],
                                    ring[n % RING_SLOTS][:, b * 512:(b + 1) * 512], kt < 4, kt >= KT - 4)
                    mm.then_inc(used, 1)

            pending = [(j, q) for j in range(2, 8) for q in range(4)]

            def ada_more(count):
                for _ in range(min(count, len(pending))):
                    ada_quarter(*pending.pop(0))

            def dense(n, hi, lo, i, bank):
                w_hi, w_lo = hi_slot(n), ring_lo[:, n % RING_SLOTS]
                for kt in range(KT):
                    if kt % 8 == 0:
                        pe.wait_ge(S("lo_ready"), i * 8 + (2 * dense_index(n) + kt // 8 + 1))
                    cols = slice(kt * P, (kt + 1) * P)
                    for e, (w, a) in enumerate(((w_hi, hi), (w_hi, lo), (w_lo, hi))):
                        mm = matmul(ps[bank][:, 0:N], w[:, cols], a[:, kt, :], kt == 0 and e == 0,
                                    kt == KT - 1 and e == 2)
                mm.then_inc(used, 1)

            def turn_picks(b):
                w = P if b < 2 else SM
                for q in range(3):
                    mm = turn(ps[4 + b][:, q * P:q * P + w], pick[0:w, b, q, :])
                mm.then_inc(S("picks_turned"), 1)

            pe.wait_ge(S("const_in"), 64)
            norm_sum(xsq, 1, 0)
            pe.wait_ge(S("cond_ready"), 1)
            for j in range(2):
                for q in range(4):
                    ada_quarter(j, q)
            ada_turn(1)

            pe.wait_ge(S("h_ready"), 1)
            pe.wait_ge(S("h_ready_act"), 1)
            pe.wait_ge(S("aux_in"), 128)
            wg = aux("wg", KT, 36)
            for kt in range(KT):
                mm = matmul(ps[2][0:36, 0:N], wg[:, kt, :], hT[:, kt, :], kt == 0, kt == KT - 1)
            mm.then_inc(S("gates_ready"), 1)
            pe.wait_ge(S("act_split"), 2)
            with pe.Fori(0, 6) as i:
                for j in range(4):
                    pe.wait_ge(S("z_free"), i * 4 + (j + 1))
                    dense(n_z + j, h_hi, h_lo, i, j % 2)
            with pe.Fori(0, 6) as i:
                for j in range(4):
                    pe.wait_ge(S("z_free"), i * 4 + (24 + j + 1))
                    dense(n_z + 24 + j, h_hi, h_lo, i, j % 2)
            for j in range(2):
                pe.wait_ge(S("z_free"), 48 + j + 1)
                dense(n_z + 48 + j, h_hi, h_lo, 0, j % 2)

            pe.wait_ge(S("row_exp"), 1)
            for u in range(2 * BH):
                q, h = u // BH, u % BH
                if u >= 2:
                    pe.wait_ge(S("bc_done"), u - 1)
                matmul(ps[2 + u % 2][:, 0:N], cst1("sel", BH, P, rows=BH)[:, h, :],
                       row["em" if q else "mx"]).then_inc(S("bc_ready"), 1)
            pe.wait_ge(S("z_free"), 52)
            for h in range(BH):
                mm = matmul(ps[0][:, h * SM:(h + 1) * SM], cst1("sel", BH, P, rows=BH)[:, h, :], row["wi"][:, 0:SM])
            for q, name in enumerate(("g", "ws")):
                for b in range(3):
                    w = P if b < 2 else SM
                    at = 4 * (2 * b + q)
                    mm = turn(ps[1][0:w, at:at + 4], row[name][:, b * P:b * P + w])
            mm.then_inc(S("cols_ready"), 1)
            pe.wait_ge(S("cols_done"), 1)
            pe.wait_ge(S("bc_done"), 2 * BH)
            fills = [("v", b, g) for b in range(3) for g in range(2)] + [("k", b, 0) for b in range(3)]
            for u, (what, b, g) in enumerate(fills):
                if u >= 4:
                    pe.wait_ge(S("turn_done"), u - 3)
                w = P if b < 2 else SM
                for j in range(4):
                    src = bv[:, 4 * g + j, b * P:b * P + w] if what == "v" else qk[:, BH + j, b * P:b * P + w]
                    mm = turn(ps[u % 4][0:w, j * P:(j + 1) * P], src)
                mm.then_inc(S("turn_ready"), 1)
            pe.wait_ge(S("turn_done"), 9)
            for h in range(BH):
                if h >= 1:
                    pe.wait_ge(S("ms_root"), h)
                matmul(ps[0][:, 0:TP], qk[:, BH + h, 0:P], qk[:, h, 0:TP])
                matmul(ps[0][:, TP:TP + P], qk[:, BH + h, P:TP], qk[:, h, P:TP])
                matmul(ps[0][0:SM, TP + P:DW], qk[:, BH + h, TP:N], qk[:, h, TP:N]).then_inc(S("qk_ready"), 1)
                ada_more(1)
                pe.wait_ge(S("s_ready"), h + 1)
                pe.wait_ge(S(f"c_landed{h % 2}"), 16 * (h // 2 + 1))
                for half in range(3):
                    def vt(b, rows=P):
                        if half == 2:
                            return ones[0:rows, :]
                        src = vtok[:, b, h] if b < 2 else vtok_s[:, h]
                        return src[:, half * P:(half + 1) * P]
                    out = ps[1 + half]
                    matmul(out[:, 0:TP], vt(0), dd[:, 1, 0:TP], True, False)
                    matmul(out[:, P:TP], vt(1), dd[:, 1, TP:TP + P], False, True)
                    mm = matmul(out[:, TP:N], vt(2, SM), dd[0:SM, 1, TP + P:DW], True, False)
                    if half < 2:
                        for b in range(NB):
                            mm = matmul(out[:, TP + b * TS:TP + (b + 1) * TS],
                                        cring[:, h % 2, b, half * P:(half + 1) * P], qw[:, 0, b * TS:(b + 1) * TS],
                                        False, b == NB - 1)
                    else:
                        mm = matmul(out[:, TP:N], ones, qw[:, 1, :], False, True)
                mm.then_inc(S("num_ready"), 1)
                ada_more(1)
                pe.wait_ge(S("hsq_ready"), h + 1)
                pe.wait_ge(S("num_used"), h + 1)
                for i in range(2):
                    mm = matmul(ps[0][:, 0:N], ones, hsq[:, i, :], i == 0, i == 1)
                mm.then_inc(S("ms_ready"), 1)
                pe.wait_ge(S("kwm_ready"), h + 1)
                for u in range(NS):
                    if u >= 3 or h > 0:
                        pe.wait_ge(S("upd_used"), h * NS + u - 2)
                    out = ps[1 + u % 3][:, 0:DV + 1]
                    if u < NB:
                        mm = matmul(out, kwm[:, u, :], vtok_s[:, h, :])
                    else:
                        matmul(out, ktok[:, 0, h, :], vtok[:, 0, h, :], True, False)
                        mm = matmul(out, ktok[:, 1, h, :], vtok[:, 1, h, :], False, True)
                    mm.then_inc(S("upd_ready"), 1)
                pe.wait_ge(S("upd_used"), (h + 1) * NS)

            pe.wait_ge(S("low_ready"), 1)
            pe.wait_ge(S("ms_root"), BH)
            for f in range(MT):
                for q, w in enumerate((aux("w2"), aux("a2"))):
                    if f >= 2:
                        pe.wait_ge(S("low_used"), 2 * (f - 2) + q + 1)
                    matmul(ps[2 * q + f % 2][:, 0:N], w[:, f * P:(f + 1) * P], low[:, 0, :]).then_inc(S("low_sum"), 1)
            ada_more(1)

            def head_sums(src, ready, made, taken):
                pe.wait_ge(S(ready), 1)
                for f in range(MT):
                    if f >= 4:
                        pe.wait_ge(S(taken), f - 3)
                    matmul(ps[f % 4][:, 0:N], blk, src[:, f, :]).then_inc(S(made), 1)

            pe.wait_ge(S("low_used"), 2 * MT)
            head_sums(bonus, "kksq_ready", "kk_sum", "kk_root")
            ada_more(1)
            pe.wait_ge(S("kk_root"), MT)
            head_sums(bonus, "rk_ready", "rk_sum", "bonus_done")
            ada_more(1)
            pe.wait_ge(S("bonus_done"), MT)
            pe.wait_ge(S("ops_ready"), 1)

            for it in range(2 * CH + 2):
                c, hg = (it // 2, it % 2)
                sample = c == CH
                w = SM if sample else L
                f0 = 4 * hg
                cols = slice(TP, N) if sample else slice(c * L, (c + 1) * L)
                if it:
                    pe.wait_ge(S("y_taken"), it)
                    pe.wait_ge(S("state_step") if it <= 4 else S("wkv_new"), min(it, 4) if it <= 4 else 4)
                tk = tok_s if sample else tok
                for q, src in enumerate((B, k, v)):
                    for j in range(4):
                        mm = turn(ps[q][0:w, j * P:(j + 1) * P], src[:, f0 + j, cols])
                    mm.then_inc(S("tok_ready"), 1)
                az = arz_s if sample else arz
                zc = slice(0, SM) if sample else cols
                if sample:
                    for q, src in enumerate((B, k)):
                        if q:
                            pe.wait_ge(S("tok_done"), it * 3 + 3)
                        for d in range(HG):
                            mm = matmul(ps[3 * (1 - q)][0:SM, d * 2 * SM:(d + 1) * 2 * SM],
                                        src[:, f0 + d // 2, cols], az[:, f0 * 2 + d, :, :])
                        mm.then_inc(S("gram_ready"), 1)
                    gram_n = 4 * 8 + 2 * hg
                    pe.wait_ge(S("gram_done"), gram_n + 2)
                else:
                    for g in range(8):
                        q, pair = g // 4, g % 4
                        if g == 1:
                            pe.wait_ge(S("tok_done"), it * 3 + 3)
                        if g >= 4:
                            pe.wait_ge(S("gram_done"), it * 8 + g - 3)
                        for d in (2 * pair, 2 * pair + 1):
                            mm = matmul(ps[(3 + g) % 4][:, (d % 2) * 2 * L:(d % 2 + 1) * 2 * L],
                                        (B, k)[q][:, f0 + d // 2, cols], az[:, f0 * 2 + d, :, cols])
                        mm.then_inc(S("gram_ready"), 1)
                    pe.wait_ge(S("gram_done"), it * 8 + 8)
                ada_more(2)
                levels = 2 if sample else LEVELS
                done = LEVELS * it if it <= 4 else LEVELS * 4 + 2 * hg
                ti, tt, x, mk = (Ti_s, Tt_s, X_s, masked_s) if sample else (Ti, Tt, X, masked)
                halves = 1 if sample else 2
                per = HG // halves
                xd = 2 * LEVELS * min(it, 4) + (2 * hg if sample else 0)
                td = 4 * LEVELS * min(it, 4) + (4 * hg if sample else 0)
                def level(i):
                    pe.wait_ge(S("masked_ready"), i + (done + 1))
                    for q in range(halves):
                        for d in range(q * per, (q + 1) * per):
                            mm = matmul(ps[q][0:w, (d % per) * w:(d % per + 1) * w], mk[:, d, :], ti[:, d, :])
                        mm.then_inc(S("x_sum"), 1)
                    for q in range(halves):
                        pe.wait_ge(S("x_copied"), i * halves + (xd + q + 1))
                        for d in range(q * per, (q + 1) * per):
                            mm = matmul(ps[2 + q][0:w, (d % per) * w:(d % per + 1) * w], tt[:, d, :], x[:, d, :])
                        mm.then_inc(S("t_sum"), 1)
                        for d in range(q * per, (q + 1) * per):
                            mm = matmul(ps[q][0:w, (d % per) * w:(d % per + 1) * w], x[:, d, :], tt[:, d, :])
                        mm.then_inc(S("t_sum"), 1)
                if sample:
                    for i in range(levels):
                        level(i)
                else:
                    with pe.Fori(0, levels) as i:
                        level(i)
                pe.wait_ge(S("t_added"), td + (4 if sample else 4 * LEVELS))
                gm = gram_s if sample else gram
                if sample:
                    pe.wait_ge(S("wkv_landed"), 16)
                    pe.wait_ge(S("azm_ready"), hg + 1)
                for d in range(HG):
                    h, f = f0 * 2 + d, f0 + d // 2
                    out = ps[0][0:w, d * AHD:(d + 1) * AHD]
                    if sample:
                        for b in range(NB):
                            matmul(out, azm[:, d, b, :], wkv_s[:, f, b, :], b == 0, False)
                    elif c:
                        matmul(out, az[:, h, 0, cols], state_c[:, f, :], True, False)
                    mm = matmul(out, gm[:, d, 2, :], tk[:, 2, d * AHD:(d + 1) * AHD], not sample and not c, True)
                mm.then_inc(S("w_sum"), 1)
                pe.wait_ge(S("w_copied"), it + 1)
                ws_, sa_ = (W_s, SA_s) if sample else (W, SA)
                for d in range(HG):
                    mm = matmul(ps[1][0:w, d * AHD:(d + 1) * AHD], tt[:, d, :], ws_[:, d * AHD:(d + 1) * AHD])
                mm.then_inc(S("sa_sum"), 1)
                ada_more(1)
                pe.wait_ge(S("sa_copied"), it + 1)
                for d in range(HG):
                    h, f, hp = f0 * 2 + d, f0 + d // 2, d % 2
                    out = ps[2][64 * hp:64 * hp + 64, (d // 2) * w:(d // 2 + 1) * w]
                    hs = slice(d * AHD, (d + 1) * AHD)
                    matmul(out, sa_[:, hs], gm[:, d, 1, :], True, False)
                    last = not sample and not c
                    mm = matmul(out, tk[:, 2, hs], gm[:, d, 3, :], False, last)
                    if sample:
                        for b in range(NB):
                            mm = matmul(out[:, b * TS:(b + 1) * TS], wkv_s[:, f, b, :],
                                        az[:, h, 1, b * TS:(b + 1) * TS], False, b == NB - 1)
                    elif c:
                        mm = matmul(out, state_c[:, f, :], az[:, h, 1, cols], False, True)
                mm.then_inc(S("y_sum"), 1)
                if not sample:
                    for d in range(HG):
                        hp = d % 2
                        hs = slice(d * AHD, (d + 1) * AHD)
                        out = ps[3][64 * hp:64 * hp + 64, (d // 2) * AHD:(d // 2 + 1) * AHD]
                        matmul(out, tk[:, 0, hs], sa_[:, hs], True, False)
                        mm = matmul(out, tk[:, 1, hs], tk[:, 2, hs], False, True)
                    mm.then_inc(S("state_sum"), 1)
                else:
                    for j in range(4):
                        f = f0 + j
                        if j % 2 == 0:
                            pe.wait_ge(S("sam_ready"), 2 * hg + j // 2 + 1)
                        bank = 3 if j % 2 else 1
                        if f >= 2:
                            pe.wait_ge(S("wkv_new"), f - 1)
                        for hp in range(2):
                            d = 2 * j + hp
                            hs = slice(d * AHD, (d + 1) * AHD)
                            out = ps[bank][64 * hp:64 * hp + 64, :]
                            e = d % 4
                            matmul(out, tk[:, 0, hs], sam[:, 0, e].rearrange("p b i -> p (b i)"), True, False)
                            mm = matmul(out, tk[:, 1, hs], sam[:, 1, e].rearrange("p b i -> p (b i)"), False, True)
                        mm.then_inc(S("wkv_sum"), 1)
            pe.wait_ge(S("wkv_new"), MT)
            pe.wait_ge(S("y_taken"), 2 * CH + 2)

            for f in range(MT):
                if f >= 4:
                    pe.wait_ge(S("centred"), f - 3)
                matmul(ps[f % 4][:, 0:N], blk, ymix[:, f, :]).then_inc(S("mean_sum"), 1)
            pe.wait_ge(S("centred"), MT)
            for f in range(MT):
                pe.wait_ge(S("ysq_ready"), f + 1)
                if f >= 2:
                    pe.wait_ge(S("var_root"), f - 1)
                    pe.wait_ge(S("gated"), f - 1)
                matmul(ps[f % 2][:, 0:N], blk, tn[:, f % 2, :]).then_inc(S("var_sum"), 1)
                matmul(ps[2 + f % 2][:, 0:N], aux("g2")[:, f * P:(f + 1) * P], low[:, 1, :]).then_inc(S("gate_sum"), 1)
            ada_more(len(pending))
            ada_turn(7)

            pe.wait_ge(S("gated"), MT)
            pe.wait_ge(S("var_root"), MT)
            pe.wait_ge(S("act_split"), 4)
            with pe.Fori(0, KT // 4) as i:
                for j in range(4):
                    pe.wait_ge(S("out_free"), i * 4 + (j + 1))
                    dense(n_wo + j, y_hi, y_lo, i, j % 2)
            norm_sum(x1sq, 2, 2)
            pe.wait_ge(S("act_split"), 6)
            pe.wait_ge(S("out_free"), KT + 2)
            with pe.Fori(0, KT // 4) as i:
                for j in range(4):
                    pe.wait_ge(S("q_free"), i * 4 + (j + 1))
                    dense(n_q + j, h2_hi, h2_lo, i, j % 2)
            pe.wait_ge(S("q_free"), KT + 2)
            pe.wait_ge(S("keys_landed"), 16)

            for b in range(3):
                w = P if b < 2 else SM
                if b == 2:
                    pe.wait_ge(S("score_copied"), 1)
                for g in range(GR):
                    key = (g % 2) * PH + g // 2
                    mm = matmul(ps[4 * (b % 2) + g // 4][0:w, (g % 4) * NK:(g % 4 + 1) * NK], qT[:, g, b * P:b * P + w],
                                keys[:, key, :])
                mm.then_inc(S("scores"), 1)
            pe.wait_ge(S("score_copied"), 3)

            def make_gates(i, j):
                for e in range(3):
                    pe.wait_ge(S("gates_copied"), i * 12 + (3 * j + e + 1))
                    pe.wait_ge(S("hot_ready"), i * 12 + (3 * j + e + 1))
                    for t in range(HOT_TOKENS):
                        mm = matmul(ps[4 + e][:, t * NK:(t + 1) * NK], hot1[:, e, t, :], hot2[:, e, t, :])
                    mm.then_inc(S("hot_done"), 1)

            def u_segment(s, q):
                n0 = n_p + s * SEG
                with pe.Fori(0, SEG // 4) as i:
                    for j in range(4):
                        pe.wait_ge(S("gelu_done"), i * 4 + (q * SEG + j + 1))
                        dense(n0 + j, h2_hi, h2_lo, i, j)
                        if q == 1:
                            make_gates(i, j)

            def v_tile(n, i, first, last, taken):
                w_hi, w_lo, slot = hi_slot(n), ring_lo[:, n % RING_SLOTS], n % 2
                turns = [(dt, e) for dt in range(8) for e in range(2)] if first or last else \
                    [(dt, e) for e in range(2) for dt in range(8)]
                pe.wait_ge(S("lo_ready"), i * 8 + (2 * dense_index(n) + 2))
                pe.wait_ge(S("acts_split"), i * 4 + acts_split_n(n) + 1)
                for dt, e in turns:
                    if first and e == 0 and taken is not None:
                        pe.wait_ge(S("out_taken"), taken + (dt + 1))
                    cols = slice((e * 8 + dt) * P, (e * 8 + dt + 1) * P)
                    for x, (w, a) in enumerate(((w_hi, act_hi), (w_hi, act_lo), (w_lo, act_hi))):
                        mm = matmul(ps[dt][:, 0:N], w[:, cols], a[:, slot, e, :], first and e == 0 and x == 0,
                                    last and e == 1 and x == 2)
                    if last and e == 1 and dt < 7:
                        mm.then_inc(S("v_sum"), 1)
                mm.then_inc(used, 1)

            def v_segment(s, q):
                n0 = n_p + s * SEG
                for half in range(2):
                    n = n0 + half * SEG // 2
                    before = 16 * q + 8 * half - 8
                    for j in range(4):
                        v_tile(n + j, 0, j == 0, False, before if before >= 0 else None)
                    with pe.Fori(1, 3) as i:
                        for j in range(4):
                            v_tile(n + j, i, False, False, None)
                    for j in range(4):
                        v_tile(n + j, 3, False, j == 3, None)

            for s, (what, q) in enumerate(segments):
                if s == 1:
                    pe.wait_ge(S("picks_ready"), 1)
                    for b in range(3):
                        turn_picks(b)
                    pe.wait_ge(S("picks_copied"), 1)
                if what == "u":
                    if q >= 2:
                        pe.wait_ge(S("out_taken"), 16 * (q - 1))
                    u_segment(s, q)
                else:
                    pe.wait_ge(S("gelu_done"), (min(q + 2, 4)) * SEG + 4)
                    pe.wait_ge(S("gates_copied"), 3 * SEG + 3)
                    v_segment(s, q)
            pe.wait_ge(S("out_taken"), 64)
            norm_sum(ysq, 3, 0)

        @block.scalar
        def _(act):
            chain = Chain(act, S("act_step"))
            eps = prm("eps", 0)

            def activate(out, in_, func, **kw):
                return act.activation(out, in_, func, **kw)

            def copy(out, in_):
                return act.activation(out, in_, ACT.Copy)

            def root(out, in_, scale, bias):
                return act.activation(out, in_, ACT.Sqrt, bias=bias, scale=scale)

            def norm_root(_, src, sq, roots, c, bank, ready=lambda: None):
                ready()
                for kt in range(KT):
                    ins = activate(sq[:, kt, :], src[:, kt, :], ACT.Square)
                ins.then_inc(S("squares"), 1)
                act.wait_ge(S("square_sum"), c)
                root(roots[:, 0, :], ps[bank][:, 0:N], 1.0 / D, eps).then_inc(S("norm_root"), 1)

            def affine(dst, gains, shift, c, done):
                act.wait_ge(S("xn_ready"), c)
                for kt in range(1, KT, 2):
                    ins = activate(dst[:, kt, 0:TP], dst[:, kt, 0:TP], ACT.Identity, bias=mods[:, shift, kt, 0:1],
                                   scale=gains[:, kt, 0:1])
                ins.then_inc(done, 1)

            def ada_take(j):
                act.wait_ge(used, (n_ada0 + (j + 1) * KT) if j < 2 else (n_ada1 + (j - 1) * KT))
                for b in range(4):
                    ins = copy(adas[:, b * 512:(b + 1) * 512], ps[4 + b][:, :])
                ins.then_inc(S("ada_copied"), 1)

            def ada_store(j):
                act.wait_ge(S("ada_turned"), j + 1)
                copy(mods[:, ada_order[j]].rearrange("p k s -> p (k s)"), ps[4][:, 0:KT * NS]).then_inc(S("mods_raw"), 1)

            pending = [(j, q) for j in range(2, 8) for q in range(4)]

            def ada_more(count):
                for _ in range(min(count, len(pending))):
                    j, q = pending.pop(0)
                    if q == 0 and j > 2:
                        ada_store(j - 1)
                    if q == 3:
                        ada_take(j)

            def hi(n, i=0):
                act.wait_ge(landed[n % RING_SLOTS], (i + (n // RING_SLOTS + 1)) * 16)
                if n >= n_z + 2:
                    act.wait_ge(used, i * 4 + (n - 1))
                for c in range(2):
                    cols = slice(c * D // 2, (c + 1) * D // 2)
                    copy(hi_slot(n)[:, cols], ring[n % RING_SLOTS][:, cols]).then_inc(S("hi_ready"), 1)

            def split_hi(src, dst, c):
                for half in range(2):
                    copy(dst[:, half * 8:(half + 1) * 8], src[:, half * 8:(half + 1) * 8]).then_inc(S("act_hi"), 1)

            act.dma_start(words(M_PRM, PRM_N), T["prm"]).then_inc(S("const_in"), 16)
            act.dma_start(craw, T["c"]).then_inc(S("const_in"), 16)
            act.dma_start(words(M_CST0, CST0_N), T["cst0"]).then_inc(S("const_in"), 16)
            act.dma_start(words(M_CST1, CST1_N), T["cst1"]).then_inc(S("const_in"), 16)
            for half in range(2):
                act.dma_start(xT[:, half * 8:(half + 1) * 8], T["x"][:, half * 8:(half + 1) * 8]).then_inc(S("x_in"), 16)
            for name, src, dst in (("n0", T["n0"], aux("n0")), ("m0", T["m0"], aux("m0", rows=BH)),
                                   ("conv", T["conv0"], aux("conv")), ("shift", T["shift0"], aux("shift")),
                                   ("wg", T["w_g"], aux("wg")), ("w2", T["w2"], aux("w2")), ("a2", T["a2"], aux("a2")),
                                   ("g2", T["g2"], aux("g2"))):
                act.dma_start(dst, src).then_inc(S("aux_in"), 16)

            act.wait_ge(S("const_in"), 64)
            activate(csig, craw, ACT.Sigmoid).then_inc(S("cond_sig"), 1)
            act.wait_ge(S("x_in"), 32)
            norm_root(None, xT, xsq, rms, 1, 0)
            ada_take(0)
            ada_store(0)
            ada_take(1)
            ada_store(1)
            affine(hT, gain, SH_A, 1, S("h_ready_act"))
            act.wait_ge(S("h_ready"), 1)
            act.wait_ge(S("h_ready_act"), 1)
            split_hi(hT, h_hi, 1)
            hi(n_z)
            hi(n_z + 1)

            act.wait_ge(S("aux_in"), 128)
            zqs = zq[:, :, TP + 3:ZQW].rearrange("p s (b t) -> p s b t", t=7)
            conv0 = aux("conv", MT, NB, 3)
            act.wait_ge(S("pads_ready"), 2)
            with act.Fori(0, 2) as i:
                for j in range(4):
                    act.wait_ge(used, i * 4 + (n_z + j + 1))
                    hi(n_z + j + 2, i)
                    act.wait_ge(S("zq_free"), i * 4 + (j + 1))
                    copy(zq[:, j % 2, 3:TP + 3], ps[j % 2][:, 0:TP])
                    copy(zqs[:, j % 2, :, 3:7], ps[j % 2][:, TP:N].rearrange("p (b t) -> p b t", t=TS)).then_inc(S("z_free"), 1)
                    copy(zqs[:, j % 2, :, 0:3],
                         conv0[:, bass.ds(i * 4 + j, 1)].rearrange("p o b t -> p (o b) t")).then_inc(S("zq_full"), 1)
                    act.wait_ge(S("conv_ready"), i * 4 + (j + 1))
                    activate(conv[:, 1, 0:TP + 56], conv[:, 0, 0:TP + 56], ACT.Sigmoid).then_inc(S("sig_ready"), 1)
            with act.Fori(0, 2) as i:
                for j in range(4):
                    act.wait_ge(used, i * 4 + (n_z + 8 + j + 1))
                    hi(n_z + 8 + j + 2, i)
                    copy(bv[:, bass.ds(i * 4 + j, 1)].rearrange("p o n -> p (o n)"), ps[j % 2][:, 0:N]).then_inc(S("z_free"), 1)
            with act.Fori(0, 2) as i:
                for j in range(4):
                    act.wait_ge(used, i * 4 + (n_z + 16 + j + 1))
                    hi(n_z + 16 + j + 2, i)
                    activate(ymix[:, bass.ds(i * 4 + (MT + j), 1)].rearrange("p o n -> p (o n)"), ps[j % 2][:, 0:N],
                             ACT.Sigmoid).then_inc(S("z_free"), 1)
            act.wait_ge(S("row_abs"), 1)
            chain.link(activate(row["t"], row["t"], ACT.Exp, scale=-1.0))
            activate(row["t"], row["t"], ACT.Ln, bias=ones[0:BH, 0:1]).then_inc(S("row_ln"), 1)
            act.wait_ge(S("row_done"), 1)
            activate(row["em"], row["m"], ACT.Exp, scale=-1.0)
            activate(row["ws"], row["ws"], ACT.Exp)
            activate(row["wi"][:, 0:SM], row["wi"][:, 0:SM], ACT.Exp).then_inc(S("row_exp"), 1)

            zxs = zx[:, :, TP + 1:ZXW].rearrange("p s (b t) -> p s b t", t=5)
            shift0 = aux("shift", AT, NB)

            def take_z(i, j, n):
                act.wait_ge(used, i * 4 + (n_z + 24 + n + 1))
                if n < 24:
                    hi(n_z + 24 + n + 2, i)
                act.wait_ge(S("zx_free"), i * 4 + (n + 1))
                copy(zx[:, j % 2, 1:TP + 1], ps[j % 2][:, 0:TP])
                copy(zxs[:, j % 2, :, 1:5], ps[j % 2][:, TP:N].rearrange("p (b t) -> p b t", t=TS)).then_inc(S("z_free"), 1)
                src = shift0[:, n] if isinstance(i, int) else shift0[:, bass.ds(i * 4 + n, 1)].rearrange("p o b -> p (o b)")
                copy(zxs[:, j % 2, :, 0], src).then_inc(S("zx_full"), 1)

            with act.Fori(0, 6) as i:
                for j in range(4):
                    take_z(i, j, j)
            for j in range(2):
                take_z(0, j, 24 + j)
            act.wait_ge(S("zx_free"), AT + 2)
            activate(low[0:64, 0, :], low[0:64, 0, :], ACT.Tanh)
            activate(low[:, 1, :], low[:, 1, :], ACT.Sigmoid).then_inc(S("low_ready"), 1)

            for u in range(2 * BH):
                act.wait_ge(S("bc_ready"), u + 1)
                copy(bc[:, u // BH, u % BH, :], ps[2 + u % 2][:, 0:N]).then_inc(S("bc_done"), 1)
            for h in range(BH):
                ada_more(1)
                act.wait_ge(S("d_ready"), h + 1)
                activate(dd[:, 0, 0:TP + P], dd[:, 0, 0:TP + P], ACT.Exp, scale=-1.0)
                activate(dd[0:SM, 0, TP + P:DW], dd[0:SM, 0, TP + P:DW], ACT.Exp, scale=-1.0).then_inc(S("d_exp"), 1)
                ada_more(1)
                act.wait_ge(S("num_used"), h + 1)
                activate(hsq, hh, ACT.Square).then_inc(S("hsq_ready"), 1)
                act.wait_ge(S("ms_ready"), h + 1)
                root(rec[:, 1, :], ps[0][:, 0:N], 1.0 / DV, eps).then_inc(S("ms_root"), 1)

            for slot in range(2):
                act.wait_ge(S(f"c_stored{slot}"), 32)
            act.wait_ge(S("arz_clear"), 1)
            act.wait_ge(S("c_new"), BH)
            for f in range(MT):
                for q, dst, bias in ((0, lg, "w0"), (1, B, "a0")):
                    act.wait_ge(S("low_sum"), 2 * f + q + 1)
                    activate(dst[:, f, :], ps[2 * q + f % 2][:, 0:N], ACT.Sigmoid, bias=prm(bias, f)).then_inc(S("low_used"), 1)
            ada_more(1)
            act.wait_ge(S("kk_ready"), 1)
            activate(bonus, kk, ACT.Square).then_inc(S("kksq_ready"), 1)
            ada_more(1)
            for f in range(MT):
                act.wait_ge(S("kk_sum"), f + 1)
                root(bonus[:, f, :], ps[f % 4][:, 0:N], 1.0, prm("zero", 0)).then_inc(S("kk_root"), 1)
            act.wait_ge(S("logs_ready"), 1)
            activate(words(m2, 3 * MT * CH + MT * NB), words(m2, 3 * MT * CH + MT * NB), ACT.Exp)
            activate(t1, t1, ACT.Exp).then_inc(S("before_ready"), 1)
            act.wait_ge(S("a_done"), 1)
            chain.link(activate(t1, lg, ACT.Exp))
            activate(lg, lg, ACT.Exp, scale=-1.0).then_inc(S("decays_ready"), 1)
            ada_more(1)

            for it in range(2 * CH + 2):
                c, hg = it // 2, it % 2
                sample = c == CH
                w = SM if sample else L
                f0 = 4 * hg
                tk = tok_s if sample else tok
                for q in range(3):
                    act.wait_ge(S("tok_ready"), it * 3 + q + 1)
                    copy(tk[:, q, :], ps[q][0:w, :]).then_inc(S("tok_done"), 1)
                ada_more(2)
                levels = 2 if sample else LEVELS
                halves = 1 if sample else 2
                x = X_s if sample else X
                per = HG // halves
                xd = 2 * LEVELS * min(it, 4) + (2 * hg if sample else 0)
                with act.Fori(0, levels) as i:
                    for q in range(halves):
                        act.wait_ge(S("x_sum"), i * halves + (xd + q + 1))
                        copy(x[:, q * per:(q + 1) * per, :].rearrange("p h t -> p (h t)"),
                             ps[q][0:w, 0:per * w]).then_inc(S("x_copied"), 1)
                act.wait_ge(S("w_sum"), it + 1)
                copy(W_s if sample else W, ps[0][0:w, :]).then_inc(S("w_copied"), 1)
                act.wait_ge(S("sa_sum"), it + 1)
                copy(SA_s if sample else SA, ps[1][0:w, :]).then_inc(S("sa_copied"), 1)
                ada_more(1)
                act.wait_ge(S("y_sum"), it + 1)
                copy(ymix[:, f0:f0 + 4, slice(TP, N) if sample else slice(c * L, (c + 1) * L)],
                     ps[2][:, 0:4 * w].rearrange("p (f t) -> p f t", f=4)).then_inc(S("y_taken"), 1)

            for f in range(MT):
                act.wait_ge(S("centred"), f + 1)
                if f >= 2:
                    act.wait_ge(S("var_sum"), f - 1)
                activate(tn[:, f % 2, :], ymix[:, f, :], ACT.Square).then_inc(S("ysq_ready"), 1)
                act.wait_ge(S("var_sum"), f + 1)
                root(hrt[:, f % 2, :], ps[f % 2][:, 0:N], 1.0 / AHD, prm("gneps", 0)).then_inc(S("var_root"), 1)
            ada_more(len(pending))
            ada_store(7)

            act.wait_ge(S("gated"), MT)
            split_hi(ymix, y_hi, 2)
            hi(n_wo)
            hi(n_wo + 1)
            with act.Fori(0, KT // 4) as i:
                for j in range(4):
                    act.wait_ge(used, i * 4 + (n_wo + j + 1))
                    hi(n_wo + j + 2, i)
            norm_root(None, x1, x1sq, rms2, 2, 2, lambda: act.wait_ge(S("out_free"), KT + 2))
            affine(h2, gain2, SH_C, 2, S("h_ready_act"))
            act.wait_ge(S("h_ready"), 2)
            act.wait_ge(S("h_ready_act"), 2)
            split_hi(h2, h2_hi, 3)
            with act.Fori(0, KT // 4) as i:
                for j in range(4):
                    act.wait_ge(used, i * 4 + (n_q + j + 1))
                    hi(n_q + j + 2, i)
                    copy(qT[:, bass.ds(i * 4 + j, 1)].rearrange("p o n -> p (o n)"), ps[j % 2][:, 0:N]).then_inc(S("q_free"), 1)
            for b in range(3):
                w = P if b < 2 else SM
                act.wait_ge(S("scores"), b + 1)
                for q in range(4):
                    ins = copy(sc[0:w, b, 4 * q:4 * q + 4].rearrange("p g k -> p (g k)"), ps[4 * (b % 2) + q][0:w, :])
                ins.then_inc(S("score_copied"), 1)

            for s, (what, q) in enumerate(segments):
                n0 = n_p + s * SEG
                if s == 1:
                    act.wait_ge(S("gate_arg"), 1)
                    activate(best, best, ACT.Exp).then_inc(S("gate_exp"), 1)
                bodies = SEG // 4 - (s == len(segments) - 1)

                def tile(i, j, ahead=True):
                    act.wait_ge(used, i * 4 + (n0 + j + 1))
                    if ahead:
                        hi(n0 + j + 2, i)
                    if what == "u":
                        activate(acts[q % 2][:, bass.ds(i * 4 + j, 1), :].rearrange("p o n -> p (o n)"), ps[j][:, 0:N],
                                 ACT.Gelu).then_inc(S("gelu_done"), 1)

                def take_gates(i, j):
                    act.wait_ge(S("g_mul"), i * 4 + (j + 1))
                    act.wait_ge(S(f"gates_stored{j % 2}"), i * 32 + 16 * (j // 2 + 1))
                    for e in range(3):
                        act.wait_ge(S("hot_done"), i * 12 + (3 * j + e + 4))
                        copy(stage[j % 2][:, :, e * HOT_TOKENS:(e + 1) * HOT_TOKENS, :],
                             ps[4 + e][:, 0:HOT_TOKENS * NK].rearrange("p (t q k) -> p q t k", q=4, k=QUARTER)
                             ).then_inc(S("gates_copied"), 1)
                    act.wait_ge(S("gates_copied"), i * 12 + (3 * j + 6))
                    width = GATE_TOKENS * QUARTER
                    at = bass.ds(i * (4 * width) + j * width, width)
                    act.dma_start(gates_dram[:, :, at].rearrange("q p c -> p q c"),
                                  stage[j % 2][:, 1:4].rearrange("p q t k -> p q (t k)")).then_inc(S(f"gates_stored{j % 2}"), 16)

                with act.Fori(0, bodies) as i:
                    for j in range(4):
                        tile(i, j)
                        if s == 1:
                            take_gates(i, j)
                if bodies < SEG // 4:
                    for j in range(4):
                        tile(bodies, j, j < 2)

            norm_root(None, xo, ysq, rms3, 3, 0, lambda: act.wait_ge(S("out_taken"), 64))
            affine(yn, gain3, SH_F, 3, S("y_done"))

        @block.vector
        def _(dve):
            chain = Chain(dve, S("dve_step"))
            link = chain.link
            tt = dve.tensor_tensor
            stt = dve.scalar_tensor_tensor

            def ts(out, in_, s1, s2, op0, op1=None):
                if op1 is None:
                    return dve.tensor_scalar(out, in_, s1, None, op0)
                return dve.tensor_scalar(out, in_, s1, s2, op0, op1)

            def add_bias(first, count):
                m = mods[:, first:first + count].rearrange("p m k s -> p (m k) s")
                link(tt(m, m, over(prm("bada", first * KT, count * KT), 2, NS), ALU.add))

            def norm(src, dst, roots, gains, shift, scale, g, c, done):
                link(stt(out=gains, in0=mods[:, scale], scalar=1.0, in1=over(prm(g), 2, NS), op0=ALU.add, op1=ALU.mult))
                dve.wait_ge(S("norm_root"), c)
                link(dve.reciprocal(roots[:, 1, :], roots[:, 0, :]))
                tt(dst, src, over(roots[:, 1, :], 1, KT), ALU.mult).then_inc(S("xn_ready"), 1)
                dve.wait_ge(S("xn_ready"), c)
                for kt in range(0, KT, 2):
                    ts(dst[:, kt, 0:TP], dst[:, kt, 0:TP], gains[:, kt, 0:1], mods[:, shift, kt, 0:1], ALU.mult, ALU.add)
                link(tt(samp(dst), samp(dst), over(gains[:, :, 1:], 3, TS), ALU.mult))
                tt(samp(dst), samp(dst), over(mods[:, shift, :, 1:], 3, TS), ALU.add).then_inc(done, 1)

            def split_lo(src, hi, dst, c):
                for half in range(2):
                    kts = slice(half * 8, (half + 1) * 8)
                    dve.wait_ge(S("act_hi"), 2 * (c - 1) + half + 1)
                    tt(dst[:, kts], src[:, kts], hi[:, kts].bitcast(F32), ALU.subtract).then_inc(S("act_split"), 1)

            dve.wait_ge(S("cond_sig"), 1)
            link(dve.memset(silc, 0.0))
            tt(silc[:, :, 0:NS], craw, csig, ALU.mult).then_inc(S("cond_ready"), 1)
            dve.wait_ge(S("mods_raw"), 2)
            add_bias(0, 2)
            norm(xT, hT, rms, gain, SH_A, SC_A, "gmix", 1, S("h_ready"))
            dve.wait_ge(S("h_ready"), 1)
            dve.wait_ge(S("h_ready_act"), 1)
            dve.wait_ge(S("gates_ready"), 1)
            split_lo(hT, h_hi, h_lo, 1)

            dve.memset(zq, 0.0).then_inc(S("pads_ready"), 1)
            dve.memset(zx, 0.0).then_inc(S("pads_ready"), 1)
            CW = TP + 56
            dve.wait_ge(S("pads_ready"), 2)
            for is_k in range(2):
                scale = 1.0 if is_k == 0 else DQK ** -0.5
                for j in range(4):
                    n = 4 * is_k + j
                    dve.wait_ge(S("zq_free"), n + 2)
                    dve.wait_ge(S("zq_full"), n + 1)
                    z = zq[:, j % 2]
                    wcol = [prm("convw", tap * MT + n) for tap in range(CONV)]
                    dve.tensor_copy(cvo[:, n], z[:, TP:TP + 7 * NS].rearrange("p (b t) -> p b t", t=7)[:, :, 0:3])
                    link(ts(conv[:, 0, 0:CW], z[:, 0:CW], wcol[0], prm("convb", n), ALU.mult, ALU.add))
                    for tap in range(1, CONV):
                        ins = stt(out=conv[:, 0, 0:CW], in0=z[:, tap:tap + CW], scalar=wcol[tap], in1=conv[:, 0, 0:CW],
                                  op0=ALU.mult, op1=ALU.add)
                        if tap < CONV - 1:
                            link(ins)
                    ins.then_inc(S("conv_ready"), 1)
                    dve.wait_ge(S("sig_ready"), n + 1)
                    stt(out=qk[:, n, 0:TP], in0=conv[:, 0, 0:TP], scalar=scale, in1=conv[:, 1, 0:TP], op0=ALU.mult, op1=ALU.mult)
                    c4 = [conv[:, e, TP + 3:TP + 3 + 56].rearrange("p (b t) -> p b t", t=7)[:, :, 0:TS] for e in range(2)]
                    stt(out=qk[:, n, TP:N].rearrange("p (b t) -> p b t", t=TS), in0=c4[0], scalar=scale, in1=c4[1],
                        op0=ALU.mult, op1=ALU.mult).then_inc(S("zq_free"), 1)

            ts(row["i"], ps[2][0:BH, 0:N], prm("gatebias", 0, rows=BH), None, ALU.add)
            link(ts(row["f"], ps[2][32:32 + BH, 0:N], prm("gatebias", 0, rows=BH, first=32), None, ALU.add))
            stt(out=row["t"], in0=row["f"], scalar=-1.0, in1=row["f"], op0=ALU.mult, op1=ALU.max).then_inc(S("row_abs"), 1)
            dve.wait_ge(S("row_ln"), 1)
            link(stt(out=row["f"], in0=row["f"], scalar=0.0, in1=row["t"], op0=ALU.min, op1=ALU.subtract))
            link(dve.tensor_tensor_scan(row["b"], cst1("breset", rows=BH), row["f"], 0.0, ALU.mult, ALU.add))
            link(tt(row["g"], row["i"], row["b"], ALU.subtract))
            link(dve.tensor_copy(row["g2"], row["g"]))
            ts(row["g2"][:, 0:1], row["g"][:, 0:1], 0.0, None, ALU.max)
            link(tt(row["g2"][:, TP:N:TS], row["g"][:, TP:N:TS], aux("m0", rows=BH), ALU.max))
            link(dve.tensor_tensor_scan(row["mx"], cst1("mreset", rows=BH), row["g2"], 0.0, ALU.add, ALU.max))
            tt(row["m"], row["b"], row["mx"], ALU.add)
            ts(row["ws"][:, 0:TP], row["g"][:, 0:TP], row["mx"][:, TP - 1:TP], None, ALU.subtract)
            tt(samp(row["ws"]), samp(row["g"]), over(row["mx"][:, TP + 3:N:TS], 2, TS), ALU.subtract)
            link(tt(row["wi"][:, 0:SM].rearrange("p (b t) -> p b t", t=TS), over(aux("m0", rows=BH), 2, TS),
                    samp(row["mx"]), ALU.subtract))
            dve.tensor_copy(mo, row["m"][:, TP - 1:N:TS]).then_inc(S("row_done"), 1)

            zxs = zx[:, :, TP + 1:ZXW].rearrange("p s (b t) -> p s b t", t=5)
            zds = zd[:, 0, TP:ZXW - 1].rearrange("p (b t) -> p b t", t=5)

            def shift_z(i, j, n, dst, at):
                def pick_(a, m):
                    return a[:, m] if isinstance(i, int) else a[:, bass.ds(i * 4 + m, 1)].rearrange("p o n -> p (o n)")
                mu = prm("mu", n) if isinstance(i, int) else prm("mu")[:, bass.ds(i * 4 + n, 1)]
                dve.wait_ge(S("zx_free"), i * 4 + (n + 2))
                dve.wait_ge(S("zx_full"), i * 4 + (n + 1))
                z = zx[:, j % 2]
                link(tt(zd[:, 0, 0:ZXW - 1], z[:, 0:ZXW - 1], z[:, 1:ZXW], ALU.subtract))
                out = pick_(dst, at)
                stt(out=out[:, 0:TP], in0=zd[:, 0, 0:TP], scalar=mu, in1=z[:, 1:TP + 1], op0=ALU.mult, op1=ALU.add)
                stt(out=out[:, TP:N].rearrange("p (b t) -> p b t", t=TS), in0=zds[:, :, 1:5], scalar=mu,
                    in1=zxs[:, j % 2, :, 1:5], op0=ALU.mult, op1=ALU.add)
                dve.tensor_copy(pick_(sho, n), z[:, TP:ZXW:5]).then_inc(S("zx_free"), 1)

            for first, count, dst in ((0, 2, r), (8, 4, words(za, 2 * MT, N))):
                base = chain.n
                with dve.Fori(0, count) as i:
                    chain.n = i * 4 + base
                    for j in range(4):
                        shift_z(i, j, first + j, dst, j)
                chain.n = base + 4 * count
            for j in range(2):
                shift_z(0, j, 24 + j, low, j)

            dve.wait_ge(S("cols_ready"), 1)
            dve.tensor_copy(wib.rearrange("p h t -> p (h t)"), ps[0][:, 0:BH * SM])
            dve.tensor_copy(colg[:, 0:2].rearrange("p b q h -> p (b q h)"), ps[1][:, 0:16])
            ins = dve.tensor_copy(colg[0:SM, 2].rearrange("p q h -> p (q h)"), ps[1][0:SM, 16:24])
            ins.then_inc(S("cols_done"), 1)
            dve.wait_ge(S("cols_done"), 1)
            link(dve.memset(words(q7, 3 * BH * (DV + 1)), 1.0))
            fills = [("v", b, g) for b in range(3) for g in range(2)] + [("k", b, 0) for b in range(3)]
            for u, (what, b, g) in enumerate(fills):
                dve.wait_ge(S("turn_ready"), u + 1)
                w = P if b < 2 else SM
                src = ps[u % 4][0:w, :]
                if what == "v":
                    out = vtok[:, b] if b < 2 else vtok_s
                    ins = dve.tensor_copy(out[:, 2 * g:2 * g + 2, 0:DV], src.rearrange("p (h d) -> p h d", h=2))
                else:
                    out = ktok[:, b] if b < 2 else ktok_s
                    ins = tt(out, src.rearrange("p (h d) -> p h d", h=BH), over(colg[0:w, b, 1, :], 2, P), ALU.mult)
                ins.then_inc(S("turn_done"), 1)
            dve.wait_ge(S("turn_done"), 9)
            dve.wait_ge(S("bc_done"), 2 * BH)
            incl, sincl = cst1("incl"), cst1("sincl", rows=SM)
            n0 = aux("n0", BH, NB)
            for h in range(BH):
                if h:
                    dve.wait_ge(S("c_new"), h)
                mx = bc[:, 0, h, :]
                ts(dd[:, 0, 0:TP], mx[:, 0:TP], colg[:, 0, 0, h:h + 1], 0.0, ALU.subtract, ALU.max)
                ts(dd[:, 0, TP:TP + P], mx[:, P:TP], colg[:, 1, 0, h:h + 1], 0.0, ALU.subtract, ALU.max)
                ts(dd[0:SM, 0, TP + P:DW], mx[0:SM, TP:N], colg[0:SM, 2, 0, h:h + 1], 0.0, ALU.subtract,
                   ALU.max).then_inc(S("d_ready"), 1)
                link(tt(qw[:, 0, :], qk[:, h, TP:N], wib[:, h, :], ALU.mult))
                tt(qw[:, 1, :].rearrange("p (b t) -> p b t", t=TS), qw[:, 0, :].rearrange("p (b t) -> p b t", t=TS),
                   over(n0[:, h, :], 2, TS), ALU.mult)
                tt(kwm, over(ktok_s[:, h, :], 1, NB), over(cst1("seq", rows=SM), 2, P), ALU.mult).then_inc(S("kwm_ready"), 1)
                dve.wait_ge(S("d_exp"), h + 1)
                tt(dd[:, 0, 0:P], dd[:, 0, 0:P], incl, ALU.mult)
                tt(dd[:, 0, TP:TP + P], dd[:, 0, TP:TP + P], incl, ALU.mult)
                link(tt(dd[0:SM, 0, TP + P:DW], dd[0:SM, 0, TP + P:DW], sincl, ALU.mult))
                dve.wait_ge(S("qk_ready"), h + 1)
                tt(dd[:, 1, 0:TP + P], ps[0][:, 0:TP + P], dd[:, 0, 0:TP + P], ALU.mult)
                tt(dd[0:SM, 1, TP + P:DW], ps[0][0:SM, TP + P:DW], dd[0:SM, 0, TP + P:DW], ALU.mult).then_inc(S("s_ready"), 1)
                dve.wait_ge(S("num_ready"), h + 1)
                link(stt(out=rec[:, 0, :], in0=ps[3][:, 0:N], scalar=-1.0, in1=bc[:, 1, h, :], op0=ALU.mult, op1=ALU.max))
                link(tt(rec[:, 0, :], ps[3][:, 0:N], rec[:, 0, :], ALU.max))
                link(dve.reciprocal(rec[:, 0, :], rec[:, 0, :]))
                tt(hh[:, 0, :], ps[1][:, 0:N], rec[:, 0, :], ALU.mult)
                tt(hh[:, 1, :], ps[2][:, 0:N], rec[:, 0, :], ALU.mult).then_inc(S("num_used"), 1)
                if h >= 2:
                    dve.wait_ge(S(f"cp_stored{h % 2}"), 16)
                for u in range(NS):
                    dve.wait_ge(S("upd_ready"), h * NS + u + 1)
                    out = ps[1 + u % 3]
                    if u < NB:
                        dC = wib[:, h, u * TS + 3:u * TS + 4]
                        c_u = cring[:, h % 2, u, :]
                        stt(out=c_u, in0=c_u, scalar=dC, in1=out[:, 0:DV], op0=ALU.mult, op1=ALU.add)
                        ins = stt(out=n_out[:, h, u + 1:u + 2], in0=n0[:, h, u:u + 1], scalar=dC, in1=out[:, DV:DV + 1],
                                  op0=ALU.mult, op1=ALU.add)
                    else:
                        dve.tensor_copy(n_out[:, h, 0:1], out[:, DV:DV + 1])
                        ins = dve.tensor_copy(c_out[:, h % 2, :], out[:, 0:DV])
                    ins.then_inc(S("upd_used"), 1)
                dve.wait_ge(S("upd_used"), (h + 1) * NS)
                dve.wait_ge(S("num_used"), h + 1)
                dve.wait_ge(S("ms_root"), h + 1)
                link(dve.reciprocal(rec[:, 1, :], rec[:, 1, :]))
                for i in range(2):
                    n = 2 * h + i
                    ins = stt(out=hh[:, i, :], in0=hh[:, i, :], scalar=prm("bnorm", n), in1=rec[:, 1, :], op0=ALU.mult,
                              op1=ALU.mult)
                link(ins)
                tt(ymix[:, MT + 2 * h:MT + 2 * h + 2, :], ymix[:, MT + 2 * h:MT + 2 * h + 2, :], hh,
                   ALU.mult).then_inc(S("c_new"), 1)
            dve.wait_ge(S("c_new"), BH)

            dve.wait_ge(S("arz_clear"), 1)
            dve.wait_ge(S("low_used"), 2 * MT)
            tt(kk, k, over(prm("kk"), 2, N), ALU.mult).then_inc(S("kk_ready"), 1)
            link(ts(t1f, lgf, -math.exp(-0.5), None, ALU.mult))
            for f in range(MT):
                ins = dve.tensor_tensor_scan(lg[:, f, :], cst1("wreset"), t1[:, f, :], 0.0, ALU.mult, ALU.add)
            link(ins)
            centre, end = lg[:, :, L // 2 - 1:TP:L], lg[:, :, L - 1:TP:L]
            dve.tensor_copy(cen[:, 0], centre)
            dve.tensor_copy(cen[:, 2], end)
            dve.tensor_copy(cen_s, lg[:, :, TP + TS - 1:N:TS])
            link(tt(cen[:, 1], end, centre, ALU.subtract))
            lgp = lg[:, :, 0:TP].rearrange("p f (c t) -> p f c t", t=L)
            link(tt(lgp, lgp, over(cen[:, 0], 3, L), ALU.subtract))
            tt(t1f, lgf, t1f, ALU.subtract).then_inc(S("logs_ready"), 1)
            dve.wait_ge(S("kk_root"), MT)
            link(ts(bonusf, bonusf, 1e-12, None, ALU.max))
            link(dve.reciprocal(bonusf, bonusf))
            link(tt(kkf, kkf, bonusf, ALU.mult))

            def halves(slot, op):
                for hp in range(2):
                    rows = slice(64 * hp, 64 * hp + 64)
                    op(arz[rows, hp::2, slot, :], rows, slice(0, TP))
                    ins = op(arz_s[rows, hp::2, slot, :], rows, slice(TP, N))
                return ins

            dve.wait_ge(S("before_ready"), 1)
            halves(0, lambda out, rows, cols: stt(out=out, in0=kk[rows, :, cols], scalar=-1.0, in1=t1[rows, :, cols],
                                                  op0=ALU.mult, op1=ALU.mult)).then_inc(S("a_done"), 1)
            link(stt(out=bonus, in0=B, scalar=-1.0, in1=over(prm("ka"), 2, N), op0=ALU.add, op1=ALU.mult))
            link(stt(out=kf, in0=bonusf, scalar=1.0, in1=kf, op0=ALU.add, op1=ALU.mult))
            tt(Bf, Bf, kkf, ALU.mult)
            link(tt(bonusf, rf, kf, ALU.mult))
            tt(bonus, bonus, over(prm("rk"), 2, N), ALU.mult).then_inc(S("rk_ready"), 1)
            dve.wait_ge(S("rk_ready"), 1)
            dve.wait_ge(S("decays_ready"), 1)
            halves(1, lambda out, rows, cols: tt(out, r[rows, :, cols], t1[rows, :, cols], ALU.mult))
            tt(kf, kf, lgf, ALU.mult)
            tt(Bf, Bf, lgf, ALU.mult).then_inc(S("ops_ready"), 1)
            for f in range(MT):
                dve.wait_ge(S("rk_sum"), f + 1)
                tt(bonus[:, f, :], ps[f % 4][:, 0:N], v[:, f, :], ALU.mult).then_inc(S("bonus_done"), 1)

            both = words(M_CST1 + CST1["strict"][0], 2 * L)
            both_s = words(M_CST1 + CST1["sstrict"][0], 2 * SM, rows=SM)
            for it in range(2 * CH + 2):
                c, hg = it // 2, it % 2
                sample = c == CH
                w = SM if sample else L
                f0 = 4 * hg
                ti, tt_, mk, gm = (Ti_s, Tt_s, masked_s, gram_s) if sample else (Ti, Tt, masked, gram)
                fills = 2 if sample else 8
                n_gram = 8 * min(it, 4) + (2 * hg if sample else 0)
                for g in range(fills):
                    dve.wait_ge(S("gram_ready"), n_gram + g + 1)
                    if sample:
                        ins = tt(gm[:, :, 2 * g:2 * g + 2, :].rearrange("p h q t -> p h (q t)"),
                                 ps[3 * (1 - g)][0:w, :].rearrange("p (h x) -> p h x", h=HG), over(both_s, 1, HG), ALU.mult)
                    else:
                        q, pair = g // 4, g % 4
                        ins = tt(gm[:, 2 * pair:2 * pair + 2, 2 * q:2 * q + 2, :].rearrange("p h q t -> p h (q t)"),
                                 ps[(3 + g) % 4][:, :].rearrange("p (h x) -> p h x", h=2), over(both, 1, 2), ALU.mult)
                    ins.then_inc(S("gram_done"), 1)
                    if g == 0:
                        dve.tensor_copy(ti, over(ident[0:w, 0:w], 1, HG))
                        link(dve.tensor_copy(tt_, over(ident[0:w, 0:w], 1, HG)))
                        if sample:
                            tt(azm, over(arz_s[:, 2 * f0:2 * f0 + HG, 0, :], 2, NB), over(cst1("seqcol", NB, SM), 1, HG),
                               ALU.mult).then_inc(S("azm_ready"), 1)
                dve.wait_ge(S("gram_done"), n_gram + fills)
                levels = 2 if sample else LEVELS
                halves_ = 1 if sample else 2
                per = HG // halves_
                td = 4 * LEVELS * min(it, 4) + (4 * hg if sample else 0)
                masks = cst1("slevel", 2, SM, rows=SM) if sample else cst1("level", LEVELS, L)
                with dve.Fori(0, levels) as i:
                    tt(mk, gm[:, :, 0, :], over(masks[:, bass.ds(i, 1)].rearrange("p o t -> p (o t)"), 1, HG),
                       ALU.mult).then_inc(S("masked_ready"), 1)
                    for q in range(halves_):
                        hs = slice(q * per, (q + 1) * per)
                        for e, (dst, bank) in enumerate(((ti, 2 + q), (tt_, q))):
                            k_ = 2 * q + e
                            dve.wait_ge(S("t_sum"), i * (2 * halves_) + (td + k_ + 1))
                            tt(dst[:, hs, :], dst[:, hs, :], ps[bank][0:w, 0:per * w].rearrange("p (h t) -> p h t", h=per),
                               ALU.add).then_inc(S("t_added"), 1)
                    dve.wait_ge(S("t_added"), i * (2 * halves_) + (td + 2 * halves_))
                if not sample:
                    fs = slice(f0, f0 + 4)
                    dve.wait_ge(S("state_sum"), it + 1)
                    src = ps[3][:, 0:4 * AHD].rearrange("p (f i) -> p f i", f=4)
                    fresh = over(cen[:, 1, fs, c], 2, AHD)
                    if c == 0:
                        link(tt(state[:, fs], src, fresh, ALU.mult))
                        tt(state_c[:, fs], state[:, fs], over(cen[:, 0, fs, 1], 2, AHD), ALU.mult).then_inc(S("state_step"), 1)
                    else:
                        tmp = words(M_AUX + AUX["w2"][0], 4, AHD)
                        tt(tmp, src, fresh, ALU.mult)
                        link(tt(state[:, fs], state[:, fs], over(cen[:, 2, fs, c], 2, AHD), ALU.mult))
                        tt(state[:, fs], state[:, fs], tmp, ALU.add).then_inc(S("state_step"), 1)
                else:
                    dve.wait_ge(S("sa_copied"), it + 1)
                    for j in range(4):
                        f = f0 + j
                        if j % 2 == 0:
                            if f:
                                dve.wait_ge(S("wkv_sum"), f)
                            hs = slice(2 * j, 2 * j + 4)
                            for q, src in enumerate((SA_s, tok_s[:, 2, :])):
                                src = src.rearrange("p (h i) -> p h i", h=HG)[:, hs]
                                ins = tt(sam[:, q], over(src, 2, NB), over(over(cst1("seq", rows=SM), 1, 4), 3, AHD), ALU.mult)
                            ins.then_inc(S("sam_ready"), 1)
                        dve.wait_ge(S("wkv_sum"), f + 1)
                        bank = 3 if j % 2 else 1
                        s_f = wkv_s[:, f]
                        link(tt(s_f, s_f, ps[bank][:, :].rearrange("p (b i) -> p b i", b=NB), ALU.add))
                        tt(s_f, s_f, over(cen_s[:, f, :], 2, AHD), ALU.mult).then_inc(S("wkv_new"), 1)

            for f in range(MT):
                dve.wait_ge(S("mean_sum"), f + 1)
                stt(out=ymix[:, f, :], in0=ps[f % 4][:, 0:N], scalar=-1.0 / AHD, in1=ymix[:, f, :], op0=ALU.mult,
                    op1=ALU.add).then_inc(S("centred"), 1)
            for f in range(MT):
                y = ymix[:, f, :]
                dve.wait_ge(S("var_root"), f + 1)
                link(dve.reciprocal(hrt[:, f % 2, :], hrt[:, f % 2, :]))
                link(tt(y, y, hrt[:, f % 2, :], ALU.mult))
                link(ts(y, y, prm("lnw", f), prm("lnb", f), ALU.mult, ALU.add))
                link(tt(y, y, bonus[:, f, :], ALU.add))
                dve.wait_ge(S("gate_sum"), f + 1)
                tt(y, ps[2 + f % 2][:, 0:N], y, ALU.mult).then_inc(S("gated"), 1)

            def gated_add(src, dst, gate, gate_s, tmp):
                link(tt(tmp.rearrange("p (b t) -> p b t", t=TS), src[:, TP:N].rearrange("p (b t) -> p b t", t=TS),
                        over(gate_s, 2, TS), ALU.mult))
                stt(out=dst[:, 0:TP], in0=src[:, 0:TP], scalar=gate, in1=dst[:, 0:TP], op0=ALU.mult, op1=ALU.add)
                return tt(dst[:, TP:N], dst[:, TP:N], tmp, ALU.add)

            dve.wait_ge(S("gated"), MT)
            split_lo(ymix, y_hi, y_lo, 2)
            dve.wait_ge(S("mods_raw"), 8)
            add_bias(2, 6)
            dve.wait_ge(S("x_again"), 16)
            base = chain.n
            with dve.Fori(0, KT // 4) as i:
                chain.n = i * 4 + base
                for j in range(4):
                    dve.wait_ge(used, i * 4 + (n_wo + j + 1))
                    dve.wait_ge(S("out_free"), i * 4 + (j + 2))
                    def at(a):
                        return a[:, bass.ds(i * 4 + j, 1)].rearrange("p o n -> p (o n)")
                    ga = at(mods[:, G_A])
                    gated_add(ps[j % 2], at(x1), ga[:, 0:1], ga[:, 1:NS], xt_s).then_inc(S("out_free"), 1)
            chain.n = base + KT
            dve.wait_ge(S("out_free"), KT + 2)
            norm(x1, h2, rms2, gain2, SH_C, SC_C, "gffn", 2, S("h_ready"))

            dve.wait_ge(S("h_ready"), 2)
            dve.wait_ge(S("h_ready_act"), 2)
            split_lo(h2, h2_hi, h2_lo, 3)

            iota16 = iota[:, 0:TOPK]
            for b in range(3):
                w = P if b < 2 else SM
                R = slice(0, w)
                dve.wait_ge(S("score_copied"), b + 1)
                cand = sc[:, b].rearrange("p g k -> p (g k)").rearrange("p (h k) -> p h k", h=PH)
                rest2 = rest.rearrange("p g k -> p (g k)").rearrange("p (h k) -> p h k", h=PH)

                def best16(src, rest, out, index, groups):
                    for g in range(groups):
                        ins = dve.max(out[R, g, 0:8], src[R, g])
                    link(ins)
                    for g in range(groups):
                        dve.max_index(index[R, g, 0:8], out[R, g, 0:8], src[R, g])
                        ins = dve.match_replace(rest[R, g], out[R, g, 0:8], src[R, g], NEG)
                    link(ins)
                    for g in range(groups):
                        ins = dve.max(out[R, g, 8:16], rest[R, g])
                    link(ins)
                    for g in range(groups):
                        ins = dve.max_index(index[R, g, 8:16], out[R, g, 8:16], rest[R, g])
                    link(ins)

                best16(sc[:, b], rest, top, topi.bitcast(U32), GR)
                link(dve.tensor_copy(topf[R], topi.bitcast(U32)[R]))
                t4 = top.rearrange("p (h q) k -> p h q k", q=2)
                link(tt(cand[R].rearrange("p h (a c) -> p h a c", a=TOPK), over(t4[R, :, 0], 3, TOPK),
                        over(t4[R, :, 1], 2, TOPK), ALU.add))
                best16(cand, rest2, best[:, b], posi.bitcast(U32), PH)
                pu = part.bitcast(U32)
                dve.tensor_scalar(pu[R, 0], posi.bitcast(U32)[R], 4, None, ALU.logical_shift_right)
                link(dve.tensor_scalar(pu[R, 1], posi.bitcast(U32)[R], TOPK - 1, None, ALU.bitwise_and))
                link(dve.tensor_copy(partf[R], pu[R]))
                link(dve.tensor_copy(psum8[R, b, 1], best[R, b, :, 0]))
                tt(best[R, b], best[R, b], over(psum8[R, b, 1], 2, TOPK), ALU.subtract)
                f4 = topf.rearrange("p (h q) k -> p h q k", q=2)
                for q in range(2):
                    at = partf[R, q].rearrange("p h s -> p (h s)")
                    link(tt(eq[R], over(at, 2, TOPK), over(iota16[R], 1, PH * TOPK), ALU.is_equal))
                    e4 = eq[R].rearrange("p (h s) a -> p h s a", h=PH)
                    link(tt(e4, e4, over(f4[R, :, q], 2, TOPK), ALU.mult))
                    link(dve.tensor_reduce(pick[R, b, q], eq[R], AX.X, ALU.add))
            dve.memset(best[SM:2 * SM, 2], 0.0)
            dve.memset(best[2 * SM:P, 2], 0.0).then_inc(S("gate_arg"), 1)
            dve.wait_ge(S("gate_exp"), 1)
            for b in range(3):
                R = slice(0, P if b < 2 else SM)
                link(dve.tensor_reduce(psum8[R, b, 0], best[R, b], AX.X, ALU.add))
                link(dve.reciprocal(psum8[R, b, 1], psum8[R, b, 0]))
                ins = tt(pick[R, b, 2].rearrange("p (h s) -> p h s", h=PH), best[R, b], over(psum8[R, b, 1], 2, TOPK), ALU.mult)
            ins.then_inc(S("picks_ready"), 1)
            for b in range(3):
                w = P if b < 2 else SM
                dve.wait_ge(S("picks_turned"), b + 1)
                ins = dve.tensor_copy(pickT[:, :, b * P:b * P + w],
                                      ps[4 + b][:, 0:3 * P].rearrange("p (q t) -> p q t", q=3)[:, :, 0:w])
            ins.then_inc(S("picks_copied"), 1)
            dve.wait_ge(S("picks_copied"), 1)

            def hot_rows(i, j, e):
                token = i * (4 * GATE_TOKENS) + (j * GATE_TOKENS + e * HOT_TOKENS)
                dve.wait_ge(S("hot_done"), i * 12 + (3 * j + e + 1))
                for t in range(HOT_TOKENS):
                    def at(row):
                        return pickT[:, row, bass.ds(token + t, 1)]
                    ts(hot1[:, e, t, :], iota, at(0), at(2), ALU.is_equal, ALU.mult)
                i2 = pickT[:, 1, bass.ds(token, HOT_TOKENS)]
                tt(hot2[:, e], over(iota, 1, HOT_TOKENS), over(i2, 2, NK), ALU.is_equal).then_inc(S("hot_ready"), 1)

            def first_quarter(i, j):
                dve.wait_ge(S("gates_copied"), i * 12 + (3 * j + 6))
                a = acts[0][:, :, bass.ds(i * (4 * GATE_TOKENS) + j * GATE_TOKENS, GATE_TOKENS)]
                tt(a, a, stage[j % 2][:, 0].rearrange("p t k -> p k t"), ALU.mult).then_inc(S("g_mul"), 1)

            def make_hots(i, j, last=False):
                hot_rows(i, j, 1)
                hot_rows(i, j, 2)
                if not last:
                    hot_rows(i, j + 1, 0)
                first_quarter(i, j)

            def apply_gates(q, i, slot):
                dve.wait_ge(S(f"gates_in{slot}"), i * 16 + 16 * (4 * (q - 1) + 1))
                a = acts[q % 2][:, :, bass.ds(i * (2 * CHUNK) + slot * CHUNK, CHUNK)]
                tt(a, a, gates_in[slot].rearrange("p (t k) -> p k t", k=QUARTER), ALU.mult).then_inc(S("gates_applied"), 1)

            def v_acts(s, q):
                n0 = n_p + s * SEG
                for half in range(2):
                    n1 = n0 + half * SEG // 2
                    with dve.Fori(0, SEG // 16) as i:
                        for j in range(8):
                            n = n1 + j
                            dve.wait_ge(used, i * 8 + (n - 1))
                            a = acts[q % 2][:, bass.ds(i * 16 + 2 * j, 2), :]
                            dve.tensor_copy(act_hi[:, n % 2], a).then_inc(S("acts_hi"), 1)
                            dve.wait_ge(S("acts_hi"), i * 8 + (acts_split_n(n) + 1))
                            tt(act_lo[:, n % 2], a, act_hi[:, n % 2].bitcast(F32), ALU.subtract).then_inc(S("acts_split"), 1)
                            if s == 6 and j % 4 == 3:
                                apply_gates(3, i + 2 * half, j // 4)
                    for dt in range(8):
                        k_ = 16 * q + 8 * half + dt
                        if k_:
                            dve.wait_ge(S("out_taken"), k_)
                        if dt < 7:
                            dve.wait_ge(S("v_sum"), 7 * (2 * q + half) + dt + 1)
                        else:
                            dve.wait_ge(used, n1 + SEG // 2)
                        m = half * 8 + dt
                        gated_add(ps[dt], xo[:, m, :], mods[:, G_C, m, 0:1], mods[:, G_C, m, 1:NS],
                                  xs3).then_inc(S("out_taken"), 1)

            for s, (what, q) in enumerate(segments):
                if s == 1:
                    dve.wait_ge(S("gelu_done"), SEG + 4)
                    hot_rows(0, 0, 0)
                    with dve.Fori(0, SEG // 4 - 1) as i:
                        for j in range(4):
                            make_hots(i, j)
                    for j in range(4):
                        make_hots(SEG // 4 - 1, j, j == 3)
                    dve.wait_ge(S("g_mul"), SEG + 2)
                    for slot in range(2):
                        dve.wait_ge(S(f"gates_stored{slot}"), 16 * (SEG // 2 + 1))
                elif what == "u" and q:
                    dve.wait_ge(S("gelu_done"), q * SEG + 4)
                    with dve.Fori(0, 4) as i:
                        for slot in range(2):
                            apply_gates(q - 1, i, slot)
                elif what == "v":
                    if q:
                        dve.wait_ge(S("gates_applied"), 8 * q + 2)
                    if s == 6:
                        dve.wait_ge(S("gelu_done"), 4 * SEG + 4)
                    v_acts(s, q)

            dve.wait_ge(S("out_taken"), 64)
            norm(xo, yn, rms3, gain3, SH_F, SC_F, "gfin", 3, S("y_done"))


OUTS = {
    "y": (P, KT, N), "shift_all": (P, AT, NS), "wkv_p": (P, MT, AHD), "wkv_s": (P, MT, NB, AHD),
    "conv_all": (P, MT, NS, 3), "c_p": (BH, P, DV), "c_s": (BH, P, NB, DV), "n_all": (P, BH, NS), "m_all": (BH, NS),
}


def tiled(w):
    c = w.shape[1] // P
    return np.ascontiguousarray(w.reshape(KT, P, c, P).transpose(2, 1, 0, 3)).reshape(c, P, D)


def by_tile(a, n=P):
    a = a.reshape(-1, a.shape[-1] // n, n)
    return a.transpose(2, 1, 0)


def kernel(x_prompt, x_sample, c_prompt, c_sample, state_rwkv_shift, state_rwkv_wkv, state_mlstm_conv,
           state_mlstm_C, state_mlstm_n, state_mlstm_m, w_ada, b_ada, norm_mix_g, w_in, a_mu, a_w0, a_w2,
           a_a0, a_a2, a_g2, a_kk, a_ka, a_rk, a_lnw, a_lnb, b_conv_w, b_conv_b, b_ig_bias, b_fg_bias,
           b_norm_g, w_out, norm_ffn_g, peer_wq, peer_keys, peer_u, peer_v, w_ada_final, b_ada_final,
           norm_final_g):
    import concourse.bacc as bacc
    from concourse.bass_utils import run_bass_kernel_spmd

    f = np.float32
    A = lambda a: np.asarray(a)
    c0, c1 = constants()
    prm = np.zeros((P, PRM_N), f)

    def vec(name, a):
        at, n = PRM[name]
        prm[:, at:at + n] = A(a).reshape(n, P).T

    for name, a in (("mu", a_mu), ("w0", a_w0), ("a0", a_a0), ("kk", a_kk), ("ka", a_ka), ("rk", a_rk), ("lnw", a_lnw),
                    ("lnb", a_lnb), ("convw", b_conv_w), ("convb", b_conv_b), ("bnorm", b_norm_g),
                    ("gmix", norm_mix_g), ("gffn", norm_ffn_g), ("gfin", norm_final_g)):
        vec(name, a)
    vec("bada", np.concatenate([A(b_ada)[0], A(b_ada_final)]))
    at = PRM["gatebias"][0]
    prm[0:BH, at] = A(b_ig_bias)[0]
    prm[32:32 + BH, at] = A(b_fg_bias)[0]
    prm[:, PRM["eps"][0]] = 1e-6
    prm[:, PRM["gneps"][0]] = AHD * 1e-5

    w_in0 = A(w_in)[0]
    w_g = np.zeros((P, KT, 36), f)
    gates = w_in0[:, 6400:6408].reshape(KT, P, 2 * BH).transpose(1, 0, 2)
    w_g[:, :, 0:BH] = gates[:, :, 0:BH]
    w_g[:, :, 32:36] = gates[:, :, BH:]
    w2, a2 = np.zeros((P, MIX), f), np.zeros((P, MIX), f)
    w2[0:64] = A(a_w2)[0]
    a2[64:128] = A(a_a2)[0]
    x = np.concatenate([A(x_prompt)[0], A(x_sample).reshape(SM, D)])
    c = np.concatenate([A(c_prompt), A(c_sample)])
    u = A(peer_u)[0].reshape(NK, NK, KT, P)
    ins = {
        "x": by_tile(x), "c": by_tile(c), "prm": prm, "cst0": c0, "cst1": c1,
        "w_ada": A(w_ada)[0], "w_adaf": A(w_ada_final), "w_in": tiled(w_in0[:, 0:6400]), "w_g": w_g.reshape(P, -1),
        "w_out": tiled(A(w_out)[0]), "w_q": tiled(A(peer_wq)[0]),
        "peer_u": np.ascontiguousarray(u.transpose(1, 3, 2, 0)).reshape(NK, P, D), "peer_v": A(peer_v)[0],
        "keys": A(peer_keys)[0].transpose(3, 0, 1, 2).reshape(P, 2 * PH, NK),
        "w2": w2, "a2": a2, "g2": A(a_g2)[0],
        "shift0": by_tile(A(state_rwkv_shift)[0]).reshape(P, -1),
        "conv0": A(state_mlstm_conv)[0].reshape(NB, 3, MT, P).transpose(3, 2, 0, 1).reshape(P, -1),
        "wkv0": A(state_rwkv_wkv)[0].reshape(NB, MT, 2, AHD, AHD).transpose(2, 4, 1, 0, 3).reshape(P, MT, NB, AHD),
        "c0": A(state_mlstm_C)[0].transpose(1, 2, 0, 3),
        "n0": A(state_mlstm_n)[0].transpose(2, 1, 0).reshape(P, -1),
        "m0": A(state_mlstm_m)[0].T,
    }
    nc = bacc.Bacc("TRN2", target_bir_lowering=False, num_devices=1)
    arrays, T = {}, {}
    for name, a in ins.items():
        arrays[f"in_{name}"] = np.ascontiguousarray(a)
        T[name] = nc.dram_tensor(f"in_{name}", a.shape, F32, kind="ExternalInput").ap()
    for name, shape in OUTS.items():
        T[name] = nc.dram_tensor(f"out_{name}", shape, F32, kind="ExternalOutput").ap()
    build(nc, T)
    res = run_bass_kernel_spmd(nc, [arrays], core_ids=[0]).results[0]
    o = {name: res[f"out_{name}"] for name in OUTS}

    y = o["y"].transpose(2, 1, 0).reshape(N, D)
    shift = o["shift_all"].transpose(2, 1, 0).reshape(NS, SHIFT)
    conv = o["conv_all"].transpose(2, 3, 1, 0).reshape(NS, 3, MIX)
    n_all = o["n_all"].transpose(2, 1, 0)
    wkv_p = o["wkv_p"].reshape(2, AHD, MT, AHD).transpose(2, 0, 3, 1).reshape(1, 1, AH, AHD, AHD)
    wkv_s = o["wkv_s"].reshape(2, AHD, MT, NB, AHD).transpose(3, 2, 0, 4, 1).reshape(1, NB, AH, AHD, AHD)
    out = (y[:TP].reshape(1, TP, D), y[TP:].reshape(NB, TS, D),
           shift[None, 0:1], wkv_p, conv[None, 0:1], o["c_p"][None, None], n_all[None, 0:1], o["m_all"].T[None, 0:1],
           shift[None, 1:], wkv_s, conv[None, 1:], o["c_s"].transpose(2, 0, 1, 3)[None], n_all[None, 1:],
           o["m_all"].T[None, 1:])
    return tuple(np.ascontiguousarray(a) for a in out)
```
